# Optimizing a Trainium2 kernel written in Bass

```python
import jax, jax.numpy as jnp
from jax import lax
import numpy as np

D_MODEL = 1024
BATCH = 1
SEQ = 512
DEPTH = 2

N_EVEN = (DEPTH + 1) // 2
N_ODD = DEPTH // 2

DN_ALPHA = (2.0 * DEPTH) ** 0.25
DN_BETA = (8.0 * DEPTH) ** -0.25

GDN_HEADS = 4
GDN_HEAD_DIM = 128
GDN_WIDTH = GDN_HEADS * GDN_HEAD_DIM
GDN_CONV = 4
GDN_CHUNK = 64
SC_WIDTH = 512
SC_CONV = 3
EVEN_SPLITS = (3 * GDN_WIDTH, GDN_WIDTH, GDN_HEADS, GDN_HEADS, SC_WIDTH, SC_WIDTH, SC_WIDTH)
EVEN_IN = sum(EVEN_SPLITS)
EVEN_MIX = GDN_WIDTH + SC_WIDTH

MLA_HEADS = 8
Q_LORA = 384
KV_LORA = 256
QK_NOPE = 128
QK_ROPE = 64
V_DIM = 128
ODD_SPLITS = (Q_LORA, KV_LORA, QK_ROPE)
ODD_IN = sum(ODD_SPLITS)
ODD_MIX = MLA_HEADS * V_DIM
ROPE_THETA = 10000.0
Q_BLOCK = 128

N_EXPERTS = 32
N_GROUPS = 4
EXPERTS_PER_GROUP = N_EXPERTS // N_GROUPS
TOP_K = 2
D_EXPERT = 512
MOE_BLOCK = 128

NORM_EPS = 1e-6
LN_EPS = 1e-5

kernel_name = 'hybrid_gdn_shortconv_mla_grouped_moe'

def split_cols(x, sizes):
    idx = np.cumsum(sizes)[:-1].tolist()
    return jnp.split(x, idx, axis=-1)

def layer_norm(x, g, b):
    xf = x.astype(jnp.float32)
    mu = xf.mean(-1, keepdims=True)
    var = jnp.square(xf - mu).mean(-1, keepdims=True)
    return ((xf - mu) * lax.rsqrt(var + LN_EPS) * g.astype(jnp.float32) + b.astype(jnp.float32)).astype(x.dtype)

def rms_norm(x, w):
    xf = x.astype(jnp.float32)
    y = xf * lax.rsqrt(jnp.mean(xf * xf, -1, keepdims=True) + NORM_EPS) * w.astype(jnp.float32)
    return y.astype(x.dtype)

def l2_norm(x):
    xf = x.astype(jnp.float32)
    return xf * lax.rsqrt(jnp.sum(xf * xf, -1, keepdims=True) + NORM_EPS)

def causal_dwconv(x, w):
    k = w.shape[0]
    return lax.conv_general_dilated(
        x, w[:, None, :].astype(x.dtype), window_strides=(1,), padding=[(k - 1, 0)],
        dimension_numbers=('NWC', 'WIO', 'NWC'), feature_group_count=x.shape[-1])

def chunk_gated_delta_rule(q, k, v, g, beta):
    bsz, s, h, dk = q.shape
    dv = v.shape[-1]
    c = GDN_CHUNK
    n = s // c

    def to_chunks(t):
        t = jnp.moveaxis(t, 2, 1)
        return t.reshape(bsz, h, n, c, *t.shape[3:])

    q = to_chunks(q * dk ** -0.5)
    k = to_chunks(k)
    v = to_chunks(v.astype(jnp.float32))
    gc = jnp.cumsum(to_chunks(g), -1)
    beta = to_chunks(beta)
    causal = jnp.tril(jnp.ones((c, c), bool))
    strict = jnp.tril(jnp.ones((c, c), bool), -1)
    decay = jnp.exp(jnp.where(causal, gc[..., :, None] - gc[..., None, :], -jnp.inf))
    kb = k * beta[..., None]
    lower = jnp.where(strict, jnp.einsum('bhnid,bhnjd->bhnij', kb, k) * decay, 0.0)
    rhs = jnp.concatenate([v * beta[..., None], kb * jnp.exp(gc)[..., None]], -1)
    sol = lax.linalg.triangular_solve(lower, rhs, left_side=True, lower=True, unit_diagonal=True)
    u, w = sol[..., :dv], sol[..., dv:]
    intra = jnp.where(causal, jnp.einsum('bhnid,bhnjd->bhnij', q, k) * decay, 0.0)
    q_dec = q * jnp.exp(gc)[..., None]
    k_dec = k * jnp.exp(gc[..., -1:] - gc)[..., None]
    g_last = jnp.exp(gc[..., -1])

    def step(state, inp):
        qd, kd, uc, wc, ic, gl = inp
        v_new = uc - jnp.einsum('bhck,bhkv->bhcv', wc, state)
        o = jnp.einsum('bhck,bhkv->bhcv', qd, state) + jnp.einsum('bhcj,bhjv->bhcv', ic, v_new)
        state = state * gl[..., None, None] + jnp.einsum('bhck,bhcv->bhkv', kd, v_new)
        return state, o

    xs = tuple(jnp.moveaxis(t, 2, 0) for t in (q_dec, k_dec, u, w, intra, g_last))
    _, o = lax.scan(step, jnp.zeros((bsz, h, dk, dv), jnp.float32), xs)
    o = jnp.moveaxis(o, 0, 2).reshape(bsz, h, s, dv)
    return jnp.moveaxis(o, 1, 2)

def even_mixer(h, w_in, gdn_conv_w, a_log, dt_bias, gdn_norm_w, sc_conv_w, w_out):
    bsz, s, _ = h.shape
    qkv, z, b, a, sc_b, sc_c, sc_h = split_cols(h @ w_in, EVEN_SPLITS)
    qkv = jax.nn.silu(causal_dwconv(qkv, gdn_conv_w))
    q, k, v = [t.reshape(bsz, s, GDN_HEADS, GDN_HEAD_DIM) for t in jnp.split(qkv, 3, -1)]
    q, k = l2_norm(q), l2_norm(k)
    beta = jax.nn.sigmoid(b.astype(jnp.float32))
    g = -jnp.exp(a_log.astype(jnp.float32)) * jax.nn.softplus(
        a.astype(jnp.float32) + dt_bias.astype(jnp.float32))
    o = chunk_gated_delta_rule(q, k, v, g, beta)
    o = rms_norm(o, gdn_norm_w) * jax.nn.silu(z.astype(jnp.float32)).reshape(bsz, s, GDN_HEADS, GDN_HEAD_DIM)
    y_a = o.reshape(bsz, s, GDN_WIDTH).astype(h.dtype)
    y_b = sc_b * causal_dwconv(sc_c * sc_h, sc_conv_w)
    return jnp.concatenate([y_a, y_b], -1) @ w_out

def rope_tables(positions, dim):
    inv = ROPE_THETA ** (-jnp.arange(0, dim, 2, dtype=jnp.float32) / dim)
    ang = positions.astype(jnp.float32)[..., None] * inv
    return jnp.cos(ang), jnp.sin(ang)

def apply_rope(x, cos, sin):
    x1, x2 = jnp.split(x.astype(jnp.float32), 2, -1)
    return jnp.concatenate([x1 * cos - x2 * sin, x2 * cos + x1 * sin], -1).astype(x.dtype)

def blocked_causal_attention(q_nope, q_rope, k_nope, k_rope, v):
    bsz, s, h, dn = q_nope.shape
    nb = s // Q_BLOCK
    scale = (QK_NOPE + QK_ROPE) ** -0.5
    qn = jnp.moveaxis(q_nope.reshape(bsz, nb, Q_BLOCK, h, dn), 1, 0)
    qr = jnp.moveaxis(q_rope.reshape(bsz, nb, Q_BLOCK, h, QK_ROPE), 1, 0)
    kpos = jnp.arange(s)

    def block(args):
        qnb, qrb, i = args
        sc = (jnp.einsum('bqhd,bkhd->bhqk', qnb, k_nope) + jnp.einsum('bqhd,bkd->bhqk', qrb, k_rope))
        sc = sc.astype(jnp.float32) * scale
        qpos = i * Q_BLOCK + jnp.arange(Q_BLOCK)
        sc = jnp.where(kpos[None, :] <= qpos[:, None], sc, -jnp.inf)
        p = jax.nn.softmax(sc, -1)
        return jnp.einsum('bhqk,bkhd->bqhd', p.astype(v.dtype), v)

    o = lax.map(block, (qn, qr, jnp.arange(nb)))
    return jnp.moveaxis(o, 0, 1).reshape(bsz, s, h * v.shape[-1])

def mla_mixer(h, positions, w_in, q_a_norm, w_q_b, kv_a_norm, w_kv_b, w_out):
    bsz, s, _ = h.shape
    qa, kva, k_rope = split_cols(h @ w_in, ODD_SPLITS)
    q = (rms_norm(qa, q_a_norm) @ w_q_b).reshape(bsz, s, MLA_HEADS, QK_NOPE + QK_ROPE)
    kv = (rms_norm(kva, kv_a_norm) @ w_kv_b).reshape(bsz, s, MLA_HEADS, QK_NOPE + V_DIM)
    q_nope, q_rope = q[..., :QK_NOPE], q[..., QK_NOPE:]
    k_nope, v = kv[..., :QK_NOPE], kv[..., QK_NOPE:]
    cos, sin = rope_tables(positions, QK_ROPE)
    q_rope = apply_rope(q_rope, cos[:, :, None], sin[:, :, None])
    k_rope = apply_rope(k_rope, cos, sin)
    return blocked_causal_attention(q_nope, q_rope, k_nope, k_rope, v) @ w_out

def moe_ffn(h, router_w, router_bias, w_gate, w_up, w_down):
    bsz, s, d = h.shape
    t = bsz * s
    hf = h.reshape(t, d)
    scores = jax.nn.sigmoid((hf @ router_w).astype(jnp.float32))
    biased = (scores + router_bias.astype(jnp.float32)).reshape(t, N_GROUPS, EXPERTS_PER_GROUP)
    group_score = lax.top_k(biased, 2)[0].sum(-1)
    gsel = jnp.argmax(group_score, -1)
    in_group = jnp.take_along_axis(biased, gsel[:, None, None], axis=1)[:, 0]
    _, local = lax.top_k(in_group, TOP_K)
    eidx = gsel[:, None] * EXPERTS_PER_GROUP + local
    wsel = jnp.take_along_axis(scores, eidx, -1)
    wsel = wsel / wsel.sum(-1, keepdims=True)
    n_assign = t * TOP_K
    e_flat = eidx.reshape(n_assign)
    order = jnp.argsort(e_flat)
    e_sorted = e_flat[order]
    tok_sorted = order // TOP_K
    counts = jnp.bincount(e_flat, length=N_EXPERTS)
    padded = (counts + MOE_BLOCK - 1) // MOE_BLOCK * MOE_BLOCK
    start = jnp.cumsum(counts) - counts
    pstart = jnp.cumsum(padded) - padded
    dest = pstart[e_sorted] + jnp.arange(n_assign) - start[e_sorted]
    n_blocks = -(-n_assign // MOE_BLOCK) + N_EXPERTS
    rows = n_blocks * MOE_BLOCK
    xs = jnp.zeros((rows, d), h.dtype).at[dest].set(hf[tok_sorted])
    block_expert = jnp.minimum(
        jnp.searchsorted(jnp.cumsum(padded), jnp.arange(n_blocks) * MOE_BLOCK, side='right'), N_EXPERTS - 1)

    def expert_block(args):
        xb, e = args
        return (jax.nn.silu(xb @ w_gate[e]) * (xb @ w_up[e])) @ w_down[e]

    ys = lax.map(expert_block, (xs.reshape(n_blocks, MOE_BLOCK, d), block_expert)).reshape(rows, d)
    contrib = ys[dest] * wsel.reshape(n_assign)[order][:, None].astype(h.dtype)
    return jax.ops.segment_sum(contrib, tok_sorted, num_segments=t).reshape(bsz, s, d)

def setup_inputs(seed: int = 0) -> dict:
    key = jax.random.key(seed)
    ks = iter(jax.random.split(key, 32))
    f32 = jnp.float32

    def nrm(shape, scale):
        return jax.random.normal(next(ks), shape, f32) * scale

    x = nrm((BATCH, SEQ, D_MODEL), 1.0)
    c = nrm((BATCH, D_MODEL), 1.0)
    positions = (jax.random.randint(next(ks), (BATCH, 1), 0, 1024) + jnp.arange(SEQ)[None, :]).astype(jnp.int32)
    ada_w = nrm((DEPTH, 2, D_MODEL, 3 * D_MODEL), 0.2 * D_MODEL ** -0.5)
    ada_b = nrm((DEPTH, 2, 3 * D_MODEL), 0.02)
    ln_g = 1.0 + nrm((DEPTH, 2, D_MODEL), 0.02)
    ln_b = nrm((DEPTH, 2, D_MODEL), 0.02)
    w_in_e = nrm((N_EVEN, D_MODEL, EVEN_IN), D_MODEL ** -0.5)
    gdn_conv_w = nrm((N_EVEN, GDN_CONV, 3 * GDN_WIDTH), GDN_CONV ** -0.5)
    gdn_a_log = jnp.log(jax.random.uniform(next(ks), (N_EVEN, GDN_HEADS), f32, 1.0, 16.0))
    dt = jnp.exp(jax.random.uniform(next(ks), (N_EVEN, GDN_HEADS), f32, float(np.log(1e-3)), float(np.log(1e-1))))
    gdn_dt_bias = dt + jnp.log(-jnp.expm1(-dt))
    gdn_norm_w = 1.0 + nrm((N_EVEN, GDN_HEAD_DIM), 0.02)
    sc_conv_w = nrm((N_EVEN, SC_CONV, SC_WIDTH), SC_CONV ** -0.5)
    w_out_e = nrm((N_EVEN, EVEN_MIX, D_MODEL), DN_BETA * EVEN_MIX ** -0.5)
    w_in_o = nrm((N_ODD, D_MODEL, ODD_IN), D_MODEL ** -0.5)
    q_a_norm = 1.0 + nrm((N_ODD, Q_LORA), 0.02)
    w_q_b = nrm((N_ODD, Q_LORA, MLA_HEADS * (QK_NOPE + QK_ROPE)), Q_LORA ** -0.5)
    kv_a_norm = 1.0 + nrm((N_ODD, KV_LORA), 0.02)
    w_kv_b = nrm((N_ODD, KV_LORA, MLA_HEADS * (QK_NOPE + V_DIM)), KV_LORA ** -0.5)
    w_out_o = nrm((N_ODD, ODD_MIX, D_MODEL), DN_BETA * ODD_MIX ** -0.5)
    router_w = nrm((D_MODEL, N_EXPERTS), D_MODEL ** -0.5)
    router_bias = nrm((N_EXPERTS,), 0.01)
    w_gate = nrm((DEPTH, N_EXPERTS, D_MODEL, D_EXPERT), D_MODEL ** -0.5)
    w_up = nrm((DEPTH, N_EXPERTS, D_MODEL, D_EXPERT), D_MODEL ** -0.5)
    w_down = nrm((DEPTH, N_EXPERTS, D_EXPERT, D_MODEL), DN_BETA * D_EXPERT ** -0.5)
    return {'x': x, 'c': c, 'positions': positions, 'ada_w': ada_w, 'ada_b': ada_b,
            'ln_g': ln_g, 'ln_b': ln_b, 'w_in_e': w_in_e, 'gdn_conv_w': gdn_conv_w,
            'gdn_a_log': gdn_a_log, 'gdn_dt_bias': gdn_dt_bias, 'gdn_norm_w': gdn_norm_w,
            'sc_conv_w': sc_conv_w, 'w_out_e': w_out_e, 'w_in_o': w_in_o, 'q_a_norm': q_a_norm,
            'w_q_b': w_q_b, 'kv_a_norm': kv_a_norm, 'w_kv_b': w_kv_b, 'w_out_o': w_out_o,
            'router_w': router_w, 'router_bias': router_bias, 'w_gate': w_gate, 'w_up': w_up,
            'w_down': w_down}

def reference(x, c, positions, ada_w, ada_b, ln_g, ln_b, w_in_e, gdn_conv_w, gdn_a_log,
              gdn_dt_bias, gdn_norm_w, sc_conv_w, w_out_e, w_in_o, q_a_norm, w_q_b, kv_a_norm,
              w_kv_b, w_out_o, router_w, router_bias, w_gate, w_up, w_down):
    cond = jax.nn.silu(c)
    for i in range(DEPTH):
        j = i // 2
        mod = jnp.einsum('bd,sde->sbe', cond, ada_w[i]) + ada_b[i][:, None, :]
        shift, scale, gate = jnp.split(mod[0][:, None, :], 3, -1)
        hmix = x * (1.0 + scale) + shift
        if i % 2 == 0:
            y = even_mixer(hmix, w_in_e[j], gdn_conv_w[j], gdn_a_log[j], gdn_dt_bias[j],
                           gdn_norm_w[j], sc_conv_w[j], w_out_e[j])
        else:
            y = mla_mixer(hmix, positions, w_in_o[j], q_a_norm[j], w_q_b[j], kv_a_norm[j],
                          w_kv_b[j], w_out_o[j])
        x = layer_norm(DN_ALPHA * x + (1.0 + gate) * y, ln_g[i, 0], ln_b[i, 0])
        shift, scale, gate = jnp.split(mod[1][:, None, :], 3, -1)
        y = moe_ffn(x * (1.0 + scale) + shift, router_w, router_bias, w_gate[i], w_up[i], w_down[i])
        x = layer_norm(DN_ALPHA * x + (1.0 + gate) * y, ln_g[i, 1], ln_b[i, 1])
    return x


_drawn_inputs = setup_inputs


def setup_inputs(seed=0):
    import zlib

    import numpy as np

    out = dict(_drawn_inputs(seed))
    spreads = {}
    factors = {'gdn_norm_w': 2.973, 'q_a_norm': 8.0, 'kv_a_norm': 7.626}
    for name, (base, spread) in spreads.items():
        noise = np.random.default_rng([zlib.crc32(name.encode()), seed]).standard_normal(out[name].shape)
        drawn = base * np.exp(spread * noise) if base else spread * noise
        out[name] = __import__('jax').numpy.asarray(drawn.astype(out[name].dtype))
    for name, factor in factors.items():
        out[name] = (out[name] * factor).astype(out[name].dtype)
    return out
```

```python
from contextlib import ExitStack

import numpy as np

import concourse.bass as bass
from concourse import mybir

F32 = mybir.dt.float32
I32 = mybir.dt.int32
U32 = mybir.dt.uint32
ALU = mybir.AluOpType
ACT = mybir.ActivationFunctionType
AX = mybir.AxisListType

P = 128
D_MODEL, SEQ, DEPTH = 1024, 512, 2
NT = SEQ // P
NJ = D_MODEL // P
DN_ALPHA = (2.0 * DEPTH) ** 0.25
H, DK, CH = 4, 128, 64
QKV_W, SC_W = 3 * H * DK, 512
MH, NOPE, ROPE, VD = 8, 128, 64, 128
Q_LORA, KV_LORA = 384, 256
E, GROUPS, EPG, FE = 32, 4, 8, 512
BLK = 64
NG = SEQ // BLK
MAX_EXTRA = 2 * SEQ // (BLK + 1)
RING, SLOT = 6, 4096
LN_EPS, NORM_EPS = 1e-5, 1e-6
BIG = 1e30
MAGIC = 1.5 * 2 ** 23
TWO_PI = 6.283185307179586
PI_A = 6.28125
PI_B = 0.0019350051879882812
PI_C = TWO_PI - PI_A - PI_B

C_ID, C_ONE, C_CUM, C_BLK, C_DEC, C_DCT, C_LEV = 0, 128, 256, 384, 512, 640, 768
C_ATT, C_SUT, C_IO, C_IO64, C_EPS6, C_EPS5, C_HPI = 1536, 1664, 1792, 1824, 1856, 1857, 1858
N_CONST = 1859
S_CW, S_SW, S_NW, S_QN, S_KN = 0, 48, 60, 61, 64
S_AL, S_DT, S_C, S_RW, S_BA, S_RB, S_INV = 66, 82, 98, 106, 362, 426, 458
N_SMALL = 490
LEVELS = (2, 4, 8, 16, 32)


def constants():
    c = np.zeros((P, N_CONST), np.float32)
    p, f = np.arange(P)[:, None], np.arange(P)[None, :]
    same = p // CH == f // CH
    c[:, C_ID:C_ID + P] = p == f
    c[:, C_ONE:C_ONE + P] = 1
    c[:, C_CUM:C_CUM + P] = same & (p <= f)
    c[:, C_BLK:C_BLK + P] = same
    c[:, C_DEC:C_DEC + P] = np.where(same & (f < p), 0, BIG)
    c[:, C_DCT:C_DCT + P] = np.where(same & (f >= p), 0, -BIG)
    c[:, C_LEV:C_LEV + P] = (p // 2 == f // 2) & (p % 2 == 1) & (f % 2 == 0)
    for n, s in enumerate(LEVELS):
        a = C_LEV + (n + 1) * P
        c[:, a:a + P] = (p // (2 * s) == f // (2 * s)) & (p % (2 * s) < s) & (f % (2 * s) >= s)
    c[:, C_ATT:C_ATT + P] = np.where(f <= p, 0, -BIG)
    c[:, C_SUT:C_SUT + P] = p < f
    c[:, C_IO:C_IO + E] = np.arange(E)
    c[:, C_IO64:C_IO64 + E] = np.arange(E) * BLK
    c[:, C_EPS6], c[:, C_EPS5], c[:, C_HPI] = NORM_EPS, LN_EPS, np.pi / 2
    return c


def ring_plan():
    base, at = {}, 0
    for name, n in (("ada00", 6), ("in_e", 7), ("out_e", 2), ("ada01", 6), ("ada10", 6), ("moe0", 96),
                    ("in_o", 2), ("qb", 2), ("kvb", 1), ("out_o", 2), ("ada11", 6), ("moe1", 96)):
        base[name] = at
        at += n
    return base


def decoder_kernel(nc, x, small, const, rows, ints, ada_w, w_in_e, w_out_e, w_in_o, w_q_b, w_kv_b,
                   w_out_o, w_gate, w_up, w_down, out):
    base = ring_plan()
    ctx = ExitStack()
    with ctx:
        def sb(name, shape, dt=F32):
            return ctx.enter_context(nc.sbuf_tensor(name, shape, dt))

        def sem(name):
            return ctx.enter_context(nc.semaphore(name))

        hm_rows = [nc.dram_tensor(f"hm_rows{i}", [SEQ, D_MODEL], F32, kind="Internal").ap() for i in range(DEPTH)]
        tok_idx = [nc.dram_tensor(f"tok_idx{i}", [BLK * NG * E, 1], I32, kind="Internal").ap() for i in range(DEPTH)]
        y_rows = nc.dram_tensor("y_rows", [(E + MAX_EXTRA) * BLK, D_MODEL], F32, kind="Internal").ap()

        ring = sb("ring", [P, RING, SLOT])
        xres = sb("xres", [P, NT, D_MODEL])
        cst = sb("cst", [P, N_CONST])
        sml = sb("sml", [P, N_SMALL])
        rws = sb("rws", [40, 512])
        intc = sb("intc", [P, 8], I32)
        area_a = sb("area_a", [P, 4096])
        area_b = sb("area_b", [P, 4096])
        area_c = sb("area_c", [P, 6144])
        area_d = sb("area_d", [P, 2048])
        modss = sb("modss", [P, 2048])
        area_e = sb("area_e", [P, 1024])
        gate_a = sb("gate_a", [P, 1024])
        tiny = sb("tiny", [P, 512])
        cond = sb("cond", [P, NJ])
        statb = sb("statb", [P, 16])

        def cc(a, n=P):
            return cst[:, a:a + n]
        ident, ones = cc(C_ID), cc(C_ONE)

        hmT = area_a[:, :].rearrange("p (j t) -> p j t", j=NJ)
        gate_b = area_c[:, 5120:6144]
        hm = [area_e[:, :], area_d[:, 1024:2048]]
        lnrs = [area_a[:, 0:1024], area_d[:, 0:1024]]
        gates = [gate_a[:, :], gate_b]

        qkv = area_c[:, :].rearrange("p (m t) -> p m t", m=12)
        zs = area_d[:, :].rearrange("p (h t) -> p h t", h=H)
        scc = area_b[:, 0:2048].rearrange("p (h t) -> p h t", h=4)
        yb_T = area_b[:, 2048:4096].rearrange("p (h t) -> p h t", h=4)
        sq = [area_e[:, 0:512], area_e[:, 512:1024]]
        rq = [modss[:, 0:512], modss[:, 512:1024]]
        pool16 = [area_a[:, 512 * n:512 * n + 512] for n in range(8)] \
            + [area_b[:, 512 * n:512 * n + 512] for n in range(4)] + [modss[:, 512 * n:512 * n + 512] for n in range(4)]

        def hv(ap):
            return ap.rearrange("p (h t) -> p h t", h=H)
        d_L, d_IT, d_X, d_Y, d_MT, d_KB, d_KD, d_U = [[hv(pool16[2 * n + k]) for k in range(2)] for n in range(8)]
        state = hv(area_e[:, 0:512])
        os_ = hv(area_e[:, 512:1024])
        g_t, g_sp, g_g, g_gc, g_eg, g_kd, g_beg, g_beta, g_ea, g_ms = [tiny[:, 16 * n:16 * n + 16] for n in range(10)]
        g_last = tiny[:, 160:192].rearrange("p (t h c) -> p t h c", t=NT, h=H)

        qaT = area_c[:, 0:1536].rearrange("p (j t) -> p j t", j=3)
        kaT = area_c[:, 1536:2560].rearrange("p (j t) -> p j t", j=2)
        krT = area_c[:, 2560:3072]
        qrT = area_c[:, 3072:5120].rearrange("p (j t) -> p j t", j=4)
        qr = area_c[:, 5120:5632]
        krd = area_c[:, 5632:5760]
        ms_o = area_c[:, 5760:5792]
        lat = area_d[:, 0:640]
        cs_t = area_d[:, 1024:1152].rearrange("p (t f) -> p t f", t=NT)
        sn_t = area_d[:, 1152:1280].rearrange("p (t f) -> p t f", t=NT)
        rt1 = area_d[:, 1280:1536].rearrange("p (h f) -> p h f", h=MH)
        rt2 = area_d[:, 1536:1792].rearrange("p (h f) -> p h f", h=MH)
        ang = area_d[:, 1792:1920]
        kround = area_d[:, 1920:2048]
        v_tok = area_a[:, :].rearrange("p (t n) -> p t n", t=NT)
        qnT = [modss[:, 0:512], modss[:, 512:1024]]
        knT = [modss[:, 1024:1536], modss[:, 1536:2048]]
        prob = [area_e[:, 0:512], area_e[:, 512:1024]]
        probT = [area_d[:, 0:512], area_d[:, 512:1024]]
        oT = area_b[:, :].rearrange("p (h t) -> p h t", h=MH)
        att_m, att_n, att_s, att_r = [tiny[:, 32 * n:32 * n + 32] for n in range(4)]

        xg = [area_b[:, 1024 * n:1024 * n + 1024] for n in range(3)]
        xT = [area_c[:, 512 * n:512 * n + 512].rearrange("p (j s) -> p j s", j=NJ) for n in range(3)]
        sg = [area_c[:, 1536 + 256 * n:1792 + 256 * n] for n in range(3)]
        hb = [area_c[:, 2304 + 256 * n:2560 + 256 * n] for n in range(3)]
        hts = [area_c[:, 3072 + 256 * n:3328 + 256 * n] for n in range(3)]
        yb = [area_b[:, 3072:3584], area_b[:, 3584:4096], area_c[:, 3840:4352]]
        idx_all = sb("idx_all", [BLK, NG * E], I32)
        idx_col = sb("idx_col", [BLK, 4], I32)
        dest_i = sb("dest_i", [P, 16], I32)
        extra_i = sb("extra_i", [1, E], I32)
        mi = sb("mi", [P, 32], U32)
        r_sc, r_bi, r_m8, r_tmp, r_o1, r_o2 = [area_d[:, 128 * n:128 * n + 128] for n in range(6)]
        r_oh, r_rk, r_gf, r_ad = [area_d[:, 768 + 128 * n:896 + 128 * n] for n in range(4)]
        r_yr = area_d[:, 1280:1408]
        r_gs, r_gm, r_ig, r_lm = [area_d[:, 1408 + 32 * n:1440 + 32 * n] for n in range(4)]
        r_sm = area_d[:, 1536:1664]
        wsel = tiny[:, 496:504]
        ycomb = [area_a[:, 0:2048].rearrange("p (k d) -> p k d", k=2), area_a[:, 2048:4096].rearrange("p (k d) -> p k d", k=2)]

        bank = [ctx.enter_context(nc.psum_tensor(f"bank{n}", [P, 512], F32)) for n in range(8)]

        ring_full = [sem(f"ring_full{n}") for n in range(RING)]
        slot_free = sem("slot_free")
        inputs_in, x_in = sem("inputs_in"), sem("x_in")
        act_step, dve_step, pool_step = sem("act_step"), sem("dve_step"), sem("pool_step")
        cond_ready, ada_done, mod_ready = sem("cond_ready"), sem("ada_done"), sem("mod_ready")
        hm_ready, tr_done, hmT_ready = sem("hm_ready"), sem("tr_done"), sem("hmT_ready")
        rows_done, y_taken, ln_done = sem("rows_done"), sem("y_taken"), sem("ln_done")
        var_ready, std_ready = sem("var_ready"), sem("std_ready")
        proj_done, conv_done, silu_done, sq_ready = sem("proj_done"), sem("conv_done"), sem("silu_done"), sem("sq_ready")
        ssq_done, rt_ready, qk_ready, zc_done, sc_read = sem("ssq_done"), sem("rt_ready"), sem("qk_ready"), sem("zc_done"), sem("sc_read")
        ba_done, t_ready, sp_ready, g_ready, gc_done = sem("ba_done"), sem("t_ready"), sem("sp_ready"), sem("g_ready"), sem("gc_done")
        gcs_ready, ge_ready, gates_ready = sem("gcs_ready"), sem("ge_ready"), sem("gates_ready")
        cg_ready, gcb_done, kq_done, eb_ready, dd_ready, dx_ready = (sem("cg_ready"), sem("gcb_done"), sem("kq_done"),
                                                                    sem("eb_ready"), sem("dd_ready"), sem("dx_ready"))
        x0_ready, xt_done, y0_ready = sem("x0_ready"), sem("xt_done"), sem("y0_ready")
        mt_done, mt_ready, y2_done, lv_ready = sem("mt_done"), sem("mt_ready"), sem("y2_done"), sem("lv_ready")
        kt_done, kd_ready, vt_done, vb_ready = sem("kt_done"), sem("kd_ready"), sem("vt_done"), sem("vb_ready")
        uw_done, u_ready, wt_ready = sem("uw_done"), sem("u_ready"), sem("wt_ready")
        vn_done, vn_ready, sd_done, s_ready, o_done = sem("vn_done"), sem("vn_ready"), sem("sd_done"), sem("s_ready"), sem("o_done")
        orms_ready, orec_ready, os_ready, ot_done, ya_ready = (sem("orms_ready"), sem("orec_ready"), sem("os_ready"),
                                                              sem("ot_done"), sem("ya_ready"))
        y_done = sem("y_done")
        lat_done, lms_ready, lrs_ready, lat_ready, kr_ready = sem("lat_done"), sem("lms_ready"), sem("lrs_ready"), sem("lat_ready"), sem("kr_ready")
        latT_done, latT_ready, krT_ready = sem("latT_done"), sem("latT_ready"), sem("krT_ready")
        ang_ready, sin_ready = sem("ang_ready"), sem("sin_ready")
        qr_done, qr_ready, qrt_done, qrT_ready, v_done, v_ready = (sem("qr_done"), sem("qr_ready"), sem("qrt_done"),
                                                                   sem("qrT_ready"), sem("v_done"), sem("v_ready"))
        qkn_done, qkn_ready, s_done, nm_ready, p_ready, pn_ready = (sem("qkn_done"), sem("qkn_ready"), sem("s_done"),
                                                                    sem("nm_ready"), sem("p_ready"), sem("pn_ready"))
        pt_done, pt_ready, av_done, oT_ready = sem("pt_done"), sem("pt_ready"), sem("av_done"), sem("oT_ready")
        hm_stored = [sem(f"hm_stored{n}") for n in range(2)]
        rows_seen, col_seen = sem("rows_seen"), sem("col_seen")
        logit_done, score_ready, oh_ready, rank_done, dest_ready = (sem("logit_done"), sem("score_ready"), sem("oh_ready"),
                                                                    sem("rank_done"), sem("dest_ready"))
        idx_filled, idx_cleared, idx_scattered, idx_loaded = sem("idx_filled"), sem("idx_cleared"), sem("idx_scattered"), sem("idx_loaded")
        col_ready, t_done, xT_ready = sem("col_ready"), sem("t_done"), sem("xT_ready")
        gathered, y_stored, y_back = ([sem(f"{n}{b}") for b in range(2)] for n in ("gathered", "y_stored", "y_back"))
        gate_done, up_done, silu_ready, h_ready = sem("gate_done"), sem("up_done"), sem("silu_ready"), sem("h_ready")
        ht_done, hts_ready, down_done, y_ready = sem("ht_done"), sem("hts_ready"), sem("down_done"), sem("y_ready")
        x_names = ("col", "gathered", "t", "xT", "gate", "up", "silu", "h", "ht", "hts", "down", "y", "stored")
        ex = {n: sem(f"extra_{n}") for n in x_names}
        y_used, out_stored, y_cleared = sem("y_used"), sem("out_stored"), sem("y_cleared")

        block = ctx.enter_context(nc.Block())

        class InOrder:

            def __init__(self, eng, done):
                self.eng, self.done, self.n = eng, done, 0

            def __call__(self, ins):
                self.n += 1
                ins.then_inc(self.done, 1)
                self.eng.wait_ge(self.done, self.n)

        def signal(eng, ins, done, value):
            ins.then_inc(done, 1)
            eng.wait_ge(done, value)

        def tcols(T):
            return slice(P * T, P * T + P)

        @block.sync
        def _(sp):
            def load(n, src, dst_cols=SLOT, shape=None):
                if n >= RING:
                    sp.wait_ge(slot_free, n - RING + 1)
                dst = ring[:, n % RING, 0:dst_cols]
                if shape:
                    dst = dst.rearrange("p (j n) -> p j n", j=shape)
                sp.dma_start(dst, src).then_inc(ring_full[n % RING], 16)

            def columns(w, a, b, j, order="(p j) n -> p j n"):
                return w[:, a:b].rearrange(order, j=j)

            def ada(name, i, s):
                for c in range(6):
                    load(base[name] + c, columns(ada_w[i, s], 512 * c, 512 * c + 512, NJ), shape=NJ)

            def experts(name, i):
                n0 = base[name]
                with sp.Fori(0, E // 2) as it:
                    for b in range(2):
                        e = sp.snap(it * 2 + b)
                        for m, w in enumerate((w_gate, w_up, w_down)):
                            k = 3 * b + m
                            sp.wait_ge(slot_free, it * 6 + (n0 + k - RING + 1))
                            src = w[i, bass.ds(e, 1)]
                            if m < 2:
                                src = src.rearrange("o (p j) n -> p (o j n)", j=NJ)
                                dst = ring[:, (n0 + k) % RING, :]
                            else:
                                src = src.rearrange("o (j p) n -> p (o j) n", p=P)
                                dst = ring[:, (n0 + k) % RING, :].rearrange("p (j n) -> p j n", j=4)
                            sp.dma_start(dst, src).then_inc(ring_full[(n0 + k) % RING], 16)

            ada("ada00", 0, 0)
            for c, a in enumerate((0, 512, 1024, 1536, 2568, 3080, 2056)):
                load(base["in_e"] + c, columns(w_in_e, a, a + 512, NJ), shape=NJ)
            for c in range(2):
                load(base["out_e"] + c, columns(w_out_e, 512 * c, 512 * c + 512, NJ, "(j p) n -> p j n"), shape=NJ)
            ada("ada01", 0, 1)
            ada("ada10", 1, 0)
            experts("moe0", 0)
            load(base["in_o"], columns(w_in_o, 0, 384, NJ), 384 * NJ, NJ)
            load(base["in_o"] + 1, columns(w_in_o, 384, 704, NJ), 320 * NJ, NJ)
            for c in range(2):
                load(base["qb"] + c, columns(w_q_b, 768 * c, 768 * c + 768, 3, "(j p) n -> p j n"), 768 * 3, 3)
            load(base["kvb"], columns(w_kv_b, 0, 2048, 2, "(j p) n -> p j n"), shape=2)
            for c in range(2):
                load(base["out_o"] + c, columns(w_out_o, 512 * c, 512 * c + 512, NJ, "(j p) n -> p j n"), shape=NJ)
            ada("ada11", 1, 1)
            experts("moe1", 1)

        @block.tensor
        def _(pe):
            def full(n):
                pe.wait_ge(ring_full[n % RING], 16 * (n // RING + 1))
                return ring[:, n % RING, :]

            def bcast_row(dst, r, start=True):
                return pe.matmul(dst, cst[0:40, C_ID + r:C_ID + r + 1].to_broadcast([40, P]), rws[:, :],
                                 start=start, stop=True)

            def ada(name, st):
                for c in range(6):
                    k = 6 * st + c
                    w = full(base[name] + c)
                    if k >= 2:
                        pe.wait_ge(mod_ready, k - 1)
                    ps = bank[c % 2][:, :]
                    for j in range(NJ):
                        mm = pe.matmul(ps, cond[:, j:j + 1].to_broadcast([P, P]), w[:, 512 * j:512 * j + 512],
                                       start=(j == 0), stop=False)
                    mm.then_inc(slot_free, 1)
                    bcast_row(ps, k, start=False).then_inc(ada_done, 1)

            def modulated(st):
                for T in range(NT):
                    k = NT * st + T
                    pe.wait_ge(hm_ready, k + 1)
                    if k:
                        pe.wait_ge(hmT_ready, 2 * k)
                    hv_ = hm[T % 2].rearrange("p (f j) -> p j f", j=NJ)
                    for j in range(NJ):
                        mm = pe.transpose(bank[2 + j // 4][:, P * (j % 4):P * (j % 4) + P], hv_[:, j, :], ident)
                        if j % 4 == 3:
                            mm.then_inc(tr_done, 1)

            def ln_rows(st):
                for n in range(4):
                    mm = bcast_row(bank[4 + n][:, :], 24 + 4 * st + n)
                mm.then_inc(rows_done, 1)

            def out_proj(name, tiles, st, ready):
                w = [full(base[name]), full(base[name] + 1)]
                ready()
                for T in range(NT):
                    if T >= 2:
                        pe.wait_ge(y_taken, NT * (st // 2) + T - 1)
                    for n in range(2):
                        for j in range(NJ):
                            mm = pe.matmul(bank[2 * (T % 2) + n][:, :], tiles[j][:, tcols(T)], w[n][:, 512 * j:512 * j + 512],
                                           start=(j == 0), stop=(j == NJ - 1))
                            if T == NT - 1 and j == NJ - 1 and n == 0:
                                mm.then_inc(slot_free, 1)
                    mm.then_inc(y_done, 1)
                pe.wait_ge(y_done, NT * (st // 2 + 1))
                pe.sem_inc(slot_free, 1)

            pe.wait_ge(inputs_in, 64)
            pe.wait_ge(cond_ready, 1)
            ada("ada00", 0)
            modulated(0)
            pe.wait_ge(hmT_ready, 2 * NT)
            for T in range(NT):
                for j in range(NJ):
                    mm = pe.matmul(bank[6][:, 8 * T:8 * T + 8], hmT[:, j, tcols(T)], sml[:, S_BA + 8 * j:S_BA + 8 * j + 8],
                                   start=(j == 0), stop=(j == NJ - 1))
            mm.then_inc(ba_done, 1)

            def ssq(m):
                pe.wait_ge(sq_ready, m + 1)
                if m >= 2:
                    pe.wait_ge(rt_ready, m - 1)
                pe.matmul(bank[4 + m % 2][:, :], ones, sq[m % 2], start=True, stop=True).then_inc(ssq_done, 1)

            for m in range(28):
                if m % 4 == 0:
                    w = full(base["in_e"] + m // 4)
                if m >= 4:
                    f = m - 4
                    if f < 12:
                        pe.wait_ge(conv_done, f + 1)
                    elif f < 20:
                        pe.wait_ge(zc_done, f - 11)
                    else:
                        pe.wait_ge(sc_read, f - 19)
                for j in range(NJ):
                    a = 512 * j + P * (m % 4)
                    mm = pe.matmul(bank[m % 4][:, :], w[:, a:a + P], hmT[:, j, :], start=(j == 0), stop=(j == NJ - 1))
                mm.then_inc(proj_done, 1)
                if m % 4 == 3:
                    pe.wait_ge(proj_done, m + 1)
                    pe.sem_inc(slot_free, 1)
                if 2 <= m < 10:
                    ssq(m - 2)
                if m == 10:
                    pe.wait_ge(g_ready, 1)
                    pe.matmul(bank[7][:, 0:16], cc(C_CUM), g_g, start=True, stop=True)
                    pe.matmul(bank[7][:, 16:32], cc(C_BLK), g_g, start=True, stop=True).then_inc(gc_done, 1)

            pe.wait_ge(sc_read, 8)
            pe.wait_ge(gates_ready, 1)
            for pair in range(2):
                tiles = [(2 * pair + k, k, [bank[4 * k + n] for n in range(4)]) for k in range(2)]
                for T, k, B in tiles:
                    if pair:
                        pe.wait_ge(ya_ready, T - 1)
                    pe.wait_ge(cg_ready, T + 1)
                    pe.matmul(B[0][:, :], ones, d_MT[k].rearrange("p h t -> p (h t)"), start=True, stop=True).then_inc(gcb_done, 1)
                    pe.wait_ge(qk_ready, 8)
                    for h in range(H):
                        pe.matmul(B[1][:, P * h:P * h + P], qkv[:, 4 + h, tcols(T)], qkv[:, 4 + h, tcols(T)], start=True, stop=True)
                    for h in range(H):
                        mm = pe.matmul(B[2][:, P * h:P * h + P], qkv[:, 4 + h, tcols(T)], qkv[:, h, tcols(T)], start=True, stop=True)
                    mm.then_inc(kq_done, 1)
                for T, k, B in tiles:
                    pe.wait_ge(x0_ready, T + 1)
                    for h in range(H):
                        mm = pe.transpose(B[0][:, P * h:P * h + P], d_X[k][:, h, :], ident)
                    mm.then_inc(xt_done, 1)
                for lv in range(5):
                    for T, k, B in tiles:
                        n = (pair * 5 + lv) * 2 + k
                        pe.wait_ge(y0_ready, T + 1)
                        if lv:
                            pe.wait_ge(lv_ready, n - 1)
                        for h in range(H):
                            mm = pe.matmul(B[1][:, P * h:P * h + P], d_L[k][:, h, :], d_Y[k][:, h, :], start=True, stop=True)
                        mm.then_inc(mt_done, 1)
                    if lv == 1:
                        for T, k, B in tiles:
                            for h in range(H):
                                mm = pe.transpose(B[0][:, P * h:P * h + P], qkv[:, 4 + h, tcols(T)], ident)
                            mm.then_inc(kt_done, 1)
                    if lv == 3:
                        for T, k, B in tiles:
                            pe.wait_ge(kd_ready, T + 1)
                            for h in range(H):
                                mm = pe.transpose(B[0][:, P * h:P * h + P], qkv[:, 8 + h, tcols(T)], ident)
                            mm.then_inc(vt_done, 1)
                    for T, k, B in tiles:
                        n = (pair * 5 + lv) * 2 + k
                        pe.wait_ge(mt_ready, n + 1)
                        for h in range(H):
                            mm = pe.matmul(B[2][:, P * h:P * h + P], d_X[k][:, h, :], d_MT[k][:, h, :], start=True, stop=True)
                        for h in range(H):
                            mm = pe.matmul(B[3][:, P * h:P * h + P], d_MT[k][:, h, :], d_X[k][:, h, :], start=True, stop=True)
                        mm.then_inc(y2_done, 1)
                for T, k, B in tiles:
                    pe.wait_ge(lv_ready, pair * 10 + 9 + k)
                    pe.wait_ge(vb_ready, T + 1)
                    for h in range(H):
                        pe.matmul(B[1][:, P * h:P * h + P], d_Y[k][:, h, :], qkv[:, 8 + h, tcols(T)], start=True, stop=True)
                    for h in range(H):
                        mm = pe.matmul(B[2][:, P * h:P * h + P], d_KB[k][:, h, :], d_Y[k][:, h, :], start=True, stop=True)
                    mm.then_inc(uw_done, 1)
                for T, k, B in tiles:
                    pe.wait_ge(wt_ready, T + 1)
                    pe.wait_ge(u_ready, T + 1)
                    for c in range(2):
                        n, r = 2 * T + c, slice(CH * c, CH * c + CH)
                        tc = slice(P * T + CH * c, P * T + CH * c + CH)
                        pe.wait_ge(s_ready, n + 1)
                        for h in range(H):
                            mm = pe.matmul(B[0][r, P * h:P * h + P], qkv[:, 4 + h, tc], state[:, h, :], start=True, stop=True)
                        mm.then_inc(vn_done, 1)
                        pe.wait_ge(vn_ready, n + 1)
                        for h in range(H):
                            mm = pe.matmul(B[1][:, P * h:P * h + P], d_KD[k][r, h, :], d_U[k][r, h, :], start=True, stop=True)
                        mm.then_inc(sd_done, 1)
                        for h in range(H):
                            pe.matmul(B[3][r, P * h:P * h + P], qkv[:, h, tc], state[:, h, :], start=True, stop=False)
                            mm = pe.matmul(B[3][r, P * h:P * h + P], d_IT[k][r, h, r], d_U[k][r, h, :], start=False, stop=True)
                        mm.then_inc(o_done, 1)
                    pe.wait_ge(os_ready, T + 1)
                    for h in range(H):
                        mm = pe.transpose(B[2][:, P * h:P * h + P], os_[:, h, :], ident)
                    mm.then_inc(ot_done, 1)

            pe.wait_ge(ya_ready, NT)
            ln_rows(0)
            out_proj("out_e", [zs[:, j, :] for j in range(4)] + [yb_T[:, j, :] for j in range(4)], 0, lambda: None)
            pe.wait_ge(y_taken, NT)
            ada("ada01", 1)

            count = pe.alloc_register("pe_extra")
            pe.reg_mov(count, 0)

            def moe(i, name):
                st = 2 * i + 1
                modulated(st)
                pe.wait_ge(hmT_ready, 2 * NT * (st + 1))
                for T in range(NT):
                    for j in range(NJ):
                        mm = pe.matmul(bank[4][:, E * T:E * T + E], hmT[:, j, tcols(T)], sml[:, S_RW + E * j:S_RW + E * j + E],
                                       start=(j == 0), stop=(j == NJ - 1))
                mm.then_inc(logit_done, 1)
                if i == 0:
                    ada("ada10", 2)
                pe.wait_ge(oh_ready, i + 1)
                oh = r_oh.rearrange("p (t e) -> p t e", t=NT)
                for T in range(NT):
                    for B in range(T):
                        pe.matmul(bank[5][:, E * T:E * T + E], ones, oh[:, B, :], start=(B == 0), stop=False)
                    pe.matmul(bank[5][:, E * T:E * T + E], cc(C_SUT), oh[:, T, :], start=(T == 0), stop=True)
                for T in range(NT):
                    mm = pe.matmul(bank[5][:, E * NT:E * NT + E], ones, oh[:, T, :], start=(T == 0), stop=(T == NT - 1))
                mm.then_inc(rank_done, 1)
                pe.wait_ge(dest_ready, i + 1)

                def block_pass(n, b, banks, s, arrivals, wg, wu, wd):
                    bt, bg, bu, bh, bd = banks
                    pe.wait_ge(s["gathered"], arrivals * 16)
                    pe.sem_inc(rows_seen, 1)
                    for j in range(NJ):
                        mm = pe.transpose(bt[:, BLK * j:BLK * j + BLK],
                                          xg[b][0:BLK, :].rearrange("p (f j) -> p j f", j=NJ)[:, j, :], ident[0:BLK, 0:BLK])
                    mm.then_inc(s["t"], 1)
                    pe.wait_ge(s["xT"], n)
                    for w_of, dst, done in ((wg, bg, s["gate"]), (wu, bu, s["up"])):
                        w = w_of()
                        for j in range(NJ):
                            for hf in range(2):
                                mm = pe.matmul(dst[BLK * hf:BLK * hf + BLK, 0:256], xT[b][:, j, :],
                                               w[:, 512 * j + 256 * hf:512 * j + 256 * hf + 256],
                                               start=(j == 0), stop=(j == NJ - 1))
                        mm.then_inc(done, 1)
                    pe.wait_ge(s["h"], n)
                    for c in range(2):
                        mm = pe.transpose(bh[:, P * c:P * c + P], hb[b][:, P * c:P * c + P], ident)
                    mm.then_inc(s["ht"], 1)
                    w = wd()
                    pe.wait_ge(s["hts"], n)
                    for kt in range(4):
                        lhs = hts[b][:, P * (kt % 2) + BLK * (kt // 2):P * (kt % 2) + BLK * (kt // 2) + BLK]
                        for hf in range(2):
                            mm = pe.matmul(bd[BLK * hf:BLK * hf + BLK, :], lhs, w[:, 1024 * kt + 512 * hf:1024 * kt + 512 * hf + 512],
                                           start=(kt == 0), stop=(kt == 3))
                    mm.then_inc(s["down"], 1)

                regular = [dict(gathered=gathered[b], t=t_done, xT=xT_ready, gate=gate_done, up=up_done, h=h_ready,
                                ht=ht_done, hts=hts_ready, down=down_done) for b in range(2)]
                n0 = base[name]
                with pe.Fori(0, E // 2) as it:
                    for b in range(2):
                        n = pe.snap(it * 2 + (E * i + b + 1))

                        def arrived(k):
                            def wait():
                                q = n0 + k
                                pe.wait_ge(ring_full[q % RING], it * 16 + 16 * (q // RING + 1))
                                return ring[:, q % RING, :]
                            return wait
                        block_pass(n, b, (bank[4], bank[2], bank[3], bank[5], bank[6 + b]), regular[b], it + (E // 2 * i + 1),
                                   arrived(3 * b), arrived(3 * b + 1), arrived(3 * b + 2))
                        pe.wait_ge(down_done, n)
                        more = pe.value_load(extra_i[0:1, bass.ds(it * 2 + b, 1)], min_val=0, max_val=NG - 1)
                        with pe.If(more > 0):
                            with pe.Fori(0, more) as _g:
                                pe.reg_add(count, count, 1)
                                m = pe.snap(count)
                                block_pass(m, 2, (bank[1], bank[2], bank[3], bank[5], bank[0]), ex, m,
                                           arrived(3 * b), arrived(3 * b + 1), arrived(3 * b + 2))
                                pe.wait_ge(ex["down"], m)
                        pe.sem_inc(slot_free, 3)
                pe.wait_ge(y_ready, E * (i + 1))
                ln_rows(st)

            moe(0, "moe0")

            modulated(2)
            pe.wait_ge(hmT_ready, 2 * NT * 3)
            wa, wb = full(base["in_o"]), full(base["in_o"] + 1)
            for T in range(NT):
                if T:
                    pe.wait_ge(lat_ready, T)
                    pe.wait_ge(kr_ready, T)
                for w, width, ps in ((wa, 384, bank[0]), (wb, 320, bank[1])):
                    for j in range(NJ):
                        mm = pe.matmul(ps[:, 0:width], hmT[:, j, tcols(T)], w[:, width * j:width * j + width],
                                       start=(j == 0), stop=(j == NJ - 1))
                mm.then_inc(lat_done, 1)
                pe.wait_ge(lat_ready, T + 1)
                pe.wait_ge(kr_ready, T + 1)
                if T:
                    pe.wait_ge(latT_ready, T)
                    pe.wait_ge(krT_ready, T)
                for j in range(5):
                    pe.transpose(bank[4 + j // 3][:, P * (j % 3):P * (j % 3) + P], lat[:, P * j:P * j + P], ident)
                pe.transpose(bank[5][:, 2 * P:3 * P], krd, ident).then_inc(latT_done, 1)
            pe.sem_inc(slot_free, 2)
            pe.wait_ge(latT_ready, NT)
            pe.wait_ge(krT_ready, NT)
            wq = [full(base["qb"] + n)[:, 0:768 * 3].rearrange("p (j h n) -> p j h n", j=3, h=4) for n in range(2)]
            wkv = full(base["kvb"]).rearrange("p (j h n) -> p j h n", j=2, h=MH)
            for T in range(NT):
                if T:
                    pe.wait_ge(qr_ready, T)
                for n in range(2):
                    for j in range(3):
                        mm = pe.matmul(bank[6][:, 256 * n:256 * n + 256], qaT[:, j, tcols(T)], wq[n][:, j, :, NOPE:NOPE + ROPE],
                                       start=(j == 0), stop=(j == 2))
                mm.then_inc(qr_done, 1)
                for n in range(2):
                    if 2 * T + n >= 2:
                        pe.wait_ge(v_ready, 2 * T + n - 1)
                    for j in range(2):
                        mm = pe.matmul(bank[n][:, :], kaT[:, j, tcols(T)], wkv[:, j, 4 * n:4 * n + 4, NOPE:NOPE + VD],
                                       start=(j == 0), stop=(j == 1))
                    mm.then_inc(v_done, 1)
                pe.wait_ge(qr_ready, T + 1)
                if T:
                    pe.wait_ge(qrT_ready, T)
                for j in range(4):
                    mm = pe.transpose(bank[7][:, P * j:P * j + P], qr[:, P * j:P * j + P], ident)
                mm.then_inc(qrt_done, 1)
            pe.wait_ge(v_ready, 2 * NT)
            pe.wait_ge(qrT_ready, NT)

            def head_proj(h):
                if h:
                    pe.wait_ge(qkn_ready, h)
                for j in range(3):
                    pe.matmul(bank[0][:, :], wq[h // 4][:, j, h % 4, 0:NOPE], qaT[:, j, :], start=(j == 0), stop=(j == 2))
                for j in range(2):
                    mm = pe.matmul(bank[1][:, :], wkv[:, j, h, 0:NOPE], kaT[:, j, :], start=(j == 0), stop=(j == 1))
                mm.then_inc(qkn_done, 1)

            def scores(u):
                h, i = divmod(u, NT)
                nk = P * (i + 1)
                pe.wait_ge(qkn_ready, h + 1)
                if u >= 2:
                    pe.wait_ge(p_ready, u - 1)
                ps = bank[2 + u % 2]
                half = slice(ROPE * (h % 2), ROPE * (h % 2) + ROPE)
                pe.matmul(ps[:, 0:nk], qnT[h % 2][:, tcols(i)], knT[h % 2][:, 0:nk], start=True, stop=False)
                pe.matmul(ps[:, 0:nk], qrT[half, h // 2, tcols(i)], krT[half, 0:nk], start=False, stop=False)
                pe.matmul(ps[:, nk - P:nk], ident, cc(C_ATT), start=False, stop=True).then_inc(s_done, 1)

            def turn(u):
                h, i = divmod(u, NT)
                pe.wait_ge(pn_ready, u + 1)
                if u >= 2:
                    pe.wait_ge(pt_ready, u - 1)
                for k in range(i + 1):
                    mm = pe.transpose(bank[4 + u % 2][:, P * k:P * k + P], prob[u % 2][:, P * k:P * k + P], ident)
                mm.then_inc(pt_done, 1)

            def values(u):
                h, i = divmod(u, NT)
                pe.wait_ge(pt_ready, u + 1)
                if i == 0 and h >= 2:
                    pe.wait_ge(oT_ready, h - 1)
                for k in range(i + 1):
                    mm = pe.matmul(bank[6 + h % 2][:, tcols(i)], v_tok[:, k, VD * h:VD * h + VD], probT[u % 2][:, P * k:P * k + P],
                                   start=(k == 0), stop=(k == i))
                mm.then_inc(av_done, 1)

            head_proj(0)
            for u in range(MH * NT + 2):
                if u < MH * NT:
                    scores(u)
                    if u % NT == 0 and u // NT + 1 < MH:
                        head_proj(u // NT + 1)
                if 1 <= u <= MH * NT:
                    turn(u - 1)
                if u >= 2:
                    values(u - 2)
            pe.wait_ge(av_done, MH * NT)
            pe.sem_inc(slot_free, 3)
            pe.wait_ge(oT_ready, MH)
            ln_rows(2)
            out_proj("out_o", [oT[:, j, :] for j in range(MH)], 2, lambda: None)
            pe.wait_ge(y_taken, 2 * NT)
            ada("ada11", 3)
            moe(1, "moe1")

        @block.scalar
        def _(act):
            step = InOrder(act, act_step)
            act.dma_start(sml[:, :], small).then_inc(inputs_in, 16)
            act.dma_start(cst[:, :], const).then_inc(inputs_in, 16)
            act.dma_start(rws[:, :], rows).then_inc(inputs_in, 16)
            act.dma_start(intc[:, :], ints).then_inc(inputs_in, 16)
            act.dma_start(xres[:, :, :], x.rearrange("(t p) d -> p t d", p=P)).then_inc(x_in, 16)
            act.wait_ge(inputs_in, 64)
            act.activation(cond[:, :], sml[:, S_C:S_C + NJ], ACT.Silu).then_inc(cond_ready, 1)

            def ada(st):
                for c in range(6):
                    k = 6 * st + c
                    act.wait_ge(ada_done, k + 1)
                    if c == 0 and st:
                        act.wait_ge(hm_ready, NT * st)
                    if c == 4 and st >= 1:
                        act.wait_ge(y_taken if st % 2 == 0 else ln_done, NT * (st // 2) if st % 2 == 0 else NT * st)
                    dst = modss[:, 512 * c:512 * c + 512] if c < 4 else gates[st % 2][:, 512 * (c - 4):512 * (c - 4) + 512]
                    act.activation(dst, bank[c % 2][:, :], ACT.Copy, bias=(0.0 if c < 2 else 1.0)).then_inc(mod_ready, 1)

            def modulated(st):
                for k in range(2 * NT * st, 2 * NT * (st + 1)):
                    T, half = divmod(k - 2 * NT * st, 2)
                    act.wait_ge(tr_done, k + 1)
                    act.activation(hmT[:, 4 * half:4 * half + 4, tcols(T)],
                                   bank[2 + half][:, :].rearrange("p (j t) -> p j t", j=4), ACT.Copy).then_inc(hmT_ready, 1)

            def ln_std(st):
                for T in range(NT):
                    act.wait_ge(var_ready, NT * st + T + 1)
                    act.activation(statb[:, 14:15], statb[:, 13:14], ACT.Sqrt, bias=cst[:, C_EPS5:C_EPS5 + 1]).then_inc(std_ready, 1)

            ada(0)
            modulated(0)
            act.wait_ge(t_ready, 1)
            step(act.activation(g_sp, g_t, ACT.Abs))
            step(act.activation(g_sp, g_sp, ACT.Exp, scale=-1.0))
            step(act.activation(g_sp, g_sp, ACT.Ln, bias=1.0))
            step(act.activation(g_ea, sml[:, S_AL:S_AL + 16], ACT.Exp))
            act.activation(g_beta.rearrange("p (t h) -> p t h", t=NT),
                           bank[6][:, 0:32].rearrange("p (t x) -> p t x", t=NT)[:, :, 0:H], ACT.Exp, scale=-1.0).then_inc(sp_ready, 1)

            def root(m):
                act.wait_ge(ssq_done, m + 1)
                if m >= 2:
                    act.wait_ge(qk_ready, m - 1)
                act.activation(rq[m % 2], bank[4 + m % 2][:, :], ACT.Sqrt, bias=cst[:, C_EPS6:C_EPS6 + 1]).then_inc(rt_ready, 1)

            for m in range(12):
                act.wait_ge(conv_done, m + 1)
                signal(act, act.activation(qkv[:, m, :], qkv[:, m, :], ACT.Silu), silu_done, m + 1)
                if m < 8:
                    if m >= 2:
                        act.wait_ge(ssq_done, m - 1)
                    act.activation(sq[m % 2], qkv[:, m, :], ACT.Square).then_inc(sq_ready, 1)
                if 1 <= m <= 8:
                    root(m - 1)
            act.wait_ge(qk_ready, 8)
            for m in range(8):
                act.wait_ge(proj_done, 13 + m)
                if m == 4:
                    act.wait_ge(y_cleared, 16)
                dst = zs[:, m, :] if m < 4 else scc[:, m - 4, :]
                act.activation(dst, bank[m % 4][:, :], ACT.Silu if m < 4 else ACT.Copy).then_inc(zc_done, 1)
            act.wait_ge(gcs_ready, 1)
            step(act.activation(g_eg, g_gc, ACT.Exp))
            act.activation(g_kd, g_kd, ACT.Exp).then_inc(ge_ready, 1)
            for pair in range(2):
                tiles = [(2 * pair + k, k, [bank[4 * k + n] for n in range(4)]) for k in range(2)]
                for T, k, B in tiles:
                    act.wait_ge(gcb_done, T + 1)
                    act.wait_ge(gates_ready, 1)
                    act.activation(d_U[k], B[0][:, :].rearrange("p (h t) -> p h t", h=H), ACT.Exp).then_inc(eb_ready, 1)
                    act.wait_ge(dd_ready, T + 1)
                    step(act.activation(d_KB[k], d_KB[k], ACT.Exp))
                    act.activation(d_MT[k], d_MT[k], ACT.Exp, scale=-1.0).then_inc(dx_ready, 1)
                for T, k, B in tiles:
                    act.wait_ge(xt_done, T + 1)
                    act.activation(d_Y[k], B[0][:, :].rearrange("p (h t) -> p h t", h=H), ACT.Copy).then_inc(y0_ready, 1)
                for T, k, B in tiles:
                    act.wait_ge(kt_done, T + 1)
                    for h in range(H):
                        q = NT * T + h
                        act.activation(d_KB[k][:, h, :], B[0][:, P * h:P * h + P], ACT.Copy, scale=g_beg[:, q:q + 1])
                        ins = act.activation(d_KD[k][:, h, :], B[0][:, P * h:P * h + P], ACT.Copy, scale=g_kd[:, q:q + 1])
                    ins.then_inc(kd_ready, 1)
                for T, k, B in tiles:
                    act.wait_ge(vt_done, T + 1)
                    for h in range(H):
                        q = NT * T + h
                        ins = act.activation(qkv[:, 8 + h, tcols(T)], B[0][:, P * h:P * h + P], ACT.Copy, scale=g_beta[:, q:q + 1])
                    ins.then_inc(vb_ready, 1)
                for T, k, B in tiles:
                    act.wait_ge(uw_done, T + 1)
                    act.activation(d_U[k], B[1][:, :].rearrange("p (h t) -> p h t", h=H), ACT.Copy).then_inc(u_ready, 1)
                for T, k, B in tiles:
                    act.wait_ge(o_done, 2 * T + 2)
                    if T:
                        act.wait_ge(ot_done, T)
                    for h in range(H):
                        step(act.activation(os_[:, h, :], B[3][:, P * h:P * h + P], ACT.Square, accum_out=g_ms[:, NT * T + h:NT * T + h + 1]))
                    act.activation(g_ms[:, NT * T:NT * T + H], g_ms[:, NT * T:NT * T + H], ACT.Sqrt, scale=1.0 / DK,
                                   bias=cst[:, C_EPS6:C_EPS6 + 1]).then_inc(orms_ready, 1)
                    act.wait_ge(orec_ready, T + 1)
                    for h in range(H):
                        ins = act.activation(os_[:, h, :], B[3][:, P * h:P * h + P], ACT.Copy, scale=g_ms[:, NT * T + h:NT * T + h + 1])
                    ins.then_inc(os_ready, 1)
            ln_std(0)
            ada(1)

            count = act.alloc_register("act_extra")
            act.reg_mov(count, 0)
            row = act.alloc_register("extra_row")

            def moe(i):
                st = 2 * i + 1
                for T in range(NT):
                    act.wait_ge(hm_ready, NT * st + T + 1)
                    act.dma_start(hm_rows[i][P * T:P * T + P, :], hm[T % 2]).then_inc(hm_stored[T % 2], 16)
                    for half in range(2):
                        act.wait_ge(tr_done, 2 * (NT * st + T) + half + 1)
                        act.activation(hmT[:, 4 * half:4 * half + 4, tcols(T)],
                                       bank[2 + half][:, :].rearrange("p (j t) -> p j t", j=4), ACT.Copy).then_inc(hmT_ready, 1)
                act.wait_ge(logit_done, i + 1)
                act.activation(r_sc, bank[4][:, 0:P], ACT.Sigmoid).then_inc(score_ready, 1)
                if i == 0:
                    ada(2)
                act.wait_ge(dest_ready, i + 1)

                def block_pass(n, b, banks, s, row):
                    bt, bg, bd = banks
                    act.wait_ge(s["t"], n)
                    act.activation(xT[b], bt[:, :].rearrange("p (j s) -> p j s", j=NJ), ACT.Copy).then_inc(s["xT"], 1)
                    act.wait_ge(s["gate"], n)
                    act.activation(sg[b], bg[:, 0:256], ACT.Silu).then_inc(s["silu"], 1)
                    act.wait_ge(s["y"], n)
                    for hf in range(2):
                        act.dma_start(y_rows[bass.ds(row, BLK), 512 * hf:512 * hf + 512],
                                      yb[b][BLK * hf:BLK * hf + BLK, :]).then_inc(s["stored"], 16)

                act.reg_mov(row, BLK * E)
                regular = [dict(t=t_done, xT=xT_ready, gate=gate_done, silu=silu_ready, y=y_ready, stored=y_stored[b])
                           for b in range(2)]
                with act.Fori(0, E // 2) as it:
                    for b in range(2):
                        n = act.snap(it * 2 + (E * i + b + 1))
                        block_pass(n, b, (bank[4], bank[2], bank[6 + b]), regular[b], it * (2 * BLK) + BLK * b)
                        more = act.value_load(extra_i[0:1, bass.ds(it * 2 + b, 1)], min_val=0, max_val=NG - 1)
                        with act.If(more > 0):
                            with act.Fori(0, more) as _g:
                                act.reg_add(count, count, 1)
                                m = act.snap(count)
                                r = act.snap(row)
                                act.reg_add(row, row, BLK)
                                block_pass(m, 2, (bank[1], bank[2], bank[0]), ex, r)
                ln_std(st)

            moe(0)
            modulated(2)

            act.wait_ge(ang_ready, 1)
            step(act.activation(sn_t, ang.rearrange("p (t f) -> p t f", t=NT), ACT.Sin))
            step(act.activation(kround, ang, ACT.Abs))
            act.activation(cs_t, kround.rearrange("p (t f) -> p t f", t=NT), ACT.Sin, scale=-1.0,
                           bias=cst[:, C_HPI:C_HPI + 1]).then_inc(sin_ready, 1)
            for T in range(NT):
                act.wait_ge(lat_done, T + 1)
                if T:
                    act.wait_ge(latT_done, T)
                step(act.activation(lat[:, 0:384], bank[0][:, 0:384], ACT.Square, accum_out=ms_o[:, 8 * T:8 * T + 1]))
                step(act.activation(lat[:, 384:640], bank[1][:, 0:256], ACT.Square, accum_out=ms_o[:, 8 * T + 1:8 * T + 2]))
                step(act.activation(ms_o[:, 8 * T + 2:8 * T + 3], ms_o[:, 8 * T:8 * T + 1], ACT.Sqrt, scale=1.0 / Q_LORA,
                                    bias=cst[:, C_EPS6:C_EPS6 + 1]))
                act.activation(ms_o[:, 8 * T + 3:8 * T + 4], ms_o[:, 8 * T + 1:8 * T + 2], ACT.Sqrt, scale=1.0 / KV_LORA,
                               bias=cst[:, C_EPS6:C_EPS6 + 1]).then_inc(lms_ready, 1)
                act.wait_ge(lrs_ready, T + 1)
                act.activation(lat[:, 0:384], bank[0][:, 0:384], ACT.Copy, scale=ms_o[:, 8 * T + 4:8 * T + 5])
                act.activation(lat[:, 384:640], bank[1][:, 0:256], ACT.Copy, scale=ms_o[:, 8 * T + 5:8 * T + 6]).then_inc(lat_ready, 1)
                act.wait_ge(latT_done, T + 1)
                for j in range(5):
                    dst = qaT[:, j, tcols(T)] if j < 3 else kaT[:, j - 3, tcols(T)]
                    w = S_QN + j if j < 3 else S_KN + j - 3
                    ins = act.activation(dst, bank[4 + j // 3][:, P * (j % 3):P * (j % 3) + P], ACT.Copy, scale=sml[:, w:w + 1])
                ins.then_inc(latT_ready, 1)
            for T in range(NT):
                for n in range(2):
                    act.wait_ge(v_done, 2 * T + n + 1)
                    act.activation(v_tok[:, T, 512 * n:512 * n + 512], bank[n][:, :], ACT.Copy).then_inc(v_ready, 1)
                act.wait_ge(qrt_done, T + 1)
                act.activation(qrT[:, :, tcols(T)], bank[7][:, :].rearrange("p (j t) -> p j t", j=4), ACT.Copy).then_inc(qrT_ready, 1)

            scale = float(NOPE + ROPE) ** -0.5

            def head_copy(h):
                act.wait_ge(qkn_done, h + 1)
                if h >= 2:
                    act.wait_ge(s_done, NT * (h - 1))
                step(act.activation(qnT[h % 2], bank[0][:, :], ACT.Copy))
                act.activation(knT[h % 2], bank[1][:, :], ACT.Copy).then_inc(qkn_ready, 1)

            head_copy(0)
            for u in range(MH * NT + 2):
                if u < MH * NT:
                    h, i = divmod(u, NT)
                    nk = P * (i + 1)
                    act.wait_ge(nm_ready, u + 1)
                    if u >= 2:
                        act.wait_ge(pt_done, u - 1)
                    act.activation(prob[u % 2][:, 0:nk], bank[2 + u % 2][:, 0:nk], ACT.Exp, bias=att_n[:, u:u + 1], scale=scale,
                                   accum_out=att_s[:, u:u + 1]).then_inc(p_ready, 1)
                    if i == 0 and h + 1 < MH:
                        head_copy(h + 1)
                if 1 <= u <= MH * NT:
                    v = u - 1
                    nk = P * (v % NT + 1)
                    act.wait_ge(pt_done, v + 1)
                    if v >= 2:
                        act.wait_ge(av_done, v - 1)
                    act.activation(probT[v % 2][:, 0:nk], bank[4 + v % 2][:, 0:nk], ACT.Copy).then_inc(pt_ready, 1)
                if u >= 2 and (u - 2) % NT == NT - 1:
                    h = (u - 2) // NT
                    act.wait_ge(av_done, NT * (h + 1))
                    act.activation(oT[:, h, :], bank[6 + h % 2][:, :], ACT.Copy).then_inc(oT_ready, 1)
            ln_std(2)
            ada(3)
            moe(1)
            for T in range(NT):
                act.wait_ge(ln_done, NT * 3 + T + 1)
                act.dma_start(out[P * T:P * T + P, :], xres[:, T, :]).then_inc(out_stored, 16)
            act.wait_ge(out_stored, 16 * NT)

        @block.vector
        def _(dve):
            step = InOrder(dve, dve_step)

            def modulate(st, T):
                k = NT * st + T
                if T >= 2:
                    dve.wait_ge(tr_done, 2 * (k - 1))
                    if st % 2:
                        dve.wait_ge(hm_stored[T % 2], 16 * (NT // 2 * (st // 2) + T // 2))
                step(dve.tensor_tensor(hm[T % 2], xres[:, T, :], modss[:, 1024:2048], ALU.mult))
                signal(dve, dve.tensor_tensor(hm[T % 2], hm[T % 2], modss[:, 0:1024], ALU.add), hm_ready, k + 1)

            def layer_norm(st, T, halves, taken):
                g, lnr = gates[st % 2], lnrs[st % 2]
                dve.wait_ge(mod_ready, 6 * (st + 1))
                for n in range(2):
                    ins = dve.tensor_tensor(lnr[:, 512 * n:512 * n + 512], halves[n], g[:, 512 * n:512 * n + 512], ALU.mult)
                    if n == 0:
                        step(ins)
                taken(ins)
                step(dve.scalar_tensor_tensor(out=lnr, in0=xres[:, T, :], scalar=DN_ALPHA, in1=lnr, op0=ALU.mult, op1=ALU.add))
                for n in range(2):
                    step(dve.bn_stats(statb[:, 6 * n:6 * n + 6], lnr[:, 512 * n:512 * n + 512]))
                k = NT * st + T
                signal(dve, dve.bn_aggr(statb[:, 12:14], statb[:, 0:12]), var_ready, k + 1)
                dve.wait_ge(std_ready, k + 1)
                step(dve.reciprocal(statb[:, 15:16], statb[:, 14:15]))
                step(dve.tensor_scalar(lnr, lnr, statb[:, 12:13], statb[:, 15:16], ALU.subtract, ALU.mult))
                if T == 0:
                    dve.wait_ge(rows_done, st + 1)
                for n in range(2):
                    c = slice(512 * n, 512 * n + 512)
                    step(dve.tensor_tensor(lnr[:, c], lnr[:, c], bank[4 + n][:, :], ALU.mult))
                for n in range(2):
                    c = slice(512 * n, 512 * n + 512)
                    ins = dve.tensor_tensor(xres[:, T, c], lnr[:, c], bank[6 + n][:, :], ALU.add)
                    if n == 0:
                        step(ins)
                signal(dve, ins, ln_done, k + 1)

            dve.wait_ge(x_in, 16)
            dve.wait_ge(mod_ready, 4)
            for T in range(NT):
                modulate(0, T)

            dve.wait_ge(inputs_in, 64)
            dve.wait_ge(ba_done, 1)
            t3 = g_t.rearrange("p (t h) -> p t h", t=NT)
            signal(dve, dve.tensor_tensor(t3, bank[6][:, 0:32].rearrange("p (t x) -> p t x", t=NT)[:, :, H:2 * H],
                                          sml[:, S_DT:S_DT + 16].rearrange("p (t h) -> p t h", t=NT), ALU.add), t_ready, 1)
            dve.wait_ge(sp_ready, 1)
            step(dve.scalar_tensor_tensor(out=g_g, in0=g_t, scalar=0.0, in1=g_sp, op0=ALU.max, op1=ALU.add))
            signal(dve, dve.scalar_tensor_tensor(out=g_g, in0=g_g, scalar=-1.0, in1=g_ea, op0=ALU.mult, op1=ALU.mult), g_ready, 1)
            step(dve.tensor_scalar(g_beta, g_beta, 1.0, None, ALU.add))
            step(dve.reciprocal(g_beta, g_beta))

            def conv(ps, acc, w, taps):
                step(dve.tensor_scalar(acc, ps, sml[:, w + taps - 1:w + taps], None, ALU.mult))
                for i in range(1, taps):
                    ins = dve.scalar_tensor_tensor(out=acc[:, i:SEQ], in0=ps[:, 0:SEQ - i], scalar=sml[:, w + taps - 1 - i:w + taps - i],
                                                   in1=acc[:, i:SEQ], op0=ALU.mult, op1=ALU.add)
                    if i < taps - 1:
                        step(ins)
                return ins

            def normalize(m):
                dve.wait_ge(rt_ready, m + 1)
                step(dve.reciprocal(rq[m % 2], rq[m % 2]))
                dve.wait_ge(sq_ready, m + 1)
                signal(dve, dve.scalar_tensor_tensor(out=qkv[:, m, :], in0=qkv[:, m, :], scalar=(DK ** -0.5 if m < H else 1.0),
                                                     in1=rq[m % 2], op0=ALU.mult, op1=ALU.mult), qk_ready, m + 1)

            for m in range(12):
                dve.wait_ge(proj_done, m + 1)
                signal(dve, conv(bank[m % 4][:, :], qkv[:, m, :], S_CW + 4 * m, 4), conv_done, m + 1)
                if 2 <= m < 10:
                    normalize(m - 2)
            dve.wait_ge(gc_done, 1)
            step(dve.tensor_copy(g_gc, bank[7][:, 0:16]))
            signal(dve, dve.tensor_tensor(g_kd, bank[7][:, 16:32], g_gc, ALU.subtract), gcs_ready, 1)
            for t in range(4):
                dve.wait_ge(proj_done, 21 + t)
                dve.wait_ge(zc_done, 5 + t)
                signal(dve, dve.tensor_tensor(scc[:, t, :], bank[t][:, :], scc[:, t, :], ALU.mult), sc_read, t + 1)
                step(conv(scc[:, t, :], yb_T[:, t, :], S_SW + 3 * t, 3))
            for t in range(4):
                dve.wait_ge(proj_done, 25 + t)
                signal(dve, dve.tensor_tensor(yb_T[:, t, :], bank[t][:, :], yb_T[:, t, :], ALU.mult), sc_read, 5 + t)
            dve.wait_ge(ge_ready, 1)
            signal(dve, dve.tensor_tensor(g_beg, g_beta, g_eg, ALU.mult), gates_ready, 1)
            signal(dve, dve.memset(state, 0.0), s_ready, 1)

            def heads(ap):
                return ap.rearrange("p (h t) -> p h t", h=H)

            for pair in range(2):
                tiles = [(2 * pair + k, k, [bank[4 * k + n] for n in range(4)]) for k in range(2)]
                for T, k, B in tiles:
                    if pair:
                        dve.wait_ge(ot_done, NT // 2)
                    for h in range(H):
                        ins = dve.tensor_scalar(d_MT[k][:, h, :], cc(C_CUM), g_g[:, NT * T + h:NT * T + h + 1], None, ALU.mult)
                        if h < H - 1:
                            step(ins)
                    signal(dve, ins, cg_ready, T + 1)
                for T, k, B in tiles:
                    dve.wait_ge(kq_done, T + 1)
                    dve.wait_ge(eb_ready, T + 1)
                    for h in range(H):
                        q = NT * T + h
                        step(dve.scalar_tensor_tensor(out=d_KB[k][:, h, :], in0=B[0][:, P * h:P * h + P], scalar=g_gc[:, q:q + 1],
                                                      in1=cc(C_DCT), op0=ALU.subtract, op1=ALU.add))
                        ins = dve.scalar_tensor_tensor(out=d_MT[k][:, h, :], in0=B[0][:, P * h:P * h + P], scalar=g_gc[:, q:q + 1],
                                                       in1=cc(C_DEC), op0=ALU.subtract, op1=ALU.add)
                        if h < H - 1:
                            step(ins)
                    signal(dve, ins, dd_ready, T + 1)
                for T, k, B in tiles:
                    dve.wait_ge(dx_ready, T + 1)
                    dve.wait_ge(eb_ready, T + 1)
                    for h in range(H):
                        step(dve.scalar_tensor_tensor(out=d_L[k][:, h, :], in0=B[1][:, P * h:P * h + P],
                                                      scalar=g_beta[:, NT * T + h:NT * T + h + 1], in1=d_MT[k][:, h, :],
                                                      op0=ALU.mult, op1=ALU.mult))
                    step(dve.tensor_tensor(d_IT[k], heads(B[2][:, :]), d_KB[k], ALU.mult))
                    step(dve.tensor_copy(g_last[:, T, :, :], d_U[k][:, :, CH - 1:P:CH]))
                    step(dve.tensor_tensor(qkv[:, 0:H, tcols(T)], qkv[:, 0:H, tcols(T)], d_U[k], ALU.mult))
                    step(dve.tensor_tensor(d_X[k], d_L[k], cc(C_LEV).unsqueeze(1).to_broadcast([P, H, P]), ALU.mult))
                    signal(dve, dve.scalar_tensor_tensor(out=d_X[k], in0=d_X[k], scalar=-1.0,
                                                         in1=ident.unsqueeze(1).to_broadcast([P, H, P]),
                                                         op0=ALU.mult, op1=ALU.add), x0_ready, T + 1)
                for lv in range(5):
                    for T, k, B in tiles:
                        n = (pair * 5 + lv) * 2 + k
                        dve.wait_ge(mt_done, n + 1)
                        signal(dve, dve.tensor_tensor(d_MT[k], heads(B[1][:, :]),
                                                      cc(C_LEV + P * (lv + 1)).unsqueeze(1).to_broadcast([P, H, P]), ALU.mult),
                               mt_ready, n + 1)
                    for T, k, B in tiles:
                        n = (pair * 5 + lv) * 2 + k
                        dve.wait_ge(y2_done, n + 1)
                        step(dve.tensor_tensor(d_Y[k], d_Y[k], heads(B[2][:, :]), ALU.subtract))
                        signal(dve, dve.tensor_tensor(d_X[k], d_X[k], heads(B[3][:, :]), ALU.subtract), lv_ready, n + 1)
                for T, k, B in tiles:
                    dve.wait_ge(uw_done, T + 1)
                    signal(dve, dve.tensor_copy(qkv[:, H:2 * H, tcols(T)], heads(B[2][:, :])), wt_ready, T + 1)
                for T, k, B in tiles:
                    dve.wait_ge(u_ready, T + 1)
                    for c in range(2):
                        n, r = 2 * T + c, slice(CH * c, CH * c + CH)
                        dve.wait_ge(vn_done, n + 1)
                        signal(dve, dve.tensor_tensor(d_U[k][r, :, :], d_U[k][r, :, :], heads(B[0][r, :]), ALU.subtract), vn_ready, n + 1)
                        dve.wait_ge(sd_done, n + 1)
                        dve.wait_ge(o_done, n + 1)
                        for h in range(H):
                            ins = dve.scalar_tensor_tensor(out=state[:, h, :], in0=state[:, h, :], scalar=g_last[:, T, h, c:c + 1],
                                                           in1=B[1][:, P * h:P * h + P], op0=ALU.mult, op1=ALU.add)
                            if h < H - 1:
                                step(ins)
                        signal(dve, ins, s_ready, n + 2)
                    dve.wait_ge(orms_ready, T + 1)
                    signal(dve, dve.reciprocal(g_ms[:, NT * T:NT * T + H], g_ms[:, NT * T:NT * T + H]), orec_ready, T + 1)
                    dve.wait_ge(ot_done, T + 1)
                    signal(dve, dve.scalar_tensor_tensor(out=zs[:, :, tcols(T)], in0=heads(B[2][:, :]), scalar=sml[:, S_NW:S_NW + 1],
                                                         in1=zs[:, :, tcols(T)], op0=ALU.mult, op1=ALU.mult), ya_ready, T + 1)

            def mixer_norm(st):
                for T in range(NT):
                    k = NT * (st // 2) + T
                    dve.wait_ge(y_done, k + 1)
                    layer_norm(st, T, [bank[2 * (T % 2) + n][:, :] for n in range(2)],
                               lambda ins: signal(dve, ins, y_taken, k + 1))

            count = dve.alloc_register("dve_extra")
            dve.reg_mov(count, 0)

            def moe(i):
                st = 2 * i + 1
                dve.wait_ge(mod_ready, 6 * st + 4)
                for T in range(NT):
                    modulate(st, T)
                if i == 0:
                    dve.wait_ge(hmT_ready, 2 * NT * (st + 1))
                for b in range(2):
                    dve.wait_ge(hm_stored[b], 16 * NT // 2 * (i + 1))
                dve.wait_ge(hmT_ready, 2 * NT * (st + 1))

                def v4(ap, n=E):
                    return ap[:, 0:NT * n].rearrange("p (t e) -> p t e", t=NT)
                sc, bi, tmp, o1, o2, oh, rk, gf, ad, yr = [v4(a) for a in (r_sc, r_bi, r_tmp, r_o1, r_o2, r_oh, r_rk, r_gf, r_ad, r_yr)]
                iota = cc(C_IO, E).unsqueeze(1).to_broadcast([P, NT, E])
                step(dve.memset(r_gs, -BIG))
                dve.wait_ge(score_ready, i + 1)
                step(dve.tensor_tensor(bi, sc, sml[:, S_RB:S_RB + E].unsqueeze(1).to_broadcast([P, NT, E]), ALU.add))
                for q in range(NT * GROUPS):
                    step(dve.max(r_m8[:, 8 * q:8 * q + 8], r_bi[:, 8 * q:8 * q + 8]))
                m8 = r_m8.rearrange("p (t g k) -> p t g k", t=NT, g=GROUPS)
                gs = v4(r_gs, 8)
                step(dve.tensor_tensor(gs[:, :, 0:GROUPS], m8[:, :, :, 0], m8[:, :, :, 1], ALU.add))
                for T in range(NT):
                    c = slice(8 * T, 8 * T + 8)
                    step(dve.max(r_gm[:, c], r_gs[:, c]))
                    step(dve.max_index(mi[:, c], r_gm[:, c], r_gs[:, c]))
                grp = r_sm[:, 0:NT]
                step(dve.tensor_copy(grp, mi[:, 0:32:8]))
                go = r_sm[:, 16:32].rearrange("p (t g) -> p t g", t=NT)
                step(dve.tensor_tensor(go, cc(C_IO, GROUPS).unsqueeze(1).to_broadcast([P, NT, GROUPS]),
                                       grp.unsqueeze(2).to_broadcast([P, NT, GROUPS]), ALU.is_equal))
                step(dve.tensor_tensor(r_tmp.rearrange("p (q k) -> p q k", k=EPG), r_bi.rearrange("p (q k) -> p q k", k=EPG),
                                       r_sm[:, 16:32].unsqueeze(2).to_broadcast([P, NT * GROUPS, EPG]), ALU.mult))
                step(dve.tensor_reduce(v4(r_ig, 8), r_tmp.rearrange("p (t g k) -> p t k g", t=NT, g=GROUPS), AX.X, ALU.add))
                for T in range(NT):
                    c = slice(8 * T, 8 * T + 8)
                    step(dve.max(r_lm[:, c], r_ig[:, c]))
                    step(dve.max_index(mi[:, c], r_lm[:, c], r_ig[:, c]))
                for k, o in ((0, o1), (1, o2)):
                    ek = r_sm[:, 4 + 4 * k:8 + 4 * k]
                    step(dve.tensor_copy(ek, mi[:, k:32:8]))
                    step(dve.scalar_tensor_tensor(out=ek, in0=grp, scalar=float(EPG), in1=ek, op0=ALU.mult, op1=ALU.add))
                    step(dve.tensor_tensor(o, iota, ek.unsqueeze(2).to_broadcast([P, NT, E]), ALU.is_equal))
                signal(dve, dve.tensor_tensor(oh, o1, o2, ALU.add), oh_ready, i + 1)
                for k, o in ((0, o1), (1, o2)):
                    step(dve.tensor_tensor(tmp, sc, o, ALU.mult))
                    step(dve.tensor_reduce(wsel[:, 4 * k:4 * k + 4], tmp, AX.X, ALU.add))
                ws = r_sm[:, 12:16]
                step(dve.tensor_tensor(ws, wsel[:, 0:4], wsel[:, 4:8], ALU.add))
                step(dve.reciprocal(ws, ws))
                for k in range(2):
                    step(dve.tensor_tensor(wsel[:, 4 * k:4 * k + 4], wsel[:, 4 * k:4 * k + 4], ws, ALU.mult))
                dve.wait_ge(rank_done, i + 1)
                step(dve.tensor_copy(rk, bank[5][:, 0:P].rearrange("p (t e) -> p t e", t=NT)))

                def floor64(dst, src):
                    step(dve.tensor_scalar(dst, src, 1.0 / BLK, -(BLK - 1.0) / (2 * BLK), ALU.mult, ALU.add))
                    step(dve.tensor_scalar(dst, dst, MAGIC, None, ALU.add))
                    step(dve.tensor_scalar(dst, dst, MAGIC, None, ALU.subtract))
                floor64(gf, rk)
                step(dve.scalar_tensor_tensor(out=ad, in0=rk, scalar=float(NG * E), in1=iota, op0=ALU.mult, op1=ALU.add))
                step(dve.scalar_tensor_tensor(out=ad, in0=gf, scalar=float(E - BLK * NG * E), in1=ad, op0=ALU.mult, op1=ALU.add))
                cnt, bef = r_sm[:, 64:64 + E], r_sm[:, 96:96 + E]
                step(dve.tensor_scalar(cnt, bank[5][:, P:P + E], 1.0, -1.0, ALU.max, ALU.add))
                floor64(cnt, cnt)
                step(dve.tensor_tensor_scan(bef, ones[:, 0:E], cnt, 0.0, ALU.mult, ALU.add))
                step(dve.tensor_tensor(bef, bef, cnt, ALU.subtract))
                step(dve.tensor_scalar(bef, bef, float(BLK), float(BLK * (E - 1)), ALU.mult, ALU.add))
                step(dve.tensor_tensor(bef, bef, cc(C_IO64, E), ALU.subtract))
                step(dve.tensor_scalar(yr, gf, 1.0, None, ALU.min))
                step(dve.tensor_tensor(yr, yr, bef.unsqueeze(1).to_broadcast([P, NT, E]), ALU.mult))
                step(dve.tensor_tensor(yr, yr, rk, ALU.add))
                step(dve.tensor_tensor(yr, yr, cc(C_IO64, E).unsqueeze(1).to_broadcast([P, NT, E]), ALU.add))
                for n, (a, o) in enumerate(((ad, o1), (ad, o2), (yr, o1), (yr, o2))):
                    step(dve.tensor_tensor(tmp, a, o, ALU.mult))
                    step(dve.tensor_reduce(r_sm[:, 32 + 4 * n:36 + 4 * n], tmp, AX.X, ALU.add))
                step(dve.tensor_copy(dest_i[:, :], r_sm[:, 32:48]))
                signal(dve, dve.tensor_copy(extra_i[:, :], cnt[0:1, :]), dest_ready, i + 1)

                def block_pass(n, b, banks, s, stored):
                    bu, bh, bd = banks
                    dve.wait_ge(s["silu"], n)
                    dve.wait_ge(s["up"], n)
                    dve.tensor_tensor(hb[b], sg[b], bu[:, 0:256], ALU.mult).then_inc(s["h"], 1)
                    dve.wait_ge(s["ht"], n)
                    dve.tensor_copy(hts[b], bh[:, 0:256]).then_inc(s["hts"], 1)
                    dve.wait_ge(s["down"], n)
                    stored()
                    dve.tensor_copy(yb[b], bd[:, :]).then_inc(s["y"], 1)

                regular = dict(silu=silu_ready, up=up_done, h=h_ready, ht=ht_done, hts=hts_ready, down=down_done, y=y_ready)
                with dve.Fori(0, E // 2) as it:
                    for b in range(2):
                        n = dve.snap(it * 2 + (E * i + b + 1))
                        block_pass(n, b, (bank[3], bank[5], bank[6 + b]), regular,
                                   lambda: dve.wait_ge(y_stored[b], it * 32 + 32 * (E // 2) * i))
                        more = dve.value_load(extra_i[0:1, bass.ds(it * 2 + b, 1)], min_val=0, max_val=NG - 1)
                        with dve.If(more > 0):
                            with dve.Fori(0, more) as _g:
                                before = dve.snap(count) * 32
                                dve.wait_ge(ex["stored"], before)
                                dve.reg_add(count, count, 1)
                                m = dve.snap(count)
                                block_pass(m, 2, (bank[3], bank[5], bank[0]), ex, lambda: None)
                for T in range(NT):
                    k = NT * i + T
                    dve.wait_ge(y_back[T % 2], 32 * (NT // 2 * i + T // 2 + 1))
                    y = ycomb[T % 2]
                    step(dve.tensor_scalar(y[:, 0, :], y[:, 0, :], wsel[:, T:T + 1], None, ALU.mult))
                    step(dve.scalar_tensor_tensor(out=y[:, 0, :], in0=y[:, 1, :], scalar=wsel[:, 4 + T:5 + T], in1=y[:, 0, :],
                                                  op0=ALU.mult, op1=ALU.add))
                    layer_norm(st, T, [y[:, 0, 512 * n:512 * n + 512] for n in range(2)],
                               lambda ins: signal(dve, ins, y_used, k + 1))

            mixer_norm(0)
            moe(0)
            dve.wait_ge(mod_ready, 6 * 2 + 4)
            for T in range(NT):
                modulate(2, T)

            dve.wait_ge(hmT_ready, 2 * NT * 3)
            posf = ms_o[:, 28:32]
            step(dve.tensor_copy(posf, intc[:, 0:NT]))
            for T in range(NT):
                step(dve.tensor_scalar(ang[:, 32 * T:32 * T + 32], sml[:, S_INV:S_INV + 32], posf[:, T:T + 1], None, ALU.mult))
            step(dve.tensor_scalar(kround, ang, 1.0 / TWO_PI, None, ALU.mult))
            step(dve.tensor_scalar(kround, kround, MAGIC, None, ALU.add))
            step(dve.tensor_scalar(kround, kround, MAGIC, None, ALU.subtract))
            for part in (PI_A, PI_B, PI_C):
                step(dve.scalar_tensor_tensor(out=ang, in0=kround, scalar=-part, in1=ang, op0=ALU.mult, op1=ALU.add))
            signal(dve, dve.tensor_scalar(ang, ang, 3.1415925, -3.1415925, ALU.min, ALU.max), ang_ready, 1)
            dve.wait_ge(sin_ready, 1)

            def rotate(src, dst, n, T, last):
                cos = cs_t[:, T, :].unsqueeze(1).to_broadcast([P, n, 32])
                sin = sn_t[:, T, :].unsqueeze(1).to_broadcast([P, n, 32])
                x1, x2 = src[:, :, 0:32], src[:, :, 32:64]
                a, b = rt1[:, 0:n, :], rt2[:, 0:n, :]
                step(dve.tensor_tensor(a, x1, cos, ALU.mult))
                step(dve.tensor_tensor(b, x2, sin, ALU.mult))
                step(dve.tensor_tensor(dst[:, :, 0:32], a, b, ALU.subtract))
                step(dve.tensor_tensor(a, x2, cos, ALU.mult))
                step(dve.tensor_tensor(b, x1, sin, ALU.mult))
                last(dve.tensor_tensor(dst[:, :, 32:64], a, b, ALU.add))

            for T in range(NT):
                dve.wait_ge(lms_ready, T + 1)
                signal(dve, dve.reciprocal(ms_o[:, 8 * T + 4:8 * T + 6], ms_o[:, 8 * T + 2:8 * T + 4]), lrs_ready, T + 1)
                if T:
                    dve.wait_ge(latT_done, T)
                dve.wait_ge(lat_ready, T + 1)
                rotate(bank[1][:, 256:320].rearrange("p (h f) -> p h f", h=1), krd[:, 0:ROPE].rearrange("p (h f) -> p h f", h=1), 1, T, step)
                signal(dve, dve.tensor_copy(krd[:, ROPE:2 * ROPE], krd[:, 0:ROPE]), kr_ready, T + 1)
                dve.wait_ge(latT_done, T + 1)
                dve.wait_ge(latT_ready, T + 1)
                signal(dve, dve.tensor_copy(krT[:, tcols(T)], bank[5][:, 2 * P:3 * P]), krT_ready, T + 1)
            for T in range(NT):
                dve.wait_ge(qr_done, T + 1)
                if T:
                    dve.wait_ge(qrt_done, T)
                rotate(bank[6][:, :].rearrange("p (h f) -> p h f", h=MH), qr.rearrange("p (h f) -> p h f", h=MH), MH, T,
                       lambda ins: signal(dve, ins, qr_ready, T + 1))

            scale = float(NOPE + ROPE) ** -0.5
            for u in range(MH * NT + 1):
                if u < MH * NT:
                    nk = P * (u % NT + 1)
                    dve.wait_ge(s_done, u + 1)
                    step(dve.tensor_reduce(att_m[:, u:u + 1], bank[2 + u % 2][:, 0:nk], AX.X, ALU.max))
                    signal(dve, dve.tensor_scalar(att_n[:, u:u + 1], att_m[:, u:u + 1], -scale, None, ALU.mult), nm_ready, u + 1)
                if u >= 1:
                    v = u - 1
                    nk = P * (v % NT + 1)
                    dve.wait_ge(p_ready, v + 1)
                    step(dve.reciprocal(att_r[:, v:v + 1], att_s[:, v:v + 1]))
                    signal(dve, dve.tensor_scalar(prob[v % 2][:, 0:nk], prob[v % 2][:, 0:nk], att_r[:, v:v + 1], None, ALU.mult),
                           pn_ready, v + 1)
            mixer_norm(2)
            moe(1)

        @block.gpsimd
        def _(pool):
            pool.memset(idx_all[:, :], SEQ).then_inc(idx_filled, 1)
            pool.wait_ge(idx_filled, 1)
            for i in range(DEPTH):
                pool.dma_start(tok_idx[i].rearrange("(s n) o -> s (n o)", s=BLK), idx_all[:, :]).then_inc(idx_cleared, 16)

            count = pool.alloc_register("pool_extra")
            pool.reg_mov(count, 0)

            pool.wait_ge(proj_done, 1)
            signal(pool, pool.memset(area_b[0:120, 0:1024], 0.0), pool_step, 1)
            pool.dma_start(y_rows[BLK * E:BLK * E + 960, :].rearrange("(p r) d -> p r d", p=120),
                           area_b[0:120, 0:1024].unsqueeze(1).to_broadcast([120, 8, 1024])).then_inc(y_cleared, 16)

            def moe(i):
                pool.wait_ge(dest_ready, i + 1)
                pool.wait_ge(idx_cleared, 16 * DEPTH)
                pool.wait_ge(y_cleared, 16)
                for b in range(3):
                    ins = pool.memset(xg[b][0:BLK, :], 0.0)
                    signal(pool, ins, pool_step, 3 * i + b + 2)
                for k in range(2):
                    for T in range(NT):
                        c = 4 * k + T
                        pool.indirect_dma_start(out=tok_idx[i], out_offset=bass.IndirectOffsetOnAxis(dest_i[:, c:c + 1], 0),
                                                in_=intc[:, 4 + T:5 + T],
                                                in_offset=None).then_inc(idx_scattered, 16)
                pool.wait_ge(idx_scattered, 16 * 8 * (i + 1))
                pool.dma_start(idx_all[:, :], tok_idx[i].rearrange("(s n) o -> s (n o)", s=BLK)).then_inc(idx_loaded, 16)
                pool.wait_ge(idx_loaded, 16 * (i + 1))
                for b in range(2):
                    pool.wait_ge(hm_stored[b], 16 * NT // 2 * (i + 1))

                def gather(n, b, col, s, guard):
                    guard()
                    pool.tensor_copy(idx_col[:, b:b + 1], idx_all[:, bass.ds(col, 1)]).then_inc(s["col"], 1)
                    pool.wait_ge(s["col"], n)
                    pool.sem_inc(col_seen, 1)
                    pool.indirect_dma_start(out=xg[b][0:BLK, :], out_offset=None, in_=hm_rows[i],
                                            in_offset=bass.IndirectOffsetOnAxis(idx_col[:, b:b + 1], 0),
                                            bounds_check=SEQ - 1, oob_is_err=False).then_inc(s["gathered"], 16)

                regular = [dict(col=col_ready, gathered=gathered[b]) for b in range(2)]
                with pool.Fori(0, E // 2) as it:
                    for b in range(2):
                        n = pool.snap(it * 2 + (E * i + b + 1))
                        gather(n, b, it * 2 + b, regular[b],
                               lambda: pool.wait_ge(t_done, it * 2 + max(0, E * i + b - 1)))
                        more = pool.value_load(extra_i[0:1, bass.ds(it * 2 + b, 1)], min_val=0, max_val=NG - 1)
                        with pool.If(more > 0):
                            with pool.Fori(0, more) as g:
                                before = pool.snap(count)
                                pool.reg_add(count, count, 1)
                                m = pool.snap(count)
                                gather(m, 2, it * 2 + g * E + (E + b), ex,
                                       lambda: pool.wait_ge(ex["t"], before))
                for b in range(2):
                    pool.wait_ge(y_stored[b], 32 * (E // 2) * (i + 1))
                pool.wait_ge(ex["stored"], pool.snap(count) * 32)
                pool.sem_inc(col_seen, 1)
                for T in range(NT):
                    if T >= 2:
                        pool.wait_ge(y_used, NT * i + T - 1)
                    for k in range(2):
                        pool.indirect_dma_start(out=ycomb[T % 2][:, k, :], out_offset=None, in_=y_rows,
                                                in_offset=bass.IndirectOffsetOnAxis(dest_i[:, 8 + 4 * k + T:9 + 4 * k + T], 0))\
                            .then_inc(y_back[T % 2], 16)

            moe(0)
            moe(1)


def kernel(x, c, positions, ada_w, ada_b, ln_g, ln_b, w_in_e, gdn_conv_w, gdn_a_log, gdn_dt_bias, gdn_norm_w,
           sc_conv_w, w_out_e, w_in_o, q_a_norm, w_q_b, kv_a_norm, w_kv_b, w_out_o, router_w, router_bias,
           w_gate, w_up, w_down):
    from concourse import bacc
    from concourse.bass_utils import run_bass_kernel_spmd

    def a(v):
        return np.ascontiguousarray(v)

    def taps(w, tiles):
        return a(w).reshape(w.shape[0], tiles, P).transpose(2, 1, 0).reshape(P, -1)

    def everywhere(v):
        return np.broadcast_to(a(v).reshape(1, -1), (P, a(v).size))

    inv = (np.float32(10000.0) ** (-np.arange(0, ROPE, 2, dtype=np.float32) / np.float32(ROPE))).astype(np.float32)
    ba = 3 * H * DK + H * DK
    small = np.concatenate([
        taps(a(gdn_conv_w)[0], 12), taps(a(sc_conv_w)[0], 4), a(gdn_norm_w)[0].reshape(P, 1),
        a(q_a_norm)[0].reshape(3, P).T, a(kv_a_norm)[0].reshape(2, P).T,
        everywhere(np.tile(a(gdn_a_log)[0], NT)), everywhere(np.tile(a(gdn_dt_bias)[0], NT)),
        a(c).reshape(P, NJ), a(router_w).reshape(P, NJ * E), a(a(w_in_e)[0][:, ba:ba + 2 * H]).reshape(P, NJ * 2 * H),
        everywhere(router_bias), everywhere(inv)], axis=1)
    rows = np.concatenate([a(ada_b).reshape(24, 512),
                           np.concatenate([a(ln_g).reshape(4, 2, 512), a(ln_b).reshape(4, 2, 512)], axis=1).reshape(16, 512)])
    token = np.arange(SEQ, dtype=np.int32).reshape(NT, P).T
    ints = np.concatenate([a(positions).reshape(NT, P).T, token], axis=1)
    arrays = dict(x=a(x)[0], small=a(small), const=constants(), rows=a(rows), ints=a(ints), ada_w=a(ada_w),
                  w_in_e=a(w_in_e)[0], w_out_e=a(w_out_e)[0], w_in_o=a(w_in_o)[0], w_q_b=a(w_q_b)[0], w_kv_b=a(w_kv_b)[0],
                  w_out_o=a(w_out_o)[0], w_gate=a(w_gate), w_up=a(w_up), w_down=a(w_down))
    nc = bacc.Bacc("TRN2", target_bir_lowering=False, num_devices=1)
    args = {n: nc.dram_tensor(f"in_{n}", v.shape, mybir.dt.from_np(v.dtype), kind="ExternalInput").ap() for n, v in arrays.items()}
    out = nc.dram_tensor("out_0", [SEQ, D_MODEL], F32, kind="ExternalOutput").ap()
    decoder_kernel(nc, out=out, **args)
    r = run_bass_kernel_spmd(nc, [{f"in_{n}": v for n, v in arrays.items()}], core_ids=[0])
    return r.results[0]["out_0"].reshape(1, SEQ, D_MODEL)
```

```python
from contextlib import ExitStack

import numpy as np

import concourse.bass as bass
from concourse import mybir

F32 = mybir.dt.float32
I32 = mybir.dt.int32
U32 = mybir.dt.uint32
ALU = mybir.AluOpType
ACT = mybir.ActivationFunctionType
AX = mybir.AxisListType

P = 128
D_MODEL, SEQ, DEPTH = 1024, 512, 2
NT = SEQ // P
NJ = D_MODEL // P
DN_ALPHA = (2.0 * DEPTH) ** 0.25
H, DK, CH = 4, 128, 64
QKV_W, SC_W = 3 * H * DK, 512
MH, NOPE, ROPE, VD = 8, 128, 64, 128
Q_LORA, KV_LORA = 384, 256
E, GROUPS, EPG, FE = 32, 4, 8, 512
BLK = 64
NG = SEQ // BLK
MAX_EXTRA = 2 * SEQ // (BLK + 1)
RING, SLOT = 6, 4096
LN_EPS, NORM_EPS = 1e-5, 1e-6
BIG = 1e30
MAGIC = 1.5 * 2 ** 23
TWO_PI = 6.283185307179586
PI_A = 6.28125
PI_B = 0.0019350051879882812
PI_C = TWO_PI - PI_A - PI_B

C_ID, C_ONE, C_CUM, C_BLK, C_DEC, C_DCT, C_LEV = 0, 128, 256, 384, 512, 640, 768
C_ATT, C_SUT, C_IO, C_EPS6, C_EPS5, C_HPI = 1536, 1664, 1792, 1856, 1857, 1858
C_SEL, C_SUM, N_CONST = 1859, 1883, 1915
CHUNKS, ROWS, DIRECT = 6, 40, 4
PARKED = 2 * DEPTH * CHUNKS - DIRECT
S_CW, S_SW, S_NW, S_QN, S_KN = 0, 48, 60, 61, 64
S_AL, S_DT, S_C, S_RW, S_BA, S_RB, S_INV = 66, 82, 98, 106, 362, 426, 458
N_SMALL = 490
LEVELS = (2, 4, 8, 16, 32)


def constants():
    c = np.zeros((P, N_CONST), np.float32)
    p, f = np.arange(P)[:, None], np.arange(P)[None, :]
    same = p // CH == f // CH
    c[:, C_ID:C_ID + P] = p == f
    c[:, C_ONE:C_ONE + P] = 1
    c[:, C_CUM:C_CUM + P] = same & (p <= f)
    c[:, C_BLK:C_BLK + P] = same
    c[:, C_DEC:C_DEC + P] = np.where(same & (f < p), 0, BIG)
    c[:, C_DCT:C_DCT + P] = np.where(same & (f >= p), 0, -BIG)
    c[:, C_LEV:C_LEV + P] = (p // 2 == f // 2) & (p % 2 == 1) & (f % 2 == 0)
    for n, s in enumerate(LEVELS):
        a = C_LEV + (n + 1) * P
        c[:, a:a + P] = (p // (2 * s) == f // (2 * s)) & (p % (2 * s) < s) & (f % (2 * s) >= s)
    c[:, C_ATT:C_ATT + P] = np.where(f <= p, 0, -BIG)
    c[:, C_SUT:C_SUT + P] = p < f
    c[:, C_IO:C_IO + BLK] = np.arange(BLK)
    c[:, C_EPS6], c[:, C_EPS5], c[:, C_HPI] = NORM_EPS, LN_EPS, np.pi / 2
    chunk = np.arange(DIRECT + PARKED)[None, :]
    c[:, C_SUM:C_SUM + E] = p % 32 == np.arange(E)[None, :]
    c[:, C_SEL:C_SUM] = (p == chunk) | ((p - ROWS) // 4 == chunk - DIRECT) & (p >= ROWS)
    return c


FILLING = [item for c, kind in enumerate("zchb") for item in [(kind, t) for t in range(4)] + [("park", 3 + c)]] \
    + [("park", n) for n in range(7, PARKED)]
UNITS = [(q, half) for q, (kind, _) in enumerate(FILLING) for half in range(1 if kind == "park" else 2)]
BEFORE, SETUP = 6, 4


def units_at(pair, point):
    first = BEFORE + (SETUP + 19) * pair + (0 if point == 0 else SETUP - 1 + point)
    last = len(UNITS) if (pair, point) == (1, 19) else first + (SETUP if point == 0 else 1)
    return range(min(first, len(UNITS)), min(last, len(UNITS)))


def ring_plan():
    base, at = {}, 0
    mixer0 = [part for c in range(7) for part in ((f"in_e{c}", 1), (f"park{c}", 1))]
    for name, n in (("ada", DIRECT), *mixer0, *((f"park{n}", 1) for n in range(7, PARKED)), ("out_e", 2), ("moe0", 3 * E),
                    ("in_o", 2), ("qb", 2), ("kvb", 1), ("out_o", 2), ("moe1", 3 * E)):
        base[name] = at
        at += n
    return base


def decoder_kernel(nc, x, small, const, rows, ints, ada_w, w_in_e, w_out_e, w_in_o, w_q_b, w_kv_b,
                   w_out_o, w_gate, w_up, w_down, out):
    base = ring_plan()
    ctx = ExitStack()
    with ctx:
        def sb(name, shape, dt=F32):
            return ctx.enter_context(nc.sbuf_tensor(name, shape, dt))

        def sem(name):
            return ctx.enter_context(nc.semaphore(name))

        hm_rows = [nc.dram_tensor(f"hm_rows{i}", [SEQ, D_MODEL], F32, kind="Internal").ap() for i in range(DEPTH)]
        y_rows = nc.dram_tensor("y_rows", [(E + MAX_EXTRA) * BLK, D_MODEL], F32, kind="Internal").ap()

        ring = sb("ring", [P, RING, SLOT])
        xres = sb("xres", [P, NT, D_MODEL])
        cst = sb("cst", [P, N_CONST])
        sml = sb("sml", [P, N_SMALL])
        rws = sb("rws", [P, 512])
        part = sb("part", [P, 512])
        intc = sb("intc", [P, 8], I32)
        area_a = sb("area_a", [P, 4096])
        area_b = sb("area_b", [P, 4096])
        area_c = sb("area_c", [P, 6144])
        area_d = sb("area_d", [P, 2048])
        modss = sb("modss", [P, 2048])
        area_e = sb("area_e", [P, 1024])
        gate_a = sb("gate_a", [P, 1024])
        tiny = sb("tiny", [P, 208])
        cond = sb("cond", [P, NJ])
        statb = sb("statb", [P, 32])

        def cc(a, n=P):
            return cst[:, a:a + n]
        ident, ones = cc(C_ID), cc(C_ONE)

        hmT = area_a[:, :].rearrange("p (j t) -> p j t", j=NJ)
        gate_b = area_c[:, 5120:6144]
        hm = [area_e[:, :], area_d[:, 1024:2048]]
        ln_rows = [(area_c[:, 2048:3072], area_c[:, 3072:4096]), (area_d[:, 0:1024], area_c[:, 4096:5120])]
        lnr = [area_c[:, 0:1024], area_c[:, 1024:2048]]
        gates = [gate_a[:, :], gate_b]

        def part_buffer(n):
            return int(n >= 7 and n % 2 == 1)
        parts = [part[:, :], area_b[:, 1536:2048]]
        kept_before = [[sum(part_buffer(m) == b for m in range(n)) for n in range(PARKED + 1)] for b in range(2)]

        qkv = area_c[:, :].rearrange("p (m t) -> p m t", m=12)
        zs = area_d[:, :].rearrange("p (h t) -> p h t", h=H)
        scc = [area_b[:, 1024:1536], area_b[:, 1536:2048]]
        yb_T = area_b[:, 2048:4096].rearrange("p (h t) -> p h t", h=4)
        sq = [area_e[:, 0:512], area_e[:, 512:1024]]
        rq = [modss[:, 0:512], modss[:, 512:1024]]
        pool16 = [xres[:, n // 2, 512 * (n % 2):512 * (n % 2) + 512] for n in range(8)] \
            + [a[:, 512 * n:512 * n + 512] for a in (area_b, gate_a) for n in range(2)] + [modss[:, 512 * n:512 * n + 512] for n in range(4)]

        def hv(ap):
            return ap.rearrange("p (h t) -> p h t", h=H)
        d_L, d_IT, d_X, d_Y, d_MT, d_KB, d_KD, d_U = [[hv(pool16[2 * n + k]) for k in range(2)] for n in range(8)]
        state = hv(area_e[:, 0:512])
        os_ = hv(area_e[:, 512:1024])
        g_t, g_sp, g_g, g_gc, g_eg, g_kd, g_beg, g_beta, g_ea, g_ms = [tiny[:, 16 * n:16 * n + 16] for n in range(10)]
        g_last = tiny[:, 160:192].rearrange("p (t h c) -> p t h c", t=NT, h=H)

        qaT = area_c[:, 0:1536].rearrange("p (j t) -> p j t", j=3)
        kaT = area_c[:, 1536:2560].rearrange("p (j t) -> p j t", j=2)
        krT = area_c[:, 2560:3072]
        qrT = area_c[:, 3072:5120].rearrange("p (j t) -> p j t", j=4)
        qr = [area_c[:, 5120:5632], area_b[:, 1024:1536]]
        krd = [area_c[:, 5632:5760], area_b[:, 1536:1664]]
        ms_o = area_c[:, 5760:5792]
        lat = [area_d[:, 0:640], area_b[:, 0:640]]
        cs_t = area_d[:, 1024:1152].rearrange("p (t f) -> p t f", t=NT)
        sn_t = area_d[:, 1152:1280].rearrange("p (t f) -> p t f", t=NT)
        rt1 = area_d[:, 1280:1536].rearrange("p (h f) -> p h f", h=MH)
        rt2 = area_d[:, 1536:1792].rearrange("p (h f) -> p h f", h=MH)
        ang = area_d[:, 1792:1920]
        kround = area_d[:, 1920:2048]
        v_tok = area_a[:, :].rearrange("p (t n) -> p t n", t=NT)
        qnT = [modss[:, 0:512], modss[:, 512:1024]]
        knT = [modss[:, 1024:1536], modss[:, 1536:2048]]
        prob = [area_e[:, 0:512], area_e[:, 512:1024]]
        probT = [area_d[:, 0:512], area_d[:, 512:1024]]
        oT = area_b[:, :].rearrange("p (h t) -> p h t", h=MH)
        att_m, att_n, att_s, att_r = [tiny[:, 32 * n:32 * n + 32] for n in range(4)]

        xg = [area_b[:, 1024 * n:1024 * n + 1024] for n in range(3)]
        xT = [area_c[:, 512 * n:512 * n + 512].rearrange("p (j s) -> p j s", j=NJ) for n in range(3)]
        sg = [area_c[:, 1536 + 256 * n:1792 + 256 * n] for n in range(3)]
        hb = [area_c[:, 2304 + 256 * n:2560 + 256 * n] for n in range(3)]
        hts = [area_c[:, 3072 + 256 * n:3328 + 256 * n] for n in range(3)]
        yb = [area_b[:, 3072:3584], area_b[:, 3584:4096], area_a[:, 0:512]]
        idx_all = sb("idx_all", [BLK, NG * E], I32)
        idx_col = sb("idx_col", [BLK, 4], I32)
        dest_i = sb("dest_i", [P, 8], I32)
        extra_i = sb("extra_i", [1, E], I32)
        mi = sb("mi", [P, 32], U32)
        r_sc, r_bi, r_m8, r_tmp, r_o1, r_o2 = [area_d[:, 128 * n:128 * n + 128] for n in range(6)]
        r_oh, r_rk = [area_d[:, 768 + 128 * n:896 + 128 * n] for n in range(2)]
        r_cum = area_d[:, 1024:1024 + (NT + 1) * E]
        r_gs, r_gm, r_ig, r_lm = [area_d[:, 1408 + 32 * n:1440 + 32 * n] for n in range(4)]
        r_sm = area_d[:, 1536:1664]
        wsel = tiny[:, 192:200]
        ycomb = [a.rearrange("p (k d) -> p k d", k=2) for a in (area_c[:, 0:2048], area_c[:, 2048:4096],
                                                                area_b[:, 0:2048], area_b[:, 2048:4096])]
        place = [area_a[:, 2048 + 256 * k:2304 + 256 * k].rearrange("p (t s) -> p t s", t=NT) for k in range(2)]
        table = [area_a[:, 1024 * k:1024 * k + 1024].rearrange("p (t g e) -> p t g e", t=NT, g=NG) for k in range(2)]

        bank = [ctx.enter_context(nc.psum_tensor(f"bank{n}", [P, 512], F32)) for n in range(8)]

        ring_full = [sem(f"ring_full{n}") for n in range(RING)]
        slot_free = sem("slot_free")
        small_in, inputs_in, x_in = sem("small_in"), sem("inputs_in"), sem("x_in")
        act_step, dve_step, pool_step = sem("act_step"), sem("dve_step"), sem("pool_step")
        park_done, part_ready = sem("park_done"), sem("part_ready")
        part_kept = [sem(f"part_kept{n}") for n in range(2)]
        cond_ready, ada_done, mod_ready = sem("cond_ready"), sem("ada_done"), sem("mod_ready")
        hm_ready, tr_done, hmT_ready = sem("hm_ready"), sem("tr_done"), sem("hmT_ready")
        ln_rows_in, y_taken = sem("ln_rows_in"), sem("y_taken")
        ln_done, last_done = sem("ln_done"), sem("last_done")
        var_ready, std_ready, rstd_ready, z_ready = sem("var_ready"), sem("std_ready"), sem("rstd_ready"), sem("z_ready")
        y_weighted, gain_done = sem("y_weighted"), sem("gain_done")
        quarters_done, quarters_ready = sem("quarters_done"), sem("quarters_ready")
        proj_done, conv_done, silu_done, sq_ready = sem("proj_done"), sem("conv_done"), sem("silu_done"), sem("sq_ready")
        ssq_done, rt_ready, qk_ready, fill_done = sem("ssq_done"), sem("rt_ready"), sem("qk_ready"), sem("fill_done")
        fill_taken = [sem(f"fill_taken{n}") for n in range(2)]
        ba_done, t_ready, sp_ready, g_ready, gc_done = sem("ba_done"), sem("t_ready"), sem("sp_ready"), sem("g_ready"), sem("gc_done")
        gcs_ready, ge_ready, gates_ready = sem("gcs_ready"), sem("ge_ready"), sem("gates_ready")
        cg_ready, gcb_done, kq_done, eb_ready, dd_ready, dx_ready = (sem("cg_ready"), sem("gcb_done"), sem("kq_done"),
                                                                    sem("eb_ready"), sem("dd_ready"), sem("dx_ready"))
        x0_ready, xt_done, y0_ready = sem("x0_ready"), sem("xt_done"), sem("y0_ready")
        mt_done, mt_ready, y2_done, lv_ready = sem("mt_done"), sem("mt_ready"), sem("y2_done"), sem("lv_ready")
        kt_done, kd_ready, vt_done, vb_ready = sem("kt_done"), sem("kd_ready"), sem("vt_done"), sem("vb_ready")
        uw_done, u_ready, wt_ready = sem("uw_done"), sem("u_ready"), sem("wt_ready")
        vn_done, vn_ready, sd_done, s_ready, o_done = sem("vn_done"), sem("vn_ready"), sem("sd_done"), sem("s_ready"), sem("o_done")
        orms_ready, orec_ready, os_ready, ot_done, ya_ready = (sem("orms_ready"), sem("orec_ready"), sem("os_ready"),
                                                              sem("ot_done"), sem("ya_ready"))
        y_done = sem("y_done")
        lat_done, lms_ready, lrs_ready, lat_ready, kr_ready = sem("lat_done"), sem("lms_ready"), sem("lrs_ready"), sem("lat_ready"), sem("kr_ready")
        latT_done, latT_ready, krT_ready = sem("latT_done"), sem("latT_ready"), sem("krT_ready")
        ang_ready, sin_ready = sem("ang_ready"), sem("sin_ready")
        qr_done, qr_ready, qrt_done, qrT_ready, v_done, v_ready = (sem("qr_done"), sem("qr_ready"), sem("qrt_done"),
                                                                   sem("qrT_ready"), sem("v_done"), sem("v_ready"))
        qkn_done, qkn_ready, s_done, nm_ready, p_ready, pn_ready = (sem("qkn_done"), sem("qkn_ready"), sem("s_done"),
                                                                    sem("nm_ready"), sem("p_ready"), sem("pn_ready"))
        pt_done, pt_ready, av_done, oT_ready = sem("pt_done"), sem("pt_ready"), sem("av_done"), sem("oT_ready")
        hm_stored = [sem(f"hm_stored{n}") for n in range(2)]
        rows_seen, col_seen = sem("rows_seen"), sem("col_seen")
        logit_done, score_ready, oh_ready, rank_done, dest_ready = (sem("logit_done"), sem("score_ready"), sem("oh_ready"),
                                                                    sem("rank_done"), sem("dest_ready"))
        table_ready, table_done = sem("table_ready"), sem("table_done")
        col_ready, t_done, xT_ready = sem("col_ready"), sem("t_done"), sem("xT_ready")
        gathered, y_stored = ([sem(f"{n}{b}") for b in range(2)] for n in ("gathered", "y_stored"))
        y_back = [sem(f"y_back{T}") for T in range(NT)]
        gate_done, up_done, silu_ready, h_ready = sem("gate_done"), sem("up_done"), sem("silu_ready"), sem("h_ready")
        ht_done, hts_ready, down_done, y_ready = sem("ht_done"), sem("hts_ready"), sem("down_done"), sem("y_ready")
        x_names = ("col", "gathered", "t", "xT", "gate", "up", "silu", "h", "ht", "hts", "down", "y", "stored")
        ex = {n: sem(f"extra_{n}") for n in x_names}
        out_stored, y_cleared = sem("out_stored"), sem("y_cleared")

        block = ctx.enter_context(nc.Block())

        class InOrder:

            def __init__(self, eng, done):
                self.eng, self.done, self.n = eng, done, 0

            def __call__(self, ins):
                self.n += 1
                ins.then_inc(self.done, 1)
                self.eng.wait_ge(self.done, self.n)

        def signal(eng, ins, done, value):
            ins.then_inc(done, 1)
            eng.wait_ge(done, value)

        def tcols(T):
            return slice(P * T, P * T + P)

        @block.sync
        def _(sp):
            def load(n, src, dst_cols=SLOT, shape=None):
                former = n - RING
                layer = [i for i in range(DEPTH) if 0 <= former - base[f"moe{i}"] < 3 * E]
                if layer:
                    e, m = divmod(former - base[f"moe{layer[0]}"], 3)
                    sp.wait_ge((gate_done, up_done, down_done)[m], E * layer[0] + e + 1)
                elif former >= 0:
                    sp.wait_ge(slot_free, former + 1 - 3 * E * sum(former >= base[f"moe{i}"] for i in range(DEPTH)))
                dst = ring[:, n % RING, 0:dst_cols]
                if shape:
                    dst = dst.rearrange("p (j n) -> p j n", j=shape)
                sp.dma_start(dst, src).then_inc(ring_full[n % RING], 16)

            def columns(w, a, b, j, order="(p j) n -> p j n"):
                return w[:, a:b].rearrange(order, j=j)

            def ada(name, k):
                (i, s), c = divmod(k // CHUNKS, 2), k % CHUNKS
                load(base[name], columns(ada_w[i, s], 512 * c, 512 * c + 512, NJ), shape=NJ)

            def experts(name, i):
                n0 = base[name]

                def matrix(m, e):
                    src = (w_gate, w_up, w_down)[m][i, bass.ds(e, 1)]
                    return src.rearrange("o (p j) n -> p (o j) n" if m < 2 else "o (j p) n -> p (o j) n", p=P)
                for k in range(6):
                    load(n0 + k, matrix(k % 3, k // 3), shape=(NJ if k % 3 < 2 else 4))
                with sp.Fori(1, E // 2) as it:
                    for b in range(2):
                        e = sp.snap(it * 2 + b)
                        done = sp.snap(it * 2 + (E * i + b - 1))
                        for m, used in enumerate((gate_done, up_done, down_done)):
                            slot = (n0 + 3 * b + m) % RING
                            sp.wait_ge(used, done)
                            sp.dma_start(ring[:, slot, :].rearrange("p (j n) -> p j n", j=(NJ if m < 2 else 4)),
                                         matrix(m, e)).then_inc(ring_full[slot], 16)

            sp.dma_start(sml[:, :], small).then_inc(small_in, 16)
            for c in range(DIRECT):
                load(base["ada"] + c, columns(ada_w[0, 0], 512 * c, 512 * c + 512, NJ), shape=NJ)
                if c == 0:
                    sp.dma_start(cst[:, :], const).then_inc(inputs_in, 16)
                    sp.dma_start(rws[0:ROWS, :], rows).then_inc(inputs_in, 16)
                    sp.dma_start(intc[:, :], ints).then_inc(inputs_in, 16)
            sp.dma_start(xres[:, :, :], x.rearrange("(t p) d -> p t d", p=P)).then_inc(x_in, 16)
            for c, a in enumerate((0, 512, 1024, 1536, 2568, 3080, 2056)):
                load(base[f"in_e{c}"], columns(w_in_e, a, a + 512, NJ), shape=NJ)
                ada(f"park{c}", DIRECT + c)
            for n in range(7, PARKED):
                ada(f"park{n}", DIRECT + n)
            for c in range(2):
                load(base["out_e"] + c, columns(w_out_e, 512 * c, 512 * c + 512, NJ, "(j p) n -> p j n"), shape=NJ)
            experts("moe0", 0)
            for T in range(NT):
                sp.wait_ge(y_back[T], 32)
            load(base["in_o"], columns(w_in_o, 0, 384, NJ), 384 * NJ, NJ)
            load(base["in_o"] + 1, columns(w_in_o, 384, 704, NJ), 320 * NJ, NJ)
            for c in range(2):
                load(base["qb"] + c, columns(w_q_b, 768 * c, 768 * c + 768, 3, "(j p) n -> p j n"), 768 * 3, 3)
            load(base["kvb"], columns(w_kv_b, 0, 2048, 2, "(j p) n -> p j n"), shape=2)
            for c in range(2):
                load(base["out_o"] + c, columns(w_out_o, 512 * c, 512 * c + 512, NJ, "(j p) n -> p j n"), shape=NJ)
            experts("moe1", 1)

        @block.tensor
        def _(pe):
            def full(n):
                pe.wait_ge(ring_full[n % RING], 16 * (n // RING + 1))
                return ring[:, n % RING, :]

            def bcast_row(dst, r, start=True):
                return pe.matmul(dst, cst[0:ROWS, C_ID + r:C_ID + r + 1].to_broadcast([ROWS, P]), rws[0:ROWS, :],
                                 start=start, stop=True)

            def direct(c):
                w = full(base["ada"] + c)
                if c >= 2:
                    pe.wait_ge(mod_ready, c - 1)
                ps = bank[c % 2][:, :]
                for j in range(NJ):
                    mm = pe.matmul(ps, cond[:, j:j + 1].to_broadcast([P, P]), w[:, 512 * j:512 * j + 512],
                                   start=(j == 0), stop=False)
                mm.then_inc(slot_free, 1)
                pe.wait_ge(inputs_in, 48)
                bcast_row(ps, c, start=False).then_inc(ada_done, 1)

            def park(n, ps):
                w = full(base[f"park{n}"])
                for half in range(2):
                    for g in range(4):
                        j = 4 * half + g
                        mm = pe.matmul(ps[32 * g:32 * g + 32, :], cond[:, j:j + 1].to_broadcast([P, 32]), w[:, 512 * j:512 * j + 512],
                                       start=(half == 0), stop=(half == 1))
                mm.then_inc(park_done, 1)
                pe.wait_ge(park_done, n + 1)
                pe.sem_inc(slot_free, 1)

            def fill(units):
                for u in units:
                    q, half = UNITS[u]
                    kind, t = FILLING[q]
                    if half == 0 and q >= 2:
                        pe.wait_ge(fill_taken[q % 2], q // 2)
                    if kind == "park":
                        park(t, bank[6 + q % 2])
                        pe.sem_inc(fill_done, 1)
                        continue
                    c = 3 + "zchb".index(kind)
                    w = full(base[f"in_e{c}"])
                    for j in range(4 * half, 4 * half + 4):
                        mm = pe.matmul(bank[6 + q % 2][:, :], w[:, 512 * j + P * t:512 * j + P * t + P], hmT[:, j, :],
                                       start=(j == 0), stop=(j == NJ - 1))
                    if half == 1:
                        mm.then_inc(fill_done, 1)
                        if t == 3:
                            pe.wait_ge(fill_done, q + 1)
                            pe.sem_inc(slot_free, 1)

            def modulations(chunks):
                for b in range(2):
                    pe.wait_ge(part_kept[b], 16 * kept_before[b][PARKED])
                for k in chunks:
                    pe.wait_ge(mod_ready, k - 1)
                    rows_n = ROWS + 4 * PARKED
                    pe.matmul(bank[k % 2][:, :], cst[0:rows_n, C_SEL + k:C_SEL + k + 1].to_broadcast([rows_n, P]), rws[0:rows_n, :],
                              start=True, stop=True).then_inc(ada_done, 1)

            def modulated(st):
                for T in range(NT):
                    k = NT * st + T
                    pe.wait_ge(hm_ready, k + 1)
                    if k:
                        pe.wait_ge(hmT_ready, 2 * k)
                    hv_ = hm[T % 2].rearrange("p (f j) -> p j f", j=NJ)
                    for j in range(NJ):
                        mm = pe.transpose(bank[2 + j // 4][:, P * (j % 4):P * (j % 4) + P], hv_[:, j, :], ident)
                        if j % 4 == 3:
                            mm.then_inc(tr_done, 1)

            def out_proj(name, tiles, st, ready):
                w = [full(base[name]), full(base[name] + 1)]
                ready()
                for T in range(NT):
                    if T >= 2:
                        pe.wait_ge(y_taken, NT * (st // 2) + T - 1)
                    for n in range(2):
                        for j in range(NJ):
                            mm = pe.matmul(bank[2 * (T % 2) + n][:, :], tiles[j][:, tcols(T)], w[n][:, 512 * j:512 * j + 512],
                                           start=(j == 0), stop=(j == NJ - 1))
                            if T == NT - 1 and j == NJ - 1 and n == 0:
                                mm.then_inc(slot_free, 1)
                    mm.then_inc(y_done, 1)
                pe.wait_ge(y_done, NT * (st // 2 + 1))
                pe.sem_inc(slot_free, 1)

            def narrow(n, a, step, dst, width, done):
                for half in range(2):
                    for g in range(4):
                        c = a + step * (4 * half + g)
                        mm = pe.matmul(bank[4][32 * g:32 * g + 32, :], sml[:, c:c + 32], hmT[:, 4 * half + g, :],
                                       start=(half == 0), stop=(half == 1))
                mm.then_inc(quarters_done, 1)
                pe.wait_ge(quarters_ready, n)
                for T in range(NT):
                    mm = pe.matmul(dst[:, width * T:width * T + width], part[:, tcols(T)], cst[:, C_SUM:C_SUM + width], start=True, stop=True)
                mm.then_inc(done, 1)

            pe.wait_ge(cond_ready, 1)
            for c in range(DIRECT):
                direct(c)
            modulated(0)
            pe.wait_ge(hmT_ready, 2 * NT)
            narrow(1, S_BA, 2 * H, bank[7], 2 * H, ba_done)

            def ssq(m):
                pe.wait_ge(sq_ready, m + 1)
                if m >= 2:
                    pe.wait_ge(rt_ready, m - 1)
                pe.matmul(bank[4 + m % 2][:, :], ones, sq[m % 2], start=True, stop=True).then_inc(ssq_done, 1)

            for m in range(12):
                if m % 4 == 0:
                    w = full(base[f"in_e{m // 4}"])
                if m >= 4:
                    pe.wait_ge(conv_done, m - 3)
                for j in range(NJ):
                    a = 512 * j + P * (m % 4)
                    mm = pe.matmul(bank[m % 4][:, :], w[:, a:a + P], hmT[:, j, :], start=(j == 0), stop=(j == NJ - 1))
                mm.then_inc(proj_done, 1)
                if m % 4 == 3:
                    pe.wait_ge(proj_done, m + 1)
                    pe.sem_inc(slot_free, 1)
                    if m > 3:
                        pe.wait_ge(part_ready, m // 4)
                    park(m // 4, bank[6])
                if 2 <= m < 10:
                    ssq(m - 2)
                if m == 10:
                    pe.wait_ge(g_ready, 1)
                    pe.matmul(bank[7][:, 0:16], cc(C_CUM), g_g, start=True, stop=True)
                    pe.matmul(bank[7][:, 16:32], cc(C_BLK), g_g, start=True, stop=True).then_inc(gc_done, 1)
            pe.wait_ge(part_ready, 3)
            pe.wait_ge(gcs_ready, 1)
            fill(range(BEFORE))
            pe.wait_ge(gates_ready, 1)
            pe.wait_ge(conv_done, 12)
            pe.wait_ge(rt_ready, 8)
            for pair in range(2):
                tiles = [(2 * pair + k, k, [bank[3 * k + n] for n in range(3)]) for k in range(2)]
                for T, k, B in tiles:
                    if pair:
                        pe.wait_ge(ya_ready, T - 1)
                    pe.wait_ge(cg_ready, T + 1)
                    pe.matmul(B[0][:, :], ones, d_MT[k].rearrange("p h t -> p (h t)"), start=True, stop=True).then_inc(gcb_done, 1)
                    pe.wait_ge(qk_ready, 8)
                    for h in range(H):
                        pe.matmul(B[1][:, P * h:P * h + P], qkv[:, 4 + h, tcols(T)], qkv[:, 4 + h, tcols(T)], start=True, stop=True)
                    for h in range(H):
                        mm = pe.matmul(B[2][:, P * h:P * h + P], qkv[:, 4 + h, tcols(T)], qkv[:, h, tcols(T)], start=True, stop=True)
                    mm.then_inc(kq_done, 1)
                fill(units_at(pair, 0))
                for T, k, B in tiles:
                    pe.wait_ge(x0_ready, T + 1)
                    for h in range(H):
                        mm = pe.transpose(B[0][:, P * h:P * h + P], d_X[k][:, h, :], ident)
                    mm.then_inc(xt_done, 1)
                for lv in range(5):
                    for T, k, B in tiles:
                        n = (pair * 5 + lv) * 2 + k
                        pe.wait_ge(y0_ready, T + 1)
                        if lv:
                            pe.wait_ge(lv_ready, n - 1)
                        for h in range(H):
                            mm = pe.matmul(B[1][:, P * h:P * h + P], d_L[k][:, h, :], d_Y[k][:, h, :], start=True, stop=True)
                        mm.then_inc(mt_done, 1)
                    fill(units_at(pair, 1 + 2 * lv))
                    if lv == 1:
                        for T, k, B in tiles:
                            for h in range(H):
                                mm = pe.transpose(B[0][:, P * h:P * h + P], qkv[:, 4 + h, tcols(T)], ident)
                            mm.then_inc(kt_done, 1)
                    if lv == 3:
                        for T, k, B in tiles:
                            pe.wait_ge(kd_ready, T + 1)
                            for h in range(H):
                                mm = pe.transpose(B[0][:, P * h:P * h + P], qkv[:, 8 + h, tcols(T)], ident)
                            mm.then_inc(vt_done, 1)
                    for T, k, B in tiles:
                        n = (pair * 5 + lv) * 2 + k
                        pe.wait_ge(mt_ready, n + 1)
                        for h in range(H):
                            mm = pe.matmul(B[2][:, P * h:P * h + P], d_X[k][:, h, :], d_MT[k][:, h, :], start=True, stop=True)
                        for h in range(H):
                            mm = pe.matmul(B[1][:, P * h:P * h + P], d_MT[k][:, h, :], d_X[k][:, h, :], start=True, stop=True)
                        mm.then_inc(y2_done, 1)
                    fill(units_at(pair, 2 + 2 * lv))
                for T, k, B in tiles:
                    pe.wait_ge(lv_ready, pair * 10 + 9 + k)
                    pe.wait_ge(vb_ready, T + 1)
                    for h in range(H):
                        pe.matmul(B[1][:, P * h:P * h + P], d_Y[k][:, h, :], qkv[:, 8 + h, tcols(T)], start=True, stop=True)
                    for h in range(H):
                        mm = pe.matmul(B[2][:, P * h:P * h + P], d_KB[k][:, h, :], d_Y[k][:, h, :], start=True, stop=True)
                    mm.then_inc(uw_done, 1)
                fill(units_at(pair, 11))
                def output_turn(T, B):
                    pe.wait_ge(os_ready, T + 1)
                    for h in range(H):
                        mm = pe.transpose(B[0][:, P * h:P * h + P], os_[:, h, :], ident)
                    mm.then_inc(ot_done, 1)
                pe.wait_ge(vb_ready, 2 * pair + 2)
                for T, k, B in tiles:
                    pe.wait_ge(wt_ready, T + 1)
                    pe.wait_ge(u_ready, T + 1)
                    for c in range(2):
                        n, r = 2 * T + c, slice(CH * c, CH * c + CH)
                        tc = slice(P * T + CH * c, P * T + CH * c + CH)
                        pe.wait_ge(s_ready, n + 1)
                        for h in range(H):
                            mm = pe.matmul(B[0][r, P * h:P * h + P], qkv[:, 4 + h, tc], state[:, h, :], start=True, stop=True)
                        mm.then_inc(vn_done, 1)
                        if (k, c) == (1, 1):
                            output_turn(T - 1, tiles[0][2])
                        fill(units_at(pair, 12 + 4 * k + 2 * c))
                        pe.wait_ge(vn_ready, n + 1)
                        for h in range(H):
                            mm = pe.matmul(B[1][:, P * h:P * h + P], d_KD[k][r, h, :], d_U[k][r, h, :], start=True, stop=True)
                        mm.then_inc(sd_done, 1)
                        for h in range(H):
                            pe.matmul(B[2][r, P * h:P * h + P], qkv[:, h, tc], state[:, h, :], start=True, stop=False)
                            mm = pe.matmul(B[2][r, P * h:P * h + P], d_IT[k][r, h, r], d_U[k][r, h, :], start=False, stop=True)
                        mm.then_inc(o_done, 1)
                        fill(units_at(pair, 13 + 4 * k + 2 * c))
                output_turn(tiles[1][0], tiles[1][2])

            pe.wait_ge(ya_ready, NT)
            modulations(range(DIRECT, 2 * CHUNKS))
            pe.wait_ge(mod_ready, 2 * CHUNKS)
            out_proj("out_e", [zs[:, j, :] for j in range(4)] + [yb_T[:, j, :] for j in range(4)], 0, lambda: None)
            pe.wait_ge(y_taken, NT)

            count = pe.alloc_register("pe_extra")
            pe.reg_mov(count, 0)

            def moe(i, name):
                st = 2 * i + 1
                modulated(st)
                pe.wait_ge(hmT_ready, 2 * NT * (st + 1))
                narrow(i + 2, S_RW, E, bank[4], E, logit_done)
                if i == 0:
                    modulations(range(2 * CHUNKS, 3 * CHUNKS))
                pe.wait_ge(oh_ready, i + 1)
                pe.matmul(bank[5][:, 0:NT * E], cc(C_SUT), r_oh, start=True, stop=False)
                pe.matmul(bank[5][:, 0:NT * E], ones, r_cum[:, 0:NT * E], start=False, stop=True)
                pe.matmul(bank[5][:, NT * E:(NT + 1) * E], ones, r_cum[:, NT * E:(NT + 1) * E], start=True, stop=True).then_inc(rank_done, 1)
                for n in range(2 * NT):
                    k, T = divmod(n, NT)
                    if T == 0:
                        pe.wait_ge(table_ready, 2 * i + k + 1)
                    mm = pe.matmul(bank[4][0:BLK, 0:NG * E], place[k][:, T, :], table[k][:, T].rearrange("p g e -> p (g e)"),
                                   start=(n == 0), stop=(n == 2 * NT - 1))
                mm.then_inc(table_done, 1)
                pe.wait_ge(dest_ready, i + 1)

                def turn_rows(b, bt, s, js):
                    for j in js:
                        mm = pe.transpose(bt[:, BLK * j:BLK * j + BLK],
                                          xg[b][0:BLK, :].rearrange("p (f j) -> p j f", j=NJ)[:, j, :], ident[0:BLK, 0:BLK])
                    if js[-1] == NJ - 1:
                        mm.then_inc(s["t"], 1)

                def rows_arrive(s, arrivals):
                    pe.wait_ge(s["gathered"], arrivals * 16)
                    pe.sem_inc(rows_seen, 1)

                def block_pass(n, b, banks, s, arrived, ahead=(None, None)):
                    bg, bu, bh, bd = banks
                    pe.wait_ge(s["xT"], n)
                    for k, dst, done in ((0, bg, s["gate"]), (1, bu, s["up"])):
                        w = arrived(k)
                        for j in range(NJ):
                            for hf in range(2):
                                mm = pe.matmul(dst[BLK * hf:BLK * hf + BLK, 0:256], xT[b][:, j, :],
                                               w[:, 512 * j + 256 * hf:512 * j + 256 * hf + 256],
                                               start=(j == 0), stop=(j == NJ - 1))
                        mm.then_inc(done, 1)
                    if ahead[0]:
                        ahead[0]()
                    pe.wait_ge(s["h"], n)
                    for c in range(2):
                        mm = pe.transpose(bh[:, P * c:P * c + P], hb[b][:, P * c:P * c + P], ident)
                    mm.then_inc(s["ht"], 1)
                    if ahead[1]:
                        ahead[1]()
                    w = arrived(2)
                    pe.wait_ge(s["hts"], n)
                    for kt in range(4):
                        lhs = hts[b][:, P * (kt % 2) + BLK * (kt // 2):P * (kt % 2) + BLK * (kt // 2) + BLK]
                        for hf in range(2):
                            mm = pe.matmul(bd[BLK * hf:BLK * hf + BLK, :], lhs, w[:, 1024 * kt + 512 * hf:1024 * kt + 512 * hf + 512],
                                           start=(kt == 0), stop=(kt == 3))
                    mm.then_inc(s["down"], 1)

                regular = [dict(gathered=gathered[b], t=t_done, xT=xT_ready, gate=gate_done, up=up_done, h=h_ready,
                                ht=ht_done, hts=hts_ready, down=down_done) for b in range(2)]
                n0 = base[name]

                def expert(it, b, last):
                    n = pe.snap(it * 2 + (E * i + b + 1))

                    def arrived(k):
                        q = n0 + 3 * b + k
                        pe.wait_ge(ring_full[q % RING], it * 16 + 16 * (q // RING + 1))
                        return ring[:, q % RING, :]
                    more = pe.value_load(extra_i[0:1, bass.ds(it * 2 + b, 1)], min_val=0, max_val=NG - 1)
                    with pe.If(more > 0):
                        with pe.Fori(0, more) as _g:
                            pe.reg_add(count, count, 1)
                            m = pe.snap(count)
                            rows_arrive(ex, m)
                            turn_rows(2, bank[1], ex, range(NJ))
                            block_pass(m, 2, (bank[2], bank[3], bank[5], bank[0]), ex, arrived)

                    def next_rows():
                        rows_arrive(regular[1 - b], it + (E // 2 * i + 1 + b))
                        turn_rows(1 - b, bank[4], regular[1 - b], range(NJ // 2))
                    block_pass(n, b, (bank[2], bank[3], bank[5], bank[6 + b]), regular[b], arrived,
                               (None, None) if last else (next_rows, lambda: turn_rows(1 - b, bank[4], regular[1 - b], range(NJ // 2, NJ))))

                if i == 0:
                    pe.wait_ge(mod_ready, 18)
                rows_arrive(regular[0], E // 2 * i + 1)
                turn_rows(0, bank[4], regular[0], range(NJ))
                with pe.Fori(0, E // 2 - 1) as it:
                    for b in range(2):
                        expert(it, b, False)
                last_pair = pe.alloc_register(f"last_pair{i}")
                pe.reg_mov(last_pair, E // 2 - 1)
                for b in range(2):
                    expert(pe.snap(last_pair), b, b == 1)
                pe.wait_ge(y_ready, E * (i + 1))

            moe(0, "moe0")

            modulated(2)
            pe.wait_ge(hmT_ready, 2 * NT * 3)
            wa, wb = full(base["in_o"]), full(base["in_o"] + 1)
            for T in range(NT + 1):
                if T < NT:
                    if T >= 2:
                        pe.wait_ge(lat_ready, T - 1)
                        pe.wait_ge(kr_ready, T - 1)
                    for w, width, ps in ((wa, 384, bank[2 * (T % 2)]), (wb, 320, bank[2 * (T % 2) + 1])):
                        for j in range(NJ):
                            mm = pe.matmul(ps[:, 0:width], hmT[:, j, tcols(T)], w[:, width * j:width * j + width],
                                           start=(j == 0), stop=(j == NJ - 1))
                    mm.then_inc(lat_done, 1)
                if T == NT:
                    pe.wait_ge(lat_done, NT)
                    pe.sem_inc(slot_free, 2)
                if T:
                    pe.wait_ge(lat_ready, T)
                    pe.wait_ge(kr_ready, T)
                    if T >= 2:
                        pe.wait_ge(latT_ready, T - 1)
                        pe.wait_ge(krT_ready, T - 1)
                    for j in range(5):
                        pe.transpose(bank[4 + j // 3][:, P * (j % 3):P * (j % 3) + P], lat[(T - 1) % 2][:, P * j:P * j + P], ident)
                    pe.transpose(bank[5][:, 2 * P:3 * P], krd[(T - 1) % 2], ident).then_inc(latT_done, 1)
            pe.wait_ge(latT_ready, NT)
            pe.wait_ge(krT_ready, NT)
            wq = [full(base["qb"] + n)[:, 0:768 * 3].rearrange("p (j h n) -> p j h n", j=3, h=4) for n in range(2)]
            wkv = full(base["kvb"]).rearrange("p (j h n) -> p j h n", j=2, h=MH)
            for T in range(NT + 1):
                if T < NT:
                    if T >= 2:
                        pe.wait_ge(qr_ready, T - 1)
                    for n in range(2):
                        for j in range(3):
                            mm = pe.matmul(bank[(6, 2)[T % 2]][:, 256 * n:256 * n + 256], qaT[:, j, tcols(T)],
                                           wq[n][:, j, :, NOPE:NOPE + ROPE], start=(j == 0), stop=(j == 2))
                    mm.then_inc(qr_done, 1)
                    for n in range(2):
                        if T:
                            pe.wait_ge(v_ready, 2 * T + n - 1)
                        for j in range(2):
                            mm = pe.matmul(bank[n][:, :], kaT[:, j, tcols(T)], wkv[:, j, 4 * n:4 * n + 4, NOPE:NOPE + VD],
                                           start=(j == 0), stop=(j == 1))
                        mm.then_inc(v_done, 1)
                if T:
                    pe.wait_ge(qr_ready, T)
                    if T >= 2:
                        pe.wait_ge(qrT_ready, T - 1)
                    for j in range(4):
                        mm = pe.transpose(bank[7][:, P * j:P * j + P], qr[(T - 1) % 2][:, P * j:P * j + P], ident)
                    mm.then_inc(qrt_done, 1)
            pe.wait_ge(v_ready, 2 * NT)
            pe.wait_ge(qrT_ready, NT)

            def head_proj(h):
                if h:
                    pe.wait_ge(qkn_ready, h)
                for j in range(3):
                    pe.matmul(bank[0][:, :], wq[h // 4][:, j, h % 4, 0:NOPE], qaT[:, j, :], start=(j == 0), stop=(j == 2))
                for j in range(2):
                    mm = pe.matmul(bank[1][:, :], wkv[:, j, h, 0:NOPE], kaT[:, j, :], start=(j == 0), stop=(j == 1))
                mm.then_inc(qkn_done, 1)

            def scores(u):
                h, i = divmod(u, NT)
                nk = P * (i + 1)
                pe.wait_ge(qkn_ready, h + 1)
                if u >= 2:
                    pe.wait_ge(p_ready, u - 1)
                ps = bank[2 + u % 2]
                half = slice(ROPE * (h % 2), ROPE * (h % 2) + ROPE)
                pe.matmul(ps[:, 0:nk], qnT[h % 2][:, tcols(i)], knT[h % 2][:, 0:nk], start=True, stop=False)
                pe.matmul(ps[:, 0:nk], qrT[half, h // 2, tcols(i)], krT[half, 0:nk], start=False, stop=False)
                pe.matmul(ps[:, nk - P:nk], ident, cc(C_ATT), start=False, stop=True).then_inc(s_done, 1)

            def turn(u):
                h, i = divmod(u, NT)
                pe.wait_ge(pn_ready, u + 1)
                if u >= 2:
                    pe.wait_ge(pt_ready, u - 1)
                for k in range(i + 1):
                    mm = pe.transpose(bank[4 + u % 2][:, P * k:P * k + P], prob[u % 2][:, P * k:P * k + P], ident)
                mm.then_inc(pt_done, 1)

            def values(u):
                h, i = divmod(u, NT)
                pe.wait_ge(pt_ready, u + 1)
                if i == 0 and h >= 2:
                    pe.wait_ge(oT_ready, h - 1)
                for k in range(i + 1):
                    mm = pe.matmul(bank[6 + h % 2][:, tcols(i)], v_tok[:, k, VD * h:VD * h + VD], probT[u % 2][:, P * k:P * k + P],
                                   start=(k == 0), stop=(k == i))
                mm.then_inc(av_done, 1)

            head_proj(0)
            for u in range(MH * NT + 3):
                if u < MH * NT:
                    scores(u)
                    if u % NT == 0 and u // NT + 1 < MH:
                        head_proj(u // NT + 1)
                if 2 <= u < MH * NT + 2:
                    turn(u - 2)
                if u >= 3:
                    values(u - 3)
            pe.wait_ge(av_done, MH * NT)
            pe.sem_inc(slot_free, 3)
            pe.wait_ge(oT_ready, MH)
            modulations(range(3 * CHUNKS, 4 * CHUNKS))
            pe.wait_ge(mod_ready, 4 * CHUNKS)
            out_proj("out_o", [oT[:, j, :] for j in range(MH)], 2, lambda: None)
            pe.wait_ge(y_taken, 2 * NT)
            moe(1, "moe1")

        @block.scalar
        def _(act):
            step = InOrder(act, act_step)
            act.wait_ge(small_in, 16)
            act.activation(cond[:, :], sml[:, S_C:S_C + NJ], ACT.Silu).then_inc(cond_ready, 1)

            def modulations(chunks):
                for k in chunks:
                    st, c = divmod(k, CHUNKS)
                    act.wait_ge(ada_done, k + 1)
                    if c == 0 and st:
                        act.wait_ge(hm_ready, NT * st)
                    dst = modss[:, 512 * c:512 * c + 512] if c < 4 else gates[st % 2][:, 512 * (c - 4):512 * (c - 4) + 512]
                    act.activation(dst, bank[k % 2][:, :], ACT.Copy, bias=(0.0 if c < 2 else 1.0)).then_inc(mod_ready, 1)

            def park(n, ps, taken=None):
                act.wait_ge(park_done, n + 1)
                b = part_buffer(n)
                if kept_before[b][n]:
                    act.wait_ge(part_kept[b], 16 * kept_before[b][n])
                signal(act, act.activation(parts[b], ps[:, :], ACT.Copy), part_ready, n + 1)
                if taken:
                    act.sem_inc(taken, 1)

            def modulated(st):
                for k in range(2 * NT * st, 2 * NT * (st + 1)):
                    T, half = divmod(k - 2 * NT * st, 2)
                    act.wait_ge(tr_done, k + 1)
                    act.activation(hmT[:, 4 * half:4 * half + 4, tcols(T)],
                                   bank[2 + half][:, :].rearrange("p (j t) -> p j t", j=4), ACT.Copy).then_inc(hmT_ready, 1)

            def load_ln_rows(st):
                for n in range(2):
                    r = 2 * DEPTH * CHUNKS + 4 * st + 2 * n
                    act.dma_start(ln_rows[st % 2][n], rows[r:r + 2, :].rearrange("(o r) n -> o (r n)", o=1).to_broadcast([P, D_MODEL]))\
                        .then_inc(ln_rows_in, 16)

            def layer_norm(st):
                def spread(T):
                    k, c = NT * st + T, 16 * (T % 2)
                    act.wait_ge(var_ready, k + 1)
                    act.activation(statb[:, c + 14:c + 15], statb[:, c + 13:c + 14], ACT.Sqrt, bias=cst[:, C_EPS5:C_EPS5 + 1])\
                        .then_inc(std_ready, 1)
                    act.wait_ge(rstd_ready, k + 1)
                    y = lnr[T % 2] if st % 2 == 0 else ycomb[T][:, 0, :]
                    act.activation(y, y, ACT.Identity, scale=statb[:, c + 15:c + 16], bias=statb[:, c + 14:c + 15]).then_inc(z_ready, 1)

                for T in range(NT + 1):
                    if st % 2 and T < NT:
                        act.wait_ge(y_back[T], 32 * (st // 2 + 1))
                        act.activation(ycomb[T][:, 0, :], ycomb[T][:, 0, :], ACT.Copy, scale=wsel[:, T:T + 1]).then_inc(y_weighted, 1)
                    if T:
                        spread(T - 1)

            def quarters(n):
                act.wait_ge(quarters_done, n)
                act.activation(part[:, :], bank[4][:, :], ACT.Copy).then_inc(quarters_ready, 1)

            modulations(range(DIRECT))
            modulated(0)
            quarters(1)
            act.wait_ge(t_ready, 1)
            step(act.activation(g_sp, g_t, ACT.Abs))
            step(act.activation(g_sp, g_sp, ACT.Exp, scale=-1.0))
            step(act.activation(g_sp, g_sp, ACT.Ln, bias=1.0))
            step(act.activation(g_ea, sml[:, S_AL:S_AL + 16], ACT.Exp))
            act.activation(g_beta.rearrange("p (t h) -> p t h", t=NT),
                           bank[7][:, 0:32].rearrange("p (t x) -> p t x", t=NT)[:, :, 0:H], ACT.Exp, scale=-1.0).then_inc(sp_ready, 1)

            def root(m):
                act.wait_ge(ssq_done, m + 1)
                if m >= 2:
                    act.wait_ge(qk_ready, m - 1)
                act.activation(rq[m % 2], bank[4 + m % 2][:, :], ACT.Sqrt, bias=cst[:, C_EPS6:C_EPS6 + 1]).then_inc(rt_ready, 1)

            for m in range(12):
                act.wait_ge(conv_done, m + 1)
                signal(act, act.activation(qkv[:, m, :], qkv[:, m, :], ACT.Silu), silu_done, m + 1)
                if m < 8:
                    if m >= 2:
                        act.wait_ge(ssq_done, m - 1)
                    act.activation(sq[m % 2], qkv[:, m, :], ACT.Square).then_inc(sq_ready, 1)
                if 1 <= m <= 8:
                    root(m - 1)
                if m % 4 == 3:
                    park(m // 4, bank[6])
            act.wait_ge(gcs_ready, 1)
            step(act.activation(g_eg, g_gc, ACT.Exp))
            act.activation(g_kd, g_kd, ACT.Exp).then_inc(ge_ready, 1)

            def take(units):
                for u in units:
                    q, half = UNITS[u]
                    kind, t = FILLING[q]
                    if kind == "park":
                        act.wait_ge(fill_done, q + 1)
                        park(t, bank[6 + q % 2], fill_taken[q % 2])
                    elif half == 1 and kind in "zc":
                        act.wait_ge(fill_done, q + 1)
                        dst = zs[:, t, :] if kind == "z" else yb_T[:, t, :]
                        act.activation(dst, bank[6 + q % 2][:, :], ACT.Silu if kind == "z" else ACT.Copy).then_inc(fill_taken[q % 2], 1)
            take(range(BEFORE))
            act.wait_ge(qk_ready, 8)
            for pair in range(2):
                tiles = [(2 * pair + k, k, [bank[3 * k + n] for n in range(3)]) for k in range(2)]
                for T, k, B in tiles:
                    act.wait_ge(gcb_done, T + 1)
                    act.wait_ge(gates_ready, 1)
                    act.activation(d_U[k], B[0][:, :].rearrange("p (h t) -> p h t", h=H), ACT.Exp).then_inc(eb_ready, 1)
                    act.wait_ge(dd_ready, T + 1)
                    step(act.activation(d_KB[k], d_KB[k], ACT.Exp))
                    act.activation(d_MT[k], d_MT[k], ACT.Exp, scale=-1.0).then_inc(dx_ready, 1)
                take(units_at(pair, 0))
                for T, k, B in tiles:
                    act.wait_ge(xt_done, T + 1)
                    act.activation(d_Y[k], B[0][:, :].rearrange("p (h t) -> p h t", h=H), ACT.Copy).then_inc(y0_ready, 1)
                for point in (1, 2, 3):
                    take(units_at(pair, point))
                for T, k, B in tiles:
                    act.wait_ge(kt_done, T + 1)
                    for h in range(H):
                        q = NT * T + h
                        act.activation(d_KB[k][:, h, :], B[0][:, P * h:P * h + P], ACT.Copy, scale=g_beg[:, q:q + 1])
                        ins = act.activation(d_KD[k][:, h, :], B[0][:, P * h:P * h + P], ACT.Copy, scale=g_kd[:, q:q + 1])
                    ins.then_inc(kd_ready, 1)
                for point in (4, 5, 6, 7):
                    take(units_at(pair, point))
                for T, k, B in tiles:
                    act.wait_ge(vt_done, T + 1)
                    for h in range(H):
                        q = NT * T + h
                        ins = act.activation(qkv[:, 8 + h, tcols(T)], B[0][:, P * h:P * h + P], ACT.Copy, scale=g_beta[:, q:q + 1])
                    ins.then_inc(vb_ready, 1)
                for point in (8, 9, 10):
                    take(units_at(pair, point))
                for T, k, B in tiles:
                    act.wait_ge(uw_done, T + 1)
                    act.activation(d_U[k], B[1][:, :].rearrange("p (h t) -> p h t", h=H), ACT.Copy).then_inc(u_ready, 1)
                take(units_at(pair, 11))
                for T, k, B in tiles:
                    for point in range(4):
                        take(units_at(pair, 12 + 4 * k + point))
                    act.wait_ge(o_done, 2 * T + 2)
                    if T:
                        act.wait_ge(ot_done, T)
                    for h in range(H):
                        step(act.activation(os_[:, h, :], B[2][:, P * h:P * h + P], ACT.Square, accum_out=g_ms[:, NT * T + h:NT * T + h + 1]))
                    act.activation(g_ms[:, NT * T:NT * T + H], g_ms[:, NT * T:NT * T + H], ACT.Sqrt, scale=1.0 / DK,
                                   bias=cst[:, C_EPS6:C_EPS6 + 1]).then_inc(orms_ready, 1)
                    act.wait_ge(orec_ready, T + 1)
                    for h in range(H):
                        ins = act.activation(os_[:, h, :], B[2][:, P * h:P * h + P], ACT.Copy, scale=g_ms[:, NT * T + h:NT * T + h + 1])
                    ins.then_inc(os_ready, 1)
            act.wait_ge(ya_ready, NT)
            act.dma_start(xres[:, :, :], x.rearrange("(t p) d -> p t d", p=P)).then_inc(x_in, 16)
            modulations(range(DIRECT, 2 * CHUNKS))
            load_ln_rows(0)
            layer_norm(0)

            count = act.alloc_register("act_extra")
            act.reg_mov(count, 0)
            row = act.alloc_register("extra_row")

            def moe(i):
                st = 2 * i + 1
                for T in range(NT):
                    act.wait_ge(hm_ready, NT * st + T + 1)
                    act.dma_start(hm_rows[i][P * T:P * T + P, :], hm[T % 2]).then_inc(hm_stored[T % 2], 16)
                    for half in range(2):
                        act.wait_ge(tr_done, 2 * (NT * st + T) + half + 1)
                        act.activation(hmT[:, 4 * half:4 * half + 4, tcols(T)],
                                       bank[2 + half][:, :].rearrange("p (j t) -> p j t", j=4), ACT.Copy).then_inc(hmT_ready, 1)
                quarters(i + 2)
                act.wait_ge(logit_done, i + 1)
                act.activation(r_sc, bank[4][:, 0:P], ACT.Sigmoid).then_inc(score_ready, 1)
                if i == 0:
                    modulations(range(2 * CHUNKS, 3 * CHUNKS))
                act.wait_ge(dest_ready, i + 1)

                def rows_copy(b, bt, s, n):
                    act.wait_ge(s["t"], n + s["t_first"])
                    act.activation(xT[b], bt[:, :].rearrange("p (j s) -> p j s", j=NJ), ACT.Copy).then_inc(s["xT"], 1)

                def silu(b, s, n):
                    act.wait_ge(s["gate"], n)
                    act.activation(sg[b], bank[2][:, 0:256], ACT.Silu).then_inc(s["silu"], 1)

                def store(b, s, n, row):
                    act.wait_ge(s["y"], n)
                    for hf in range(2):
                        act.dma_start(y_rows[bass.ds(row, BLK), 512 * hf:512 * hf + 512],
                                      yb[b][BLK * hf:BLK * hf + BLK, :]).then_inc(s["stored"], 16)

                act.reg_mov(row, BLK * E)
                regular = [dict(t=t_done, t_first=2, xT=xT_ready, gate=gate_done, silu=silu_ready, y=y_ready, stored=y_stored[b])
                           for b in range(2)]
                extra = dict(ex, t_first=1)

                def expert(it, b, last):
                    n = act.snap(it * 2 + (E * i + b + 1))
                    more = act.value_load(extra_i[0:1, bass.ds(it * 2 + b, 1)], min_val=0, max_val=NG - 1)
                    with act.If(more > 0):
                        with act.Fori(0, more) as _g:
                            act.reg_add(count, count, 1)
                            m = act.snap(count)
                            r = act.snap(row)
                            act.reg_add(row, row, BLK)
                            rows_copy(2, bank[1], extra, m)
                            silu(2, extra, m)
                            store(2, extra, m, r)
                    silu(b, regular[b], n)
                    if not last:
                        rows_copy(1 - b, bank[4], regular[1 - b], it * 2 + (E * i + b + 2))
                    store(b, regular[b], n, it * (2 * BLK) + BLK * b)

                rows_copy(0, bank[4], regular[0], E * i + 1)
                with act.Fori(0, E // 2 - 1) as it:
                    for b in range(2):
                        expert(it, b, False)
                load_ln_rows(st)
                last_pair = act.alloc_register(f"act_last_pair{i}")
                act.reg_mov(last_pair, E // 2 - 1)
                for b in range(2):
                    expert(act.snap(last_pair), b, b == 1)
                layer_norm(st)

            moe(0)
            modulated(2)

            act.wait_ge(ang_ready, 1)
            step(act.activation(sn_t, ang.rearrange("p (t f) -> p t f", t=NT), ACT.Sin))
            step(act.activation(kround, ang, ACT.Abs))
            act.activation(cs_t, kround.rearrange("p (t f) -> p t f", t=NT), ACT.Sin, scale=-1.0,
                           bias=cst[:, C_HPI:C_HPI + 1]).then_inc(sin_ready, 1)
            for T in range(NT + 1):
                if T < NT:
                    bq, bk, rows_T = bank[2 * (T % 2)], bank[2 * (T % 2) + 1], lat[T % 2]
                    act.wait_ge(lat_done, T + 1)
                    if T >= 2:
                        act.wait_ge(latT_done, T - 1)
                    step(act.activation(rows_T[:, 0:384], bq[:, 0:384], ACT.Square, accum_out=ms_o[:, 8 * T:8 * T + 1]))
                    step(act.activation(rows_T[:, 384:640], bk[:, 0:256], ACT.Square, accum_out=ms_o[:, 8 * T + 1:8 * T + 2]))
                    step(act.activation(ms_o[:, 8 * T + 2:8 * T + 3], ms_o[:, 8 * T:8 * T + 1], ACT.Sqrt, scale=1.0 / Q_LORA,
                                        bias=cst[:, C_EPS6:C_EPS6 + 1]))
                    act.activation(ms_o[:, 8 * T + 3:8 * T + 4], ms_o[:, 8 * T + 1:8 * T + 2], ACT.Sqrt, scale=1.0 / KV_LORA,
                                   bias=cst[:, C_EPS6:C_EPS6 + 1]).then_inc(lms_ready, 1)
                    act.wait_ge(lrs_ready, T + 1)
                    act.activation(rows_T[:, 0:384], bq[:, 0:384], ACT.Copy, scale=ms_o[:, 8 * T + 4:8 * T + 5])
                    act.activation(rows_T[:, 384:640], bk[:, 0:256], ACT.Copy, scale=ms_o[:, 8 * T + 5:8 * T + 6]).then_inc(lat_ready, 1)
                if T:
                    act.wait_ge(latT_done, T)
                    for j in range(5):
                        dst = qaT[:, j, tcols(T - 1)] if j < 3 else kaT[:, j - 3, tcols(T - 1)]
                        w = S_QN + j if j < 3 else S_KN + j - 3
                        ins = act.activation(dst, bank[4 + j // 3][:, P * (j % 3):P * (j % 3) + P], ACT.Copy, scale=sml[:, w:w + 1])
                    ins.then_inc(latT_ready, 1)
            for T in range(NT + 1):
                if T < NT:
                    for n in range(2):
                        act.wait_ge(v_done, 2 * T + n + 1)
                        act.activation(v_tok[:, T, 512 * n:512 * n + 512], bank[n][:, :], ACT.Copy).then_inc(v_ready, 1)
                if T:
                    act.wait_ge(qrt_done, T)
                    act.activation(qrT[:, :, tcols(T - 1)], bank[7][:, :].rearrange("p (j t) -> p j t", j=4), ACT.Copy).then_inc(qrT_ready, 1)

            scale = float(NOPE + ROPE) ** -0.5

            def head_copy(h):
                act.wait_ge(qkn_done, h + 1)
                if h >= 2:
                    act.wait_ge(s_done, NT * (h - 1))
                step(act.activation(qnT[h % 2], bank[0][:, :], ACT.Copy))
                act.activation(knT[h % 2], bank[1][:, :], ACT.Copy).then_inc(qkn_ready, 1)

            head_copy(0)
            for u in range(MH * NT + 3):
                if u < MH * NT:
                    h, i = divmod(u, NT)
                    nk = P * (i + 1)
                    act.wait_ge(nm_ready, u + 1)
                    if u >= 2:
                        act.wait_ge(pt_done, u - 1)
                    act.activation(prob[u % 2][:, 0:nk], bank[2 + u % 2][:, 0:nk], ACT.Exp, bias=att_n[:, u:u + 1], scale=scale,
                                   accum_out=att_s[:, u:u + 1]).then_inc(p_ready, 1)
                    if i == 0 and h + 1 < MH:
                        head_copy(h + 1)
                if 2 <= u < MH * NT + 2:
                    v = u - 2
                    nk = P * (v % NT + 1)
                    act.wait_ge(pt_done, v + 1)
                    if v >= 2:
                        act.wait_ge(av_done, v - 1)
                    act.activation(probT[v % 2][:, 0:nk], bank[4 + v % 2][:, 0:nk], ACT.Copy).then_inc(pt_ready, 1)
                if u >= 3 and (u - 3) % NT == NT - 1:
                    h = (u - 3) // NT
                    act.wait_ge(av_done, NT * (h + 1))
                    act.activation(oT[:, h, :], bank[6 + h % 2][:, :], ACT.Copy).then_inc(oT_ready, 1)
            modulations(range(3 * CHUNKS, 4 * CHUNKS))
            load_ln_rows(2)
            layer_norm(2)
            moe(1)
            for T in range(NT):
                act.wait_ge(*((ln_done, 3 * (NT - 1) + T + 1) if T < NT - 1 else (last_done, 2 * DEPTH)))
                act.dma_start(out[P * T:P * T + P, :], xres[:, T, :]).then_inc(out_stored, 16)
            act.wait_ge(out_stored, 16 * NT)

        @block.vector
        def _(dve):
            step = InOrder(dve, dve_step)

            def modulate(st, T):
                k = NT * st + T
                if st:
                    if T < NT - 1:
                        dve.wait_ge(ln_done, (NT - 1) * (st - 1) + T + 1)
                    dve.wait_ge(mod_ready, CHUNKS * st + 4)
                if T >= 2:
                    dve.wait_ge(tr_done, 2 * (k - 1))
                    if st % 2:
                        dve.wait_ge(hm_stored[T % 2], 16 * (NT // 2 * (st // 2) + T // 2))
                step(dve.tensor_tensor(hm[T % 2], xres[:, T, :], modss[:, 1024:2048], ALU.mult))
                signal(dve, dve.tensor_tensor(hm[T % 2], hm[T % 2], modss[:, 0:1024], ALU.add), hm_ready, k + 1)

            def combined(st, T, y, halves, taken):
                k, c = NT * st + T, 16 * (T % 2)
                dve.wait_ge(mod_ready, CHUNKS * (st + 1))
                for n in range(2):
                    ins = dve.tensor_tensor(y[:, 512 * n:512 * n + 512], halves[n], gates[st % 2][:, 512 * n:512 * n + 512], ALU.mult)
                    if n == 0:
                        step(ins)
                taken(ins)
                step(dve.scalar_tensor_tensor(out=y, in0=xres[:, T, :], scalar=DN_ALPHA, in1=y, op0=ALU.mult, op1=ALU.add))
                for n in range(2):
                    step(dve.bn_stats(statb[:, c + 6 * n:c + 6 * n + 6], y[:, 512 * n:512 * n + 512]))
                signal(dve, dve.bn_aggr(statb[:, c + 12:c + 14], statb[:, c:c + 12]), var_ready, k + 1)

            def normalizer(st, T):
                k, c = NT * st + T, 16 * (T % 2)
                dve.wait_ge(std_ready, k + 1)
                step(dve.reciprocal(statb[:, c + 15:c + 16], statb[:, c + 14:c + 15]))
                signal(dve, dve.scalar_tensor_tensor(out=statb[:, c + 14:c + 15], in0=statb[:, c + 12:c + 13], scalar=-1.0,
                                                     in1=statb[:, c + 15:c + 16], op0=ALU.mult, op1=ALU.mult), rstd_ready, k + 1)

            def last_tile(st):
                g, b = ln_rows[st % 2]
                y = lnr[(NT - 1) % 2] if st % 2 == 0 else ycomb[NT - 1][:, 0, :]
                dve.wait_ge(ln_rows_in, 32 * (st + 1))
                dve.wait_ge(z_ready, NT * (st + 1))
                step(dve.tensor_tensor(y, y, g, ALU.mult))
                signal(dve, dve.tensor_tensor(xres[:, NT - 1, :], y, b, ALU.add), last_done, st + 1)

            def norm_stage(st, combine):
                for T in range(NT + 2):
                    if T < NT:
                        combine(T)
                    if 1 <= T <= NT:
                        normalizer(st, T - 1)
                    if T == NT:
                        last_tile(st)
                    if T >= 2 and st < 2 * DEPTH - 1:
                        modulate(st + 1, T - 2)

            dve.wait_ge(x_in, 16)
            dve.wait_ge(mod_ready, 4)
            for T in range(NT):
                modulate(0, T)

            dve.wait_ge(inputs_in, 48)
            dve.wait_ge(ba_done, 1)
            t3 = g_t.rearrange("p (t h) -> p t h", t=NT)
            signal(dve, dve.tensor_tensor(t3, bank[7][:, 0:32].rearrange("p (t x) -> p t x", t=NT)[:, :, H:2 * H],
                                          sml[:, S_DT:S_DT + 16].rearrange("p (t h) -> p t h", t=NT), ALU.add), t_ready, 1)
            dve.wait_ge(sp_ready, 1)
            step(dve.scalar_tensor_tensor(out=g_g, in0=g_t, scalar=0.0, in1=g_sp, op0=ALU.max, op1=ALU.add))
            signal(dve, dve.scalar_tensor_tensor(out=g_g, in0=g_g, scalar=-1.0, in1=g_ea, op0=ALU.mult, op1=ALU.mult), g_ready, 1)
            step(dve.tensor_scalar(g_beta, g_beta, 1.0, None, ALU.add))
            step(dve.reciprocal(g_beta, g_beta))

            def conv(ps, acc, w, taps):
                step(dve.tensor_scalar(acc, ps, sml[:, w + taps - 1:w + taps], None, ALU.mult))
                for i in range(1, taps):
                    ins = dve.scalar_tensor_tensor(out=acc[:, i:SEQ], in0=ps[:, 0:SEQ - i], scalar=sml[:, w + taps - 1 - i:w + taps - i],
                                                   in1=acc[:, i:SEQ], op0=ALU.mult, op1=ALU.add)
                    if i < taps - 1:
                        step(ins)
                return ins

            def normalize(m):
                dve.wait_ge(rt_ready, m + 1)
                step(dve.reciprocal(rq[m % 2], rq[m % 2]))
                dve.wait_ge(sq_ready, m + 1)
                signal(dve, dve.scalar_tensor_tensor(out=qkv[:, m, :], in0=qkv[:, m, :], scalar=(DK ** -0.5 if m < H else 1.0),
                                                     in1=rq[m % 2], op0=ALU.mult, op1=ALU.mult), qk_ready, m + 1)

            for m in range(12):
                dve.wait_ge(proj_done, m + 1)
                signal(dve, conv(bank[m % 4][:, :], qkv[:, m, :], S_CW + 4 * m, 4), conv_done, m + 1)
                if 2 <= m < 10:
                    normalize(m - 2)
            dve.wait_ge(gc_done, 1)
            step(dve.tensor_copy(g_gc, bank[7][:, 0:16]))
            signal(dve, dve.tensor_tensor(g_kd, bank[7][:, 16:32], g_gc, ALU.subtract), gcs_ready, 1)
            def take(units):
                for u in units:
                    q, half = UNITS[u]
                    kind, t = FILLING[q]
                    if half == 1 and kind in "hb":
                        dve.wait_ge(fill_done, q + 1)
                        dst = scc[t % 2] if kind == "h" else yb_T[:, t, :]
                        taken = fill_taken[q % 2]
                        if kind == "h" and t == 0:
                            dve.wait_ge(fill_taken[(q + 1) % 2], 4)
                        signal(dve, dve.tensor_tensor(dst, bank[6 + q % 2][:, :], yb_T[:, t, :], ALU.mult), taken, q // 2 + 1)
                        if kind == "h":
                            step(conv(scc[t % 2], yb_T[:, t, :], S_SW + 3 * t, 3))
            dve.wait_ge(ge_ready, 1)
            signal(dve, dve.tensor_tensor(g_beg, g_beta, g_eg, ALU.mult), gates_ready, 1)
            signal(dve, dve.memset(state, 0.0), s_ready, 1)
            dve.wait_ge(y_cleared, 16)
            dve.wait_ge(hmT_ready, 2 * NT)

            def heads(ap):
                return ap.rearrange("p (h t) -> p h t", h=H)

            def per_head(gates_of, T):
                return gates_of[:, H * T:H * T + H].unsqueeze(2).to_broadcast([P, H, P])

            for pair in range(2):
                tiles = [(2 * pair + k, k, [bank[3 * k + n] for n in range(3)]) for k in range(2)]
                for T, k, B in tiles:
                    if pair:
                        dve.wait_ge(ot_done, NT // 2)
                    signal(dve, dve.tensor_tensor(d_MT[k], cc(C_CUM).unsqueeze(1).to_broadcast([P, H, P]), per_head(g_g, T), ALU.mult),
                           cg_ready, T + 1)
                for T, k, B in tiles:
                    dve.wait_ge(kq_done, T + 1)
                    dve.wait_ge(eb_ready, T + 1)
                    step(dve.tensor_tensor(d_X[k], heads(B[0][:, :]), per_head(g_gc, T), ALU.subtract))
                    step(dve.tensor_tensor(d_KB[k], d_X[k], cc(C_DCT).unsqueeze(1).to_broadcast([P, H, P]), ALU.add))
                    signal(dve, dve.tensor_tensor(d_MT[k], d_X[k], cc(C_DEC).unsqueeze(1).to_broadcast([P, H, P]), ALU.add), dd_ready, T + 1)
                for T, k, B in tiles:
                    dve.wait_ge(dx_ready, T + 1)
                    dve.wait_ge(eb_ready, T + 1)
                    for h in range(H):
                        step(dve.scalar_tensor_tensor(out=d_L[k][:, h, :], in0=B[1][:, P * h:P * h + P],
                                                      scalar=g_beta[:, NT * T + h:NT * T + h + 1], in1=d_MT[k][:, h, :],
                                                      op0=ALU.mult, op1=ALU.mult))
                    step(dve.tensor_tensor(d_IT[k], heads(B[2][:, :]), d_KB[k], ALU.mult))
                    step(dve.tensor_copy(g_last[:, T, :, :], d_U[k][:, :, CH - 1:P:CH]))
                    step(dve.tensor_tensor(qkv[:, 0:H, tcols(T)], qkv[:, 0:H, tcols(T)], d_U[k], ALU.mult))
                    step(dve.tensor_tensor(d_X[k], d_L[k], cc(C_LEV).unsqueeze(1).to_broadcast([P, H, P]), ALU.mult))
                    signal(dve, dve.scalar_tensor_tensor(out=d_X[k], in0=d_X[k], scalar=-1.0,
                                                         in1=ident.unsqueeze(1).to_broadcast([P, H, P]),
                                                         op0=ALU.mult, op1=ALU.add), x0_ready, T + 1)
                take(units_at(pair, 0))
                for lv in range(5):
                    for T, k, B in tiles:
                        n = (pair * 5 + lv) * 2 + k
                        dve.wait_ge(mt_done, n + 1)
                        signal(dve, dve.tensor_tensor(d_MT[k], heads(B[1][:, :]),
                                                      cc(C_LEV + P * (lv + 1)).unsqueeze(1).to_broadcast([P, H, P]), ALU.mult),
                               mt_ready, n + 1)
                    take(units_at(pair, 1 + 2 * lv))
                    for T, k, B in tiles:
                        n = (pair * 5 + lv) * 2 + k
                        dve.wait_ge(y2_done, n + 1)
                        step(dve.tensor_tensor(d_Y[k], d_Y[k], heads(B[2][:, :]), ALU.subtract))
                        signal(dve, dve.tensor_tensor(d_X[k], d_X[k], heads(B[1][:, :]), ALU.subtract), lv_ready, n + 1)
                    take(units_at(pair, 2 + 2 * lv))
                for T, k, B in tiles:
                    dve.wait_ge(uw_done, T + 1)
                    signal(dve, dve.tensor_copy(qkv[:, H:2 * H, tcols(T)], heads(B[2][:, :])), wt_ready, T + 1)
                take(units_at(pair, 11))
                def reciprocal_rms(T):
                    dve.wait_ge(orms_ready, T + 1)
                    signal(dve, dve.reciprocal(g_ms[:, NT * T:NT * T + H], g_ms[:, NT * T:NT * T + H]), orec_ready, T + 1)

                def gated(T, B):
                    dve.wait_ge(ot_done, T + 1)
                    signal(dve, dve.scalar_tensor_tensor(out=zs[:, :, tcols(T)], in0=heads(B[0][:, :]), scalar=sml[:, S_NW:S_NW + 1],
                                                         in1=zs[:, :, tcols(T)], op0=ALU.mult, op1=ALU.mult), ya_ready, T + 1)
                for T, k, B in tiles:
                    dve.wait_ge(u_ready, T + 1)
                    for c in range(2):
                        n, r = 2 * T + c, slice(CH * c, CH * c + CH)
                        dve.wait_ge(vn_done, n + 1)
                        signal(dve, dve.tensor_tensor(d_U[k][r, :, :], d_U[k][r, :, :], heads(B[0][r, :]), ALU.subtract), vn_ready, n + 1)
                        if (k, c) == (1, 0):
                            reciprocal_rms(T - 1)
                        take(units_at(pair, 12 + 4 * k + 2 * c))
                        dve.wait_ge(sd_done, n + 1)
                        dve.wait_ge(o_done, n + 1)
                        for h in range(H):
                            ins = dve.scalar_tensor_tensor(out=state[:, h, :], in0=state[:, h, :], scalar=g_last[:, T, h, c:c + 1],
                                                           in1=B[1][:, P * h:P * h + P], op0=ALU.mult, op1=ALU.add)
                            if h < H - 1:
                                step(ins)
                        signal(dve, ins, s_ready, n + 2)
                        take(units_at(pair, 13 + 4 * k + 2 * c))
                gated(tiles[0][0], tiles[0][2])
                reciprocal_rms(tiles[1][0])
                gated(tiles[1][0], tiles[1][2])

            def mixer_norm(st):
                def combine(T):
                    k = NT * (st // 2) + T
                    dve.wait_ge(y_done, k + 1)
                    if T >= 2:
                        dve.wait_ge(ln_done, (NT - 1) * st + T - 1)
                    combined(st, T, lnr[T % 2], [bank[2 * (T % 2) + n][:, :] for n in range(2)],
                             lambda ins: signal(dve, ins, y_taken, k + 1))
                if st == 0:
                    dve.wait_ge(x_in, 32)
                norm_stage(st, combine)

            count = dve.alloc_register("dve_extra")
            dve.reg_mov(count, 0)
            for begun in y_stored + [ex["stored"]]:
                dve.sem_inc(begun, 32)

            def moe(i):
                st = 2 * i + 1
                for b in range(2):
                    dve.wait_ge(hm_stored[b], 16 * NT // 2 * (i + 1))
                dve.wait_ge(hmT_ready, 2 * NT * (st + 1))

                def v4(ap, n=E):
                    return ap[:, 0:NT * n].rearrange("p (t e) -> p t e", t=NT)
                sc, bi, tmp, o1, o2, oh, rk = [v4(a) for a in (r_sc, r_bi, r_tmp, r_o1, r_o2, r_oh, r_rk)]
                iota = cc(C_IO, E).unsqueeze(1).to_broadcast([P, NT, E])
                step(dve.memset(r_gs, -BIG))
                dve.wait_ge(score_ready, i + 1)
                step(dve.tensor_tensor(bi, sc, sml[:, S_RB:S_RB + E].unsqueeze(1).to_broadcast([P, NT, E]), ALU.add))
                for q in range(NT * GROUPS):
                    step(dve.max(r_m8[:, 8 * q:8 * q + 8], r_bi[:, 8 * q:8 * q + 8]))
                m8 = r_m8.rearrange("p (t g k) -> p t g k", t=NT, g=GROUPS)
                gs = v4(r_gs, 8)
                step(dve.tensor_tensor(gs[:, :, 0:GROUPS], m8[:, :, :, 0], m8[:, :, :, 1], ALU.add))
                for T in range(NT):
                    c = slice(8 * T, 8 * T + 8)
                    step(dve.max(r_gm[:, c], r_gs[:, c]))
                    step(dve.max_index(mi[:, c], r_gm[:, c], r_gs[:, c]))
                grp = r_sm[:, 0:NT]
                step(dve.tensor_copy(grp, mi[:, 0:32:8]))
                go = r_sm[:, 16:32].rearrange("p (t g) -> p t g", t=NT)
                step(dve.tensor_tensor(go, cc(C_IO, GROUPS).unsqueeze(1).to_broadcast([P, NT, GROUPS]),
                                       grp.unsqueeze(2).to_broadcast([P, NT, GROUPS]), ALU.is_equal))
                step(dve.tensor_tensor(r_tmp.rearrange("p (q k) -> p q k", k=EPG), r_bi.rearrange("p (q k) -> p q k", k=EPG),
                                       r_sm[:, 16:32].unsqueeze(2).to_broadcast([P, NT * GROUPS, EPG]), ALU.mult))
                step(dve.tensor_reduce(v4(r_ig, 8), r_tmp.rearrange("p (t g k) -> p t k g", t=NT, g=GROUPS), AX.X, ALU.add))
                for T in range(NT):
                    c = slice(8 * T, 8 * T + 8)
                    step(dve.max(r_lm[:, c], r_ig[:, c]))
                    step(dve.max_index(mi[:, c], r_lm[:, c], r_ig[:, c]))
                for k, o in ((0, o1), (1, o2)):
                    ek = r_sm[:, 4 + 4 * k:8 + 4 * k]
                    step(dve.tensor_copy(ek, mi[:, k:32:8]))
                    step(dve.scalar_tensor_tensor(out=ek, in0=grp, scalar=float(EPG), in1=ek, op0=ALU.mult, op1=ALU.add))
                    step(dve.tensor_tensor(o, iota, ek.unsqueeze(2).to_broadcast([P, NT, E]), ALU.is_equal))
                step(dve.tensor_tensor(oh, o1, o2, ALU.add))
                step(dve.memset(r_cum[:, 0:E], 0.0))
                for T in range(NT):
                    ins = dve.tensor_tensor(r_cum[:, E * (T + 1):E * (T + 2)], r_cum[:, E * T:E * (T + 1)], oh[:, T, :], ALU.add)
                    if T < NT - 1:
                        step(ins)
                signal(dve, ins, oh_ready, i + 1)
                for k, o in ((0, o1), (1, o2)):
                    step(dve.tensor_tensor(tmp, sc, o, ALU.mult))
                    step(dve.tensor_reduce(wsel[:, 4 * k:4 * k + 4], tmp, AX.X, ALU.add))
                ws = r_sm[:, 12:16]
                step(dve.tensor_tensor(ws, wsel[:, 0:4], wsel[:, 4:8], ALU.add))
                step(dve.reciprocal(ws, ws))
                for k in range(2):
                    step(dve.tensor_tensor(wsel[:, 4 * k:4 * k + 4], wsel[:, 4 * k:4 * k + 4], ws, ALU.mult))
                dve.wait_ge(rank_done, i + 1)
                step(dve.tensor_copy(rk, bank[5][:, 0:P].rearrange("p (t e) -> p t e", t=NT)))

                def floor64(dst, src):
                    step(dve.tensor_scalar(dst, src, 1.0 / BLK, -(BLK - 1.0) / (2 * BLK), ALU.mult, ALU.add))
                    step(dve.tensor_scalar(dst, dst, MAGIC, None, ALU.add))
                    step(dve.tensor_scalar(dst, dst, MAGIC, None, ALU.subtract))

                def chosen(dst, values):
                    for k, o in ((0, o1), (1, o2)):
                        step(dve.tensor_tensor(tmp, values, o, ALU.mult))
                        step(dve.tensor_reduce(dst[:, 4 * k:4 * k + 4], tmp, AX.X, ALU.add))
                rank, block, rest, row = [r_sm[:, 32 + 8 * n:40 + 8 * n] for n in range(4)]
                chosen(rank, rk)
                floor64(block, rank)
                step(dve.scalar_tensor_tensor(out=rest, in0=block, scalar=-float(BLK), in1=rank, op0=ALU.mult, op1=ALU.add))
                for k, o in ((0, o1), (1, o2)):
                    b4 = block[:, 4 * k:4 * k + 4]
                    step(dve.tensor_tensor(place[k], cc(C_IO, BLK).unsqueeze(1).to_broadcast([P, NT, BLK]),
                                           rest[:, 4 * k:4 * k + 4].unsqueeze(2).to_broadcast([P, NT, BLK]), ALU.is_equal))
                    at = v4(r_gs, NG)
                    step(dve.tensor_tensor(at, cc(C_IO, NG).unsqueeze(1).to_broadcast([P, NT, NG]),
                                           b4.unsqueeze(2).to_broadcast([P, NT, NG]), ALU.is_equal))
                    step(dve.tensor_copy(r_sm[:, 16:20], intc[:, 4:8]))
                    step(dve.tensor_scalar(r_sm[:, 16:20], r_sm[:, 16:20], 1.0, None, ALU.add))
                    step(dve.tensor_tensor(at, at, r_sm[:, 16:20].unsqueeze(2).to_broadcast([P, NT, NG]), ALU.mult))
                    ins = dve.tensor_tensor(table[k], at.unsqueeze(3).to_broadcast([P, NT, NG, E]),
                                            o.unsqueeze(2).to_broadcast([P, NT, NG, E]), ALU.mult)
                    signal(dve, ins, table_ready, 2 * i + k + 1)
                cnt, bef = r_sm[:, 64:64 + E], r_sm[:, 96:96 + E]
                step(dve.tensor_scalar(cnt, bank[5][:, P:P + E], 1.0, -1.0, ALU.max, ALU.add))
                floor64(cnt, cnt)
                step(dve.tensor_copy(extra_i[:, :], cnt[0:1, :]))
                step(dve.tensor_tensor_scan(bef, ones[:, 0:E], cnt, 0.0, ALU.mult, ALU.add))
                step(dve.tensor_tensor(bef, bef, cnt, ALU.subtract))
                step(dve.tensor_tensor(bef, bef, cc(C_IO, E), ALU.subtract))
                step(dve.tensor_scalar(bef, bef, float(BLK), float(BLK * (E - 1)), ALU.mult, ALU.add))
                chosen(row, bef.unsqueeze(1).to_broadcast([P, NT, E]))
                step(dve.tensor_scalar(block, block, 1.0, None, ALU.min))
                step(dve.tensor_tensor(row, row, block, ALU.mult))
                step(dve.tensor_tensor(row, row, rank, ALU.add))
                step(dve.scalar_tensor_tensor(out=row, in0=r_sm[:, 4:12], scalar=float(BLK), in1=row, op0=ALU.mult, op1=ALU.add))
                step(dve.tensor_copy(dest_i[:, :], row))
                dve.wait_ge(table_done, i + 1)
                places = area_d[0:BLK, 1024:1280]
                step(dve.tensor_scalar(places, bank[4][0:BLK, 0:NG * E], 0.0, float(SEQ + 1), ALU.is_equal, ALU.mult))
                step(dve.scalar_tensor_tensor(out=places, in0=bank[4][0:BLK, 0:NG * E], scalar=-1.0, in1=places, op0=ALU.add, op1=ALU.add))
                signal(dve, dve.tensor_copy(idx_all[:, :], places), dest_ready, i + 1)

                def block_pass(n, b, bd, s, stores):
                    dve.wait_ge(s["silu"], n)
                    dve.wait_ge(s["up"], n)
                    dve.tensor_tensor(hb[b], sg[b], bank[3][:, 0:256], ALU.mult).then_inc(s["h"], 1)
                    dve.wait_ge(s["ht"], n)
                    dve.tensor_copy(hts[b], bank[5][:, 0:256]).then_inc(s["hts"], 1)
                    dve.wait_ge(s["down"], n)
                    dve.wait_ge(s["stored"], stores)
                    dve.tensor_copy(yb[b], bd[:, :]).then_inc(s["y"], 1)

                regular = [dict(silu=silu_ready, up=up_done, h=h_ready, ht=ht_done, hts=hts_ready, down=down_done, y=y_ready,
                                stored=y_stored[b]) for b in range(2)]
                with dve.Fori(0, E // 2) as it:
                    for b in range(2):
                        more = dve.value_load(extra_i[0:1, bass.ds(it * 2 + b, 1)], min_val=0, max_val=NG - 1)
                        with dve.If(more > 0):
                            with dve.Fori(0, more) as _g:
                                dve.reg_add(count, count, 1)
                                m = dve.snap(count)
                                block_pass(m, 2, bank[0], ex, dve.snap(m * 32))
                        block_pass(dve.snap(it * 2 + (E * i + b + 1)), b, bank[6 + b], regular[b], it * 32 + 32 * (E // 2 * i + 1))
                def combine(T):
                    y = ycomb[T]
                    dve.wait_ge(y_weighted, NT * i + T + 1)
                    dve.wait_ge(y_back[T], 32 * (i + 1))
                    step(dve.scalar_tensor_tensor(out=y[:, 0, :], in0=y[:, 1, :], scalar=wsel[:, 4 + T:5 + T], in1=y[:, 0, :],
                                                  op0=ALU.mult, op1=ALU.add))
                    combined(st, T, y[:, 0, :], [y[:, 0, 512 * n:512 * n + 512] for n in range(2)], step)
                norm_stage(st, combine)

            mixer_norm(0)
            moe(0)

            dve.wait_ge(hmT_ready, 2 * NT * 3)
            posf = ms_o[:, 28:32]
            step(dve.tensor_copy(posf, intc[:, 0:NT]))
            for T in range(NT):
                step(dve.tensor_scalar(ang[:, 32 * T:32 * T + 32], sml[:, S_INV:S_INV + 32], posf[:, T:T + 1], None, ALU.mult))
            step(dve.tensor_scalar(kround, ang, 1.0 / TWO_PI, None, ALU.mult))
            step(dve.tensor_scalar(kround, kround, MAGIC, None, ALU.add))
            step(dve.tensor_scalar(kround, kround, MAGIC, None, ALU.subtract))
            for part in (PI_A, PI_B, PI_C):
                step(dve.scalar_tensor_tensor(out=ang, in0=kround, scalar=-part, in1=ang, op0=ALU.mult, op1=ALU.add))
            signal(dve, dve.tensor_scalar(ang, ang, 3.1415925, -3.1415925, ALU.min, ALU.max), ang_ready, 1)
            dve.wait_ge(sin_ready, 1)

            def rotate(src, dst, n, T, last):
                cos = cs_t[:, T, :].unsqueeze(1).to_broadcast([P, n, 32])
                sin = sn_t[:, T, :].unsqueeze(1).to_broadcast([P, n, 32])
                x1, x2 = src[:, :, 0:32], src[:, :, 32:64]
                a, b = rt1[:, 0:n, :], rt2[:, 0:n, :]
                step(dve.tensor_tensor(a, x1, cos, ALU.mult))
                step(dve.tensor_tensor(b, x2, sin, ALU.mult))
                step(dve.tensor_tensor(dst[:, :, 0:32], a, b, ALU.subtract))
                step(dve.tensor_tensor(a, x2, cos, ALU.mult))
                step(dve.tensor_tensor(b, x1, sin, ALU.mult))
                last(dve.tensor_tensor(dst[:, :, 32:64], a, b, ALU.add))

            for T in range(NT + 1):
                if T < NT:
                    dve.wait_ge(lms_ready, T + 1)
                    signal(dve, dve.reciprocal(ms_o[:, 8 * T + 4:8 * T + 6], ms_o[:, 8 * T + 2:8 * T + 4]), lrs_ready, T + 1)
                    if T >= 2:
                        dve.wait_ge(latT_done, T - 1)
                    dve.wait_ge(lat_ready, T + 1)
                    k = krd[T % 2]
                    rotate(bank[2 * (T % 2) + 1][:, 256:320].rearrange("p (h f) -> p h f", h=1),
                           k[:, 0:ROPE].rearrange("p (h f) -> p h f", h=1), 1, T, step)
                    signal(dve, dve.tensor_copy(k[:, ROPE:2 * ROPE], k[:, 0:ROPE]), kr_ready, T + 1)
                if T:
                    dve.wait_ge(latT_done, T)
                    dve.wait_ge(latT_ready, T)
                    signal(dve, dve.tensor_copy(krT[:, tcols(T - 1)], bank[5][:, 2 * P:3 * P]), krT_ready, T)
            for T in range(NT):
                dve.wait_ge(qr_done, T + 1)
                if T >= 2:
                    dve.wait_ge(qrt_done, T - 1)
                rotate(bank[(6, 2)[T % 2]][:, :].rearrange("p (h f) -> p h f", h=MH), qr[T % 2].rearrange("p (h f) -> p h f", h=MH), MH, T,
                       lambda ins: signal(dve, ins, qr_ready, T + 1))

            scale = float(NOPE + ROPE) ** -0.5
            for u in range(MH * NT + 1):
                if u < MH * NT:
                    nk = P * (u % NT + 1)
                    dve.wait_ge(s_done, u + 1)
                    step(dve.tensor_reduce(att_m[:, u:u + 1], bank[2 + u % 2][:, 0:nk], AX.X, ALU.max))
                    signal(dve, dve.tensor_scalar(att_n[:, u:u + 1], att_m[:, u:u + 1], -scale, None, ALU.mult), nm_ready, u + 1)
                if u >= 1:
                    v = u - 1
                    nk = P * (v % NT + 1)
                    dve.wait_ge(p_ready, v + 1)
                    step(dve.reciprocal(att_r[:, v:v + 1], att_s[:, v:v + 1]))
                    signal(dve, dve.tensor_scalar(prob[v % 2][:, 0:nk], prob[v % 2][:, 0:nk], att_r[:, v:v + 1], None, ALU.mult),
                           pn_ready, v + 1)
            mixer_norm(2)
            moe(1)

        @block.gpsimd
        def _(pool):
            count = pool.alloc_register("pool_extra")
            pool.reg_mov(count, 0)
            pool.sem_inc(t_done, 2)
            pool.sem_inc(ex["t"], 1)

            pool.wait_ge(proj_done, 1)
            signal(pool, pool.memset(area_b[0:120, 0:1024], 0.0), pool_step, 1)
            pool.dma_start(y_rows[BLK * E:BLK * E + 960, :].rearrange("(p r) d -> p r d", p=120),
                           area_b[0:120, 0:1024].unsqueeze(1).to_broadcast([120, 8, 1024])).then_inc(y_cleared, 16)

            for n in range(PARKED):
                pool.wait_ge(part_ready, n + 1)
                pool.dma_start(rws[ROWS + 4 * n:ROWS + 4 * n + 4, :], parts[part_buffer(n)][0:P:32, :]).then_inc(part_kept[part_buffer(n)], 16)

            def layer_norm(st):
                g, b = ln_rows[st % 2]
                pool.wait_ge(ln_rows_in, 32 * (st + 1))
                for T in range(NT - 1):
                    k = (NT - 1) * st + T
                    pool.wait_ge(z_ready, NT * st + T + 1)
                    y = lnr[T % 2] if st % 2 == 0 else ycomb[T][:, 0, :]
                    signal(pool, pool.tensor_tensor(y, y, g, ALU.mult), gain_done, k + 1)
                    pool.tensor_tensor(xres[:, T, :], y, b, ALU.add).then_inc(ln_done, 1)

            def moe(i):
                layer_norm(2 * i)
                pool.wait_ge(y_cleared, 16)
                for b in range(3):
                    ins = pool.memset(xg[b][0:BLK, :], 0.0)
                    signal(pool, ins, pool_step, 3 * i + b + 2)
                pool.wait_ge(dest_ready, i + 1)
                for b in range(2):
                    pool.wait_ge(hm_stored[b], 16 * NT // 2 * (i + 1))

                def gather(n, b, col, s, guard):
                    guard()
                    pool.tensor_copy(idx_col[:, b:b + 1], idx_all[:, bass.ds(col, 1)]).then_inc(s["col"], 1)
                    pool.wait_ge(s["col"], n)
                    pool.sem_inc(col_seen, 1)
                    pool.indirect_dma_start(out=xg[b][0:BLK, :], out_offset=None, in_=hm_rows[i],
                                            in_offset=bass.IndirectOffsetOnAxis(idx_col[:, b:b + 1], 0),
                                            bounds_check=SEQ - 1, oob_is_err=False).then_inc(s["gathered"], 16)

                regular = [dict(col=col_ready, gathered=gathered[b]) for b in range(2)]
                with pool.Fori(0, E // 2) as it:
                    for b in range(2):
                        n = pool.snap(it * 2 + (E * i + b + 1))
                        gather(n, b, it * 2 + b, regular[b],
                               lambda: pool.wait_ge(t_done, n))
                        more = pool.value_load(extra_i[0:1, bass.ds(it * 2 + b, 1)], min_val=0, max_val=NG - 1)
                        with pool.If(more > 0):
                            with pool.Fori(0, more) as g:
                                pool.reg_add(count, count, 1)
                                m = pool.snap(count)
                                gather(m, 2, it * 2 + g * E + (E + b), ex,
                                       lambda: pool.wait_ge(ex["t"], m))
                for b in range(2):
                    pool.wait_ge(y_stored[b], 32 * (E // 2 * (i + 1) + 1))
                pool.wait_ge(ex["stored"], pool.snap(count) * 32 + 32)
                pool.sem_inc(col_seen, 1)
                for T in range(NT):
                    for k in range(2):
                        pool.indirect_dma_start(out=ycomb[T][:, k, :], out_offset=None, in_=y_rows,
                                                in_offset=bass.IndirectOffsetOnAxis(dest_i[:, 4 * k + T:4 * k + T + 1], 0))\
                            .then_inc(y_back[T], 16)
                layer_norm(2 * i + 1)

            moe(0)
            moe(1)


def kernel(x, c, positions, ada_w, ada_b, ln_g, ln_b, w_in_e, gdn_conv_w, gdn_a_log, gdn_dt_bias, gdn_norm_w,
           sc_conv_w, w_out_e, w_in_o, q_a_norm, w_q_b, kv_a_norm, w_kv_b, w_out_o, router_w, router_bias,
           w_gate, w_up, w_down):
    from concourse import bacc
    from concourse.bass_utils import run_bass_kernel_spmd

    def a(v):
        return np.ascontiguousarray(v)

    def taps(w, tiles):
        return a(w).reshape(w.shape[0], tiles, P).transpose(2, 1, 0).reshape(P, -1)

    def everywhere(v):
        return np.broadcast_to(a(v).reshape(1, -1), (P, a(v).size))

    inv = (np.float32(10000.0) ** (-np.arange(0, ROPE, 2, dtype=np.float32) / np.float32(ROPE))).astype(np.float32)
    ba = 3 * H * DK + H * DK
    small = np.concatenate([
        taps(a(gdn_conv_w)[0], 12), taps(a(sc_conv_w)[0], 4), a(gdn_norm_w)[0].reshape(P, 1),
        a(q_a_norm)[0].reshape(3, P).T, a(kv_a_norm)[0].reshape(2, P).T,
        everywhere(np.tile(a(gdn_a_log)[0], NT)), everywhere(np.tile(a(gdn_dt_bias)[0], NT)),
        a(c).reshape(P, NJ), a(router_w).reshape(P, NJ * E), a(a(w_in_e)[0][:, ba:ba + 2 * H]).reshape(P, NJ * 2 * H),
        everywhere(router_bias), everywhere(inv)], axis=1)
    rows = np.concatenate([a(ada_b).reshape(24, 512),
                           np.concatenate([a(ln_g).reshape(4, 2, 512), a(ln_b).reshape(4, 2, 512)], axis=1).reshape(16, 512)])
    token = np.arange(SEQ, dtype=np.int32).reshape(NT, P).T
    ints = np.concatenate([a(positions).reshape(NT, P).T, token], axis=1)
    arrays = dict(x=a(x)[0], small=a(small), const=constants(), rows=a(rows), ints=a(ints), ada_w=a(ada_w),
                  w_in_e=a(w_in_e)[0], w_out_e=a(w_out_e)[0], w_in_o=a(w_in_o)[0], w_q_b=a(w_q_b)[0], w_kv_b=a(w_kv_b)[0],
                  w_out_o=a(w_out_o)[0], w_gate=a(w_gate), w_up=a(w_up), w_down=a(w_down))
    nc = bacc.Bacc("TRN2", target_bir_lowering=False, num_devices=1)
    args = {n: nc.dram_tensor(f"in_{n}", v.shape, mybir.dt.from_np(v.dtype), kind="ExternalInput").ap() for n, v in arrays.items()}
    out = nc.dram_tensor("out_0", [SEQ, D_MODEL], F32, kind="ExternalOutput").ap()
    decoder_kernel(nc, out=out, **args)
    r = run_bass_kernel_spmd(nc, [{f"in_{n}": v for n, v in arrays.items()}], core_ids=[0])
    return r.results[0]["out_0"].reshape(1, SEQ, D_MODEL)
```

```python
from contextlib import ExitStack

import numpy as np

import concourse.bass as bass
from concourse import mybir

F32 = mybir.dt.float32
I32 = mybir.dt.int32
U32 = mybir.dt.uint32
ALU = mybir.AluOpType
ACT = mybir.ActivationFunctionType
AX = mybir.AxisListType

P = 128
D_MODEL, SEQ, DEPTH = 1024, 512, 2
NT = SEQ // P
NJ = D_MODEL // P
DN_ALPHA = (2.0 * DEPTH) ** 0.25
H, DK, CH = 4, 128, 64
QKV_W, SC_W = 3 * H * DK, 512
MH, NOPE, ROPE, VD = 8, 128, 64, 128
Q_LORA, KV_LORA = 384, 256
E, GROUPS, EPG, FE = 32, 4, 8, 512
BLK = 64
NG = SEQ // BLK
MAX_EXTRA = 2 * SEQ // (BLK + 1)
RING, SLOT = 6, 4096
LN_EPS, NORM_EPS = 1e-5, 1e-6
BIG = 1e30
MAGIC = 1.5 * 2 ** 23
TWO_PI = 6.283185307179586
PI_A = 6.28125
PI_B = 0.0019350051879882812
PI_C = TWO_PI - PI_A - PI_B

C_ID, C_ONE, C_CUM, C_BLK, C_DEC, C_DCT, C_LEV = 0, 128, 256, 384, 512, 640, 768
C_ATT, C_SUT, C_IO, C_EPS6, C_EPS5, C_HPI = 1536, 1664, 1792, 1856, 1857, 1858
C_SEL, C_SUM, N_CONST = 1859, 1883, 1915
CHUNKS, ROWS, DIRECT = 6, 40, 4
PARKED = 2 * DEPTH * CHUNKS - DIRECT
S_CW, S_SW, S_NW, S_QN, S_KN = 0, 48, 60, 61, 64
S_AL, S_DT, S_C, S_RW, S_BA, S_RB, S_INV = 66, 82, 98, 106, 362, 426, 458
N_SMALL = 490
LEVELS = (2, 4, 8, 16, 32)


def constants():
    c = np.zeros((P, N_CONST), np.float32)
    p, f = np.arange(P)[:, None], np.arange(P)[None, :]
    same = p // CH == f // CH
    c[:, C_ID:C_ID + P] = p == f
    c[:, C_ONE:C_ONE + P] = 1
    c[:, C_CUM:C_CUM + P] = same & (p <= f)
    c[:, C_BLK:C_BLK + P] = same
    c[:, C_DEC:C_DEC + P] = np.where(same & (f < p), 0, BIG)
    c[:, C_DCT:C_DCT + P] = np.where(same & (f >= p), 0, -BIG)
    c[:, C_LEV:C_LEV + P] = (p // 2 == f // 2) & (p % 2 == 1) & (f % 2 == 0)
    for n, s in enumerate(LEVELS):
        a = C_LEV + (n + 1) * P
        c[:, a:a + P] = (p // (2 * s) == f // (2 * s)) & (p % (2 * s) < s) & (f % (2 * s) >= s)
    c[:, C_ATT:C_ATT + P] = np.where(f <= p, 0, -BIG)
    c[:, C_SUT:C_SUT + P] = p < f
    c[:, C_IO:C_IO + BLK] = np.arange(BLK)
    c[:, C_EPS6], c[:, C_EPS5], c[:, C_HPI] = NORM_EPS, LN_EPS, np.pi / 2
    chunk = np.arange(DIRECT + PARKED)[None, :]
    c[:, C_SUM:C_SUM + E] = p % 32 == np.arange(E)[None, :]
    c[:, C_SEL:C_SUM] = (p == chunk) | ((p - ROWS) // 4 == chunk - DIRECT) & (p >= ROWS)
    return c


EARLY, BETWEEN = 3, 2
BEHIND = EARLY + 3 * BETWEEN
FILLING = [item for c, kind in enumerate("zchb") for item in [(kind, t) for t in range(4)]
           + [("park", n) for n in (range(EARLY + BETWEEN * c, EARLY + BETWEEN * (c + 1)) if kind != "b" else range(BEHIND, PARKED))]]
UNITS = [(q, half) for q, (kind, _) in enumerate(FILLING) for half in range(1 if kind == "park" else 2)]
BEFORE, SETUP, POINTS = 4, 6, 19


def units_at(pair, point):
    first = BEFORE + (SETUP + POINTS) * pair + (0 if point == 0 else SETUP - 1 + point)
    last = len(UNITS) if (pair, point) == (1, POINTS) else first + (SETUP if point == 0 else 1)
    return range(min(first, len(UNITS)), min(last, len(UNITS)))


def mixer_loads():
    loads = [load for c in range(EARLY) for load in ((f"in_e{c}", c), (f"park{c}", c))]
    for kind, t in FILLING:
        if kind == "park":
            loads.append((f"park{t}", t))
        elif t == 0:
            loads.append((f"in_e{3 + 'zchb'.index(kind)}", 3 + "zchb".index(kind)))
    return loads


def ring_plan():
    base, at = {}, 0
    for name, n in (("ada", DIRECT), *((name, 1) for name, _ in mixer_loads()), ("out_e", 2), ("moe0", 3 * E),
                    ("in_o", 2), ("qb", 2), ("kvb", 1), ("out_o", 2), ("moe1", 3 * E)):
        base[name] = at
        at += n
    return base


def decoder_kernel(nc, x, small, const, rows, ints, ada_w, w_in_e, w_out_e, w_in_o, w_q_b, w_kv_b,
                   w_out_o, w_gate, w_up, w_down, out):
    base = ring_plan()
    ctx = ExitStack()
    with ctx:
        def sb(name, shape, dt=F32):
            return ctx.enter_context(nc.sbuf_tensor(name, shape, dt))

        def sem(name):
            return ctx.enter_context(nc.semaphore(name))

        hm_rows = [nc.dram_tensor(f"hm_rows{i}", [SEQ, D_MODEL], F32, kind="Internal").ap() for i in range(DEPTH)]
        y_rows = nc.dram_tensor("y_rows", [(E + MAX_EXTRA) * BLK, D_MODEL], F32, kind="Internal").ap()

        ring = sb("ring", [P, RING, SLOT])
        xres = sb("xres", [P, NT, D_MODEL])
        cst = sb("cst", [P, N_CONST])
        sml = sb("sml", [P, N_SMALL])
        rws = sb("rws", [P, 512])
        part = sb("part", [P, 512])
        intc = sb("intc", [P, 8], I32)
        area_a = sb("area_a", [P, 4096])
        area_b = sb("area_b", [P, 4096])
        area_c = sb("area_c", [P, 6144])
        area_d = sb("area_d", [P, 2048])
        modss = sb("modss", [P, 2048])
        area_e = sb("area_e", [P, 1024])
        gate_a = sb("gate_a", [P, 1024])
        tiny = sb("tiny", [P, 208])
        cond = sb("cond", [P, NJ])
        statb = sb("statb", [P, 32])

        def cc(a, n=P):
            return cst[:, a:a + n]
        ident, ones = cc(C_ID), cc(C_ONE)

        hmT = area_a[:, :].rearrange("p (j t) -> p j t", j=NJ)
        gate_b = area_c[:, 5120:6144]
        hm = [[area_e[:, :], area_d[:, 1024:2048] if st % 2 == 0 else area_c[:, 4096:5120]] for st in range(2 * DEPTH)]
        ln_rows = [(area_c[:, 2048:3072], area_c[:, 3072:4096]), (area_d[:, 0:1024], area_c[:, 4096:5120])]
        lnr = [area_c[:, 0:1024], area_c[:, 1024:2048]]
        gates = [gate_a[:, :], gate_b]

        parts = [part[:, :], area_b[:, 1536:2048]] + [area_a[:, 512 * n:512 * n + 512] for n in range(2)]
        part_buffer = [n % 2 if EARLY <= n < EARLY + 2 * BETWEEN else 2 + n % 2 if n >= BEHIND else 0 for n in range(PARKED)]
        kept_before = [[part_buffer[:n].count(b) for n in range(PARKED + 1)] for b in range(len(parts))]

        qkv = area_c[:, :].rearrange("p (m t) -> p m t", m=12)
        zs = area_d[:, :].rearrange("p (h t) -> p h t", h=H)
        scc = [area_b[:, 1024:1536], area_b[:, 1536:2048]]
        yb_T = area_b[:, 2048:4096].rearrange("p (h t) -> p h t", h=4)
        sq = [area_e[:, 0:512], area_e[:, 512:1024]]
        rq = [modss[:, 0:512], modss[:, 512:1024]]
        pool16 = [xres[:, n // 2, 512 * (n % 2):512 * (n % 2) + 512] for n in range(8)] \
            + [a[:, 512 * n:512 * n + 512] for a in (area_b, gate_a) for n in range(2)] + [modss[:, 512 * n:512 * n + 512] for n in range(4)]

        def hv(ap):
            return ap.rearrange("p (h t) -> p h t", h=H)
        d_L, d_IT, d_X, d_Y, d_MT, d_KB, d_KD, d_U = [[hv(pool16[2 * n + k]) for k in range(2)] for n in range(8)]
        state = hv(area_e[:, 0:512])
        os_ = hv(area_e[:, 512:1024])
        g_t, g_sp, g_g, g_gc, g_eg, g_kd, g_beg, g_beta, g_ea, g_ms = [tiny[:, 16 * n:16 * n + 16] for n in range(10)]
        g_last = tiny[:, 160:192].rearrange("p (t h c) -> p t h c", t=NT, h=H)

        qaT = area_c[:, 0:1536].rearrange("p (j t) -> p j t", j=3)
        kaT = area_c[:, 1536:2560].rearrange("p (j t) -> p j t", j=2)
        krT = area_c[:, 2560:3072]
        qrT = area_c[:, 3072:5120].rearrange("p (j t) -> p j t", j=4)
        qr = [area_c[:, 5120:5632], area_b[:, 1024:1536]]
        krd = [area_c[:, 5632:5760], area_b[:, 1536:1664]]
        ms_o = area_c[:, 5760:5792]
        lat = [area_d[:, 0:640], area_b[:, 0:640]]
        cs_t = area_d[:, 1024:1152].rearrange("p (t f) -> p t f", t=NT)
        sn_t = area_d[:, 1152:1280].rearrange("p (t f) -> p t f", t=NT)
        rt1 = area_d[:, 1280:1536].rearrange("p (h f) -> p h f", h=MH)
        rt2 = area_d[:, 1536:1792].rearrange("p (h f) -> p h f", h=MH)
        ang = area_d[:, 1792:1920]
        kround = area_d[:, 1920:2048]
        v_tok = area_a[:, :].rearrange("p (t n) -> p t n", t=NT)
        qnT = [modss[:, 0:512], modss[:, 512:1024]]
        knT = [modss[:, 1024:1536], modss[:, 1536:2048]]
        prob = [area_e[:, 0:512], area_e[:, 512:1024]]
        probT = [area_d[:, 0:512], area_d[:, 512:1024]]
        oT = area_b[:, :].rearrange("p (h t) -> p h t", h=MH)
        att_m, att_n, att_s, att_r = [tiny[:, 32 * n:32 * n + 32] for n in range(4)]

        xg = [area_b[:, 1024 * n:1024 * n + 1024] for n in range(3)]
        xT = [area_c[:, 512 * n:512 * n + 512].rearrange("p (j s) -> p j s", j=NJ) for n in range(3)]
        sg = [area_c[:, 1536 + 256 * n:1792 + 256 * n] for n in range(3)]
        hb = [area_c[:, 2304 + 256 * n:2560 + 256 * n] for n in range(3)]
        hts = [area_c[:, 3072 + 256 * n:3328 + 256 * n] for n in range(3)]
        yb = [area_b[:, 3072:3584], area_b[:, 3584:4096], area_a[:, 0:512]]
        idx_all = sb("idx_all", [BLK, NG * E], I32)
        idx_col = sb("idx_col", [BLK, 4], I32)
        dest_i = sb("dest_i", [P, 8], I32)
        extra_i = sb("extra_i", [1, E], I32)
        mi = sb("mi", [P, 32], U32)
        r_sc, r_bi, r_m8, r_tmp, r_o1, r_o2 = [area_d[:, 128 * n:128 * n + 128] for n in range(6)]
        r_oh, r_rk = [area_d[:, 768 + 128 * n:896 + 128 * n] for n in range(2)]
        r_cum = area_d[:, 1024:1024 + (NT + 1) * E]
        r_gs, r_gm, r_ig, r_lm = [area_d[:, 1408 + 32 * n:1440 + 32 * n] for n in range(4)]
        r_sm = area_d[:, 1536:1664]
        wsel = tiny[:, 192:200]
        ycomb = [a.rearrange("p (k d) -> p k d", k=2) for a in (area_c[:, 0:2048], area_c[:, 2048:4096],
                                                                area_b[:, 0:2048], area_b[:, 2048:4096])]
        diag = [area_a[:, 1024 + 512 * k:1536 + 512 * k].rearrange("p (t s) -> p t s", t=NT) for k in range(2)]
        place = [area_a[:, 2048 + 256 * k:2304 + 256 * k].rearrange("p (t s) -> p t s", t=NT) for k in range(2)]
        table = [area_a[:, 1024 * k:1024 * k + 1024].rearrange("p (t g e) -> p t g e", t=NT, g=NG) for k in range(2)]

        bank = [ctx.enter_context(nc.psum_tensor(f"bank{n}", [P, 512], F32)) for n in range(8)]

        ring_full = [sem(f"ring_full{n}") for n in range(RING)]
        slot_free = sem("slot_free")
        small_in, inputs_in, x_in = sem("small_in"), sem("inputs_in"), sem("x_in")
        act_step, dve_step, pool_step = sem("act_step"), sem("dve_step"), sem("pool_step")
        park_done, part_ready = sem("park_done"), sem("part_ready")
        part_kept = [sem(f"part_kept{n}") for n in range(len(parts))]
        cond_ready, ada_done, mod_ready = sem("cond_ready"), sem("ada_done"), sem("mod_ready")
        hm_ready, tr_done, hmT_ready = sem("hm_ready"), sem("tr_done"), sem("hmT_ready")
        ln_rows_in, y_taken = sem("ln_rows_in"), sem("y_taken")
        ln_done, diag_ready = sem("ln_done"), sem("diag_ready")
        var_ready, std_ready, rstd_ready, z_ready = sem("var_ready"), sem("std_ready"), sem("rstd_ready"), sem("z_ready")
        gain_done = sem("gain_done")
        quarters_done, quarters_ready = sem("quarters_done"), sem("quarters_ready")
        proj_done, conv_done, silu_done, sq_ready = sem("proj_done"), sem("conv_done"), sem("silu_done"), sem("sq_ready")
        ssq_done, rt_ready, qk_ready, fill_done = sem("ssq_done"), sem("rt_ready"), sem("qk_ready"), sem("fill_done")
        fill_taken = [sem(f"fill_taken{n}") for n in range(2)]
        ba_done, t_ready, sp_ready, g_ready, gc_done = sem("ba_done"), sem("t_ready"), sem("sp_ready"), sem("g_ready"), sem("gc_done")
        gcs_ready, ge_ready, gates_ready = sem("gcs_ready"), sem("ge_ready"), sem("gates_ready")
        cg_ready, gcb_done, kq_done, eb_ready, dd_ready, dx_ready = (sem("cg_ready"), sem("gcb_done"), sem("kq_done"),
                                                                    sem("eb_ready"), sem("dd_ready"), sem("dx_ready"))
        x0_ready, xt_done, y0_ready = sem("x0_ready"), sem("xt_done"), sem("y0_ready")
        mt_done, mt_ready, y2_done, lv_ready = sem("mt_done"), sem("mt_ready"), sem("y2_done"), sem("lv_ready")
        kt_done, kd_ready, vt_done, vb_ready = sem("kt_done"), sem("kd_ready"), sem("vt_done"), sem("vb_ready")
        uw_done, u_ready, wt_ready = sem("uw_done"), sem("u_ready"), sem("wt_ready")
        vn_done, vn_ready, sd_done, s_ready, o_done = sem("vn_done"), sem("vn_ready"), sem("sd_done"), sem("s_ready"), sem("o_done")
        orms_ready, orec_ready, os_ready, ot_done, ya_ready = (sem("orms_ready"), sem("orec_ready"), sem("os_ready"),
                                                              sem("ot_done"), sem("ya_ready"))
        y_done = sem("y_done")
        lat_done, lms_ready, lrs_ready, lat_ready, kr_ready = sem("lat_done"), sem("lms_ready"), sem("lrs_ready"), sem("lat_ready"), sem("kr_ready")
        latT_done, latT_ready, krT_ready = sem("latT_done"), sem("latT_ready"), sem("krT_ready")
        ang_ready, sin_ready = sem("ang_ready"), sem("sin_ready")
        qr_done, qr_ready, qrt_done, qrT_ready, v_done, v_ready = (sem("qr_done"), sem("qr_ready"), sem("qrt_done"),
                                                                   sem("qrT_ready"), sem("v_done"), sem("v_ready"))
        qkn_done, qkn_ready, s_done, nm_ready, p_ready, pn_ready = (sem("qkn_done"), sem("qkn_ready"), sem("s_done"),
                                                                    sem("nm_ready"), sem("p_ready"), sem("pn_ready"))
        pt_done, pt_ready, av_done, oT_ready = sem("pt_done"), sem("pt_ready"), sem("av_done"), sem("oT_ready")
        hm_stored = [sem(f"hm_stored{n}") for n in range(2)]
        rows_seen, col_seen = sem("rows_seen"), sem("col_seen")
        logit_done, score_ready, oh_ready, rank_done, dest_ready = (sem("logit_done"), sem("score_ready"), sem("oh_ready"),
                                                                    sem("rank_done"), sem("dest_ready"))
        table_ready, table_done = sem("table_ready"), sem("table_done")
        col_ready, t_done, xT_ready = sem("col_ready"), sem("t_done"), sem("xT_ready")
        gathered, y_stored = ([sem(f"{n}{b}") for b in range(2)] for n in ("gathered", "y_stored"))
        y_back = [sem(f"y_back{T}") for T in range(NT)]
        gate_done, up_done, silu_ready, h_ready = sem("gate_done"), sem("up_done"), sem("silu_ready"), sem("h_ready")
        ht_done, hts_ready, down_done, y_ready = sem("ht_done"), sem("hts_ready"), sem("down_done"), sem("y_ready")
        x_names = ("col", "gathered", "t", "xT", "gate", "up", "silu", "h", "ht", "hts", "down", "y", "stored")
        ex = {n: sem(f"extra_{n}") for n in x_names}
        out_stored, y_cleared = sem("out_stored"), sem("y_cleared")

        block = ctx.enter_context(nc.Block())

        class InOrder:

            def __init__(self, eng, done):
                self.eng, self.done, self.n = eng, done, 0

            def __call__(self, ins):
                self.n += 1
                ins.then_inc(self.done, 1)
                self.eng.wait_ge(self.done, self.n)

        def signal(eng, ins, done, value):
            ins.then_inc(done, 1)
            eng.wait_ge(done, value)

        def tcols(T):
            return slice(P * T, P * T + P)

        @block.sync
        def _(sp):
            def load(n, src, dst_cols=SLOT, shape=None):
                former = n - RING
                layer = [i for i in range(DEPTH) if 0 <= former - base[f"moe{i}"] < 3 * E]
                if layer:
                    e, m = divmod(former - base[f"moe{layer[0]}"], 3)
                    sp.wait_ge((gate_done, up_done, down_done)[m], E * layer[0] + e + 1)
                elif former >= 0:
                    sp.wait_ge(slot_free, former + 1 - 3 * E * sum(former >= base[f"moe{i}"] for i in range(DEPTH)))
                dst = ring[:, n % RING, 0:dst_cols]
                if shape:
                    dst = dst.rearrange("p (j n) -> p j n", j=shape)
                sp.dma_start(dst, src).then_inc(ring_full[n % RING], 16)

            def columns(w, a, b, j, order="(p j) n -> p j n"):
                return w[:, a:b].rearrange(order, j=j)

            def ada(name, k):
                (i, s), c = divmod(k // CHUNKS, 2), k % CHUNKS
                load(base[name], columns(ada_w[i, s], 512 * c, 512 * c + 512, NJ), shape=NJ)

            def experts(name, i):
                n0 = base[name]

                def matrix(m, e):
                    src = (w_gate, w_up, w_down)[m][i, bass.ds(e, 1)]
                    return src.rearrange("o (p j) n -> p (o j) n" if m < 2 else "o (j p) n -> p (o j) n", p=P)
                for k in range(6):
                    load(n0 + k, matrix(k % 3, k // 3), shape=(NJ if k % 3 < 2 else 4))
                with sp.Fori(1, E // 2) as it:
                    for b in range(2):
                        e = sp.snap(it * 2 + b)
                        done = sp.snap(it * 2 + (E * i + b - 1))
                        for m, used in enumerate((gate_done, up_done, down_done)):
                            slot = (n0 + 3 * b + m) % RING
                            sp.wait_ge(used, done)
                            sp.dma_start(ring[:, slot, :].rearrange("p (j n) -> p j n", j=(NJ if m < 2 else 4)),
                                         matrix(m, e)).then_inc(ring_full[slot], 16)

            sp.dma_start(sml[:, :], small).then_inc(small_in, 16)
            for c in range(DIRECT):
                load(base["ada"] + c, columns(ada_w[0, 0], 512 * c, 512 * c + 512, NJ), shape=NJ)
                if c == 0:
                    sp.dma_start(cst[:, :], const).then_inc(inputs_in, 16)
                    sp.dma_start(rws[0:ROWS, :], rows).then_inc(inputs_in, 16)
                    sp.dma_start(intc[:, :], ints).then_inc(inputs_in, 16)
            sp.dma_start(xres[:, :, :], x.rearrange("(t p) d -> p t d", p=P)).then_inc(x_in, 16)
            first_column = (0, 512, 1024, 1536, 2568, 3080, 2056)
            for name, c in mixer_loads():
                if name.startswith("park"):
                    ada(name, DIRECT + c)
                else:
                    load(base[name], columns(w_in_e, first_column[c], first_column[c] + 512, NJ), shape=NJ)
            for c in range(2):
                load(base["out_e"] + c, columns(w_out_e, 512 * c, 512 * c + 512, NJ, "(j p) n -> p j n"), shape=NJ)
            experts("moe0", 0)
            for T in range(NT):
                sp.wait_ge(y_back[T], 32)
            load(base["in_o"], columns(w_in_o, 0, 384, NJ), 384 * NJ, NJ)
            load(base["in_o"] + 1, columns(w_in_o, 384, 704, NJ), 320 * NJ, NJ)
            for c in range(2):
                load(base["qb"] + c, columns(w_q_b, 768 * c, 768 * c + 768, 3, "(j p) n -> p j n"), 768 * 3, 3)
            load(base["kvb"], columns(w_kv_b, 0, 2048, 2, "(j p) n -> p j n"), shape=2)
            for c in range(2):
                load(base["out_o"] + c, columns(w_out_o, 512 * c, 512 * c + 512, NJ, "(j p) n -> p j n"), shape=NJ)
            experts("moe1", 1)

        @block.tensor
        def _(pe):
            def full(n):
                pe.wait_ge(ring_full[n % RING], 16 * (n // RING + 1))
                return ring[:, n % RING, :]

            def quarter_sums(w, ps):
                for half in range(2):
                    for g in range(4):
                        j = 4 * half + g
                        mm = pe.matmul(ps[32 * g:32 * g + 32, :], cond[:, j:j + 1].to_broadcast([P, 32]), w[:, 512 * j:512 * j + 512],
                                       start=(half == 0), stop=(half == 1))
                return mm

            def direct():
                for c in range(DIRECT + 1):
                    if c < DIRECT:
                        w = full(base["ada"] + c)
                        if c >= 2:
                            pe.wait_ge(quarters_ready, c - 1)
                        quarter_sums(w, bank[c % 2]).then_inc(quarters_done, 1)
                        pe.wait_ge(quarters_done, c + 1)
                        pe.sem_inc(slot_free, 1)
                    if c:
                        ps = bank[2 + (c - 1) % 2][:, :]
                        pe.wait_ge(inputs_in, 48)
                        pe.wait_ge(quarters_ready, c)
                        if c >= 3:
                            pe.wait_ge(mod_ready, c - 2)
                        pe.matmul(ps, cst[:, C_SUM:C_SUM + 1].to_broadcast([P, P]), parts[(c - 1) % 2], start=True, stop=False)
                        pe.matmul(ps, cst[0:ROWS, C_ID + c - 1:C_ID + c].to_broadcast([ROWS, P]), rws[0:ROWS, :], start=False, stop=True)\
                            .then_inc(ada_done, 1)

            def park(n, ps):
                mm = quarter_sums(full(base[f"park{n}"]), ps)
                mm.then_inc(park_done, 1)
                pe.wait_ge(park_done, n + 1)
                pe.sem_inc(slot_free, 1)

            def fill(units):
                for u in units:
                    q, half = UNITS[u]
                    kind, t = FILLING[q]
                    if half == 0 and q >= 2:
                        pe.wait_ge(fill_taken[q % 2], q // 2)
                    if kind == "park":
                        park(t, bank[6 + q % 2])
                        pe.sem_inc(fill_done, 1)
                        continue
                    c = 3 + "zchb".index(kind)
                    w = full(base[f"in_e{c}"])
                    for j in range(4 * half, 4 * half + 4):
                        mm = pe.matmul(bank[6 + q % 2][:, :], w[:, 512 * j + P * t:512 * j + P * t + P], hmT[:, j, :],
                                       start=(j == 0), stop=(j == NJ - 1))
                    if half == 1:
                        mm.then_inc(fill_done, 1)
                        if t == 3:
                            pe.wait_ge(fill_done, q + 1)
                            pe.sem_inc(slot_free, 1)

            def modulations(chunks):
                for b in range(len(parts)):
                    pe.wait_ge(part_kept[b], 16 * kept_before[b][PARKED])
                for k in chunks:
                    pe.wait_ge(mod_ready, k - 1)
                    rows_n = ROWS + 4 * PARKED
                    pe.matmul(bank[k % 2][:, :], cst[0:rows_n, C_SEL + k:C_SEL + k + 1].to_broadcast([rows_n, P]), rws[0:rows_n, :],
                              start=True, stop=True).then_inc(ada_done, 1)

            def modulated(st):
                for T in range(NT):
                    k = NT * st + T
                    pe.wait_ge(hm_ready, k + 1)
                    if k:
                        pe.wait_ge(hmT_ready, 2 * k)
                    hv_ = hm[st][T % 2].rearrange("p (f j) -> p j f", j=NJ)
                    for j in range(NJ):
                        mm = pe.transpose(bank[2 + j // 4][:, P * (j % 4):P * (j % 4) + P], hv_[:, j, :], ident)
                        if j % 4 == 3:
                            mm.then_inc(tr_done, 1)

            def out_proj(name, tiles, st):
                w = [full(base[name]), full(base[name] + 1)]
                for T in range(NT):
                    if T >= 2:
                        pe.wait_ge(y_taken, NT * st + T - 1)
                    for n in range(2):
                        for j in range(NJ):
                            mm = pe.matmul(bank[2 * (T % 2) + n][:, :], tiles[j][:, tcols(T)], w[n][:, 512 * j:512 * j + 512],
                                           start=(j == 0), stop=(j == NJ - 1))
                            if T == NT - 1 and j == NJ - 1 and n == 0:
                                mm.then_inc(slot_free, 1)
                    mm.then_inc(y_done, 1)
                pe.wait_ge(y_done, NT * (st + 1))
                pe.sem_inc(slot_free, 1)

            def narrow(n, a, step, dst, width, done, meanwhile=lambda: None):
                for half in range(2):
                    for g in range(4):
                        c = a + step * (4 * half + g)
                        mm = pe.matmul(bank[4][32 * g:32 * g + 32, :], sml[:, c:c + 32], hmT[:, 4 * half + g, :],
                                       start=(half == 0), stop=(half == 1))
                mm.then_inc(quarters_done, 1)
                meanwhile()
                pe.wait_ge(quarters_ready, DIRECT + n)
                for T in range(NT):
                    mm = pe.matmul(dst[:, width * T:width * T + width], part[:, tcols(T)], cst[:, C_SUM:C_SUM + width], start=True, stop=True)
                mm.then_inc(done, 1)

            pe.wait_ge(cond_ready, 1)
            direct()
            modulated(0)
            pe.wait_ge(hmT_ready, 2 * NT)
            def project(m):
                w = full(base[f"in_e{m // 4}"])
                for j in range(NJ):
                    a = 512 * j + P * (m % 4)
                    mm = pe.matmul(bank[m % 4][:, :], w[:, a:a + P], hmT[:, j, :], start=(j == 0), stop=(j == NJ - 1))
                mm.then_inc(proj_done, 1)
            narrow(1, S_BA, 2 * H, bank[7], 2 * H, ba_done, lambda: project(0))

            def ssq(m):
                pe.wait_ge(sq_ready, m + 1)
                if m >= 2:
                    pe.wait_ge(rt_ready, m - 1)
                pe.matmul(bank[4 + m % 2][:, :], ones, sq[m % 2], start=True, stop=True).then_inc(ssq_done, 1)

            for m in range(12):
                if m >= 4:
                    pe.wait_ge(conv_done, m - 3)
                if m:
                    project(m)
                if m % 4 == 3:
                    pe.wait_ge(proj_done, m + 1)
                    pe.sem_inc(slot_free, 1)
                    if m > 3:
                        pe.wait_ge(part_ready, m // 4)
                    park(m // 4, bank[6])
                if 2 <= m < 10:
                    ssq(m - 2)
                if m == 10:
                    pe.wait_ge(g_ready, 1)
                    pe.matmul(bank[7][:, 0:16], cc(C_CUM), g_g, start=True, stop=True)
                    pe.matmul(bank[7][:, 16:32], cc(C_BLK), g_g, start=True, stop=True).then_inc(gc_done, 1)
            pe.wait_ge(part_ready, 3)
            pe.wait_ge(gcs_ready, 1)
            fill(range(BEFORE))
            pe.wait_ge(gates_ready, 1)
            pe.wait_ge(conv_done, 12)
            pe.wait_ge(rt_ready, 8)
            for pair in range(2):
                tiles = [(2 * pair + k, k, [bank[3 * k + n] for n in range(3)]) for k in range(2)]
                for T, k, B in tiles:
                    if pair:
                        pe.wait_ge(ya_ready, T - 1)
                    pe.wait_ge(cg_ready, T + 1)
                    pe.matmul(B[0][:, :], ones, d_MT[k].rearrange("p h t -> p (h t)"), start=True, stop=True).then_inc(gcb_done, 1)
                    pe.wait_ge(qk_ready, 8)
                    for h in range(H):
                        pe.matmul(B[1][:, P * h:P * h + P], qkv[:, 4 + h, tcols(T)], qkv[:, 4 + h, tcols(T)], start=True, stop=True)
                    for h in range(H):
                        mm = pe.matmul(B[2][:, P * h:P * h + P], qkv[:, 4 + h, tcols(T)], qkv[:, h, tcols(T)], start=True, stop=True)
                    mm.then_inc(kq_done, 1)
                fill(units_at(pair, 0))
                for T, k, B in tiles:
                    pe.wait_ge(x0_ready, T + 1)
                    for h in range(H):
                        mm = pe.transpose(B[0][:, P * h:P * h + P], d_X[k][:, h, :], ident)
                    mm.then_inc(xt_done, 1)
                for lv in range(5):
                    for T, k, B in tiles:
                        n = (pair * 5 + lv) * 2 + k
                        pe.wait_ge(y0_ready, T + 1)
                        if lv:
                            pe.wait_ge(lv_ready, n - 1)
                        for h in range(H):
                            mm = pe.matmul(B[1][:, P * h:P * h + P], d_L[k][:, h, :], d_Y[k][:, h, :], start=True, stop=True)
                        mm.then_inc(mt_done, 1)
                    fill(units_at(pair, 1 + 2 * lv))
                    if lv == 1:
                        for T, k, B in tiles:
                            for h in range(H):
                                mm = pe.transpose(B[0][:, P * h:P * h + P], qkv[:, 4 + h, tcols(T)], ident)
                            mm.then_inc(kt_done, 1)
                    if lv == 3:
                        for T, k, B in tiles:
                            pe.wait_ge(kd_ready, T + 1)
                            for h in range(H):
                                mm = pe.transpose(B[0][:, P * h:P * h + P], qkv[:, 8 + h, tcols(T)], ident)
                            mm.then_inc(vt_done, 1)
                    for T, k, B in tiles:
                        n = (pair * 5 + lv) * 2 + k
                        pe.wait_ge(mt_ready, n + 1)
                        for h in range(H):
                            mm = pe.matmul(B[2][:, P * h:P * h + P], d_X[k][:, h, :], d_MT[k][:, h, :], start=True, stop=True)
                        for h in range(H):
                            mm = pe.matmul(B[1][:, P * h:P * h + P], d_MT[k][:, h, :], d_X[k][:, h, :], start=True, stop=True)
                        mm.then_inc(y2_done, 1)
                    fill(units_at(pair, 2 + 2 * lv))
                for T, k, B in tiles:
                    pe.wait_ge(lv_ready, pair * 10 + 9 + k)
                    pe.wait_ge(vb_ready, T + 1)
                    for h in range(H):
                        pe.matmul(B[1][:, P * h:P * h + P], d_Y[k][:, h, :], qkv[:, 8 + h, tcols(T)], start=True, stop=True)
                    for h in range(H):
                        mm = pe.matmul(B[2][:, P * h:P * h + P], d_KB[k][:, h, :], d_Y[k][:, h, :], start=True, stop=True)
                    mm.then_inc(uw_done, 1)
                fill(units_at(pair, 11))
                def output_turn(T, B):
                    pe.wait_ge(os_ready, T + 1)
                    for h in range(H):
                        mm = pe.transpose(B[0][:, P * h:P * h + P], os_[:, h, :], ident)
                    mm.then_inc(ot_done, 1)
                pe.wait_ge(vb_ready, 2 * pair + 2)
                for T, k, B in tiles:
                    pe.wait_ge(wt_ready, T + 1)
                    pe.wait_ge(u_ready, T + 1)
                    for c in range(2):
                        n, r = 2 * T + c, slice(CH * c, CH * c + CH)
                        tc = slice(P * T + CH * c, P * T + CH * c + CH)
                        pe.wait_ge(s_ready, n + 1)
                        for h in range(H):
                            mm = pe.matmul(B[0][r, P * h:P * h + P], qkv[:, 4 + h, tc], state[:, h, :], start=True, stop=True)
                        mm.then_inc(vn_done, 1)
                        if (k, c) == (1, 1):
                            output_turn(T - 1, tiles[0][2])
                        fill(units_at(pair, 12 + 4 * k + 2 * c))
                        pe.wait_ge(vn_ready, n + 1)
                        for h in range(H):
                            mm = pe.matmul(B[1][:, P * h:P * h + P], d_KD[k][r, h, :], d_U[k][r, h, :], start=True, stop=True)
                        mm.then_inc(sd_done, 1)
                        for h in range(H):
                            pe.matmul(B[2][r, P * h:P * h + P], qkv[:, h, tc], state[:, h, :], start=True, stop=False)
                            mm = pe.matmul(B[2][r, P * h:P * h + P], d_IT[k][r, h, r], d_U[k][r, h, :], start=False, stop=True)
                        mm.then_inc(o_done, 1)
                        fill(units_at(pair, 13 + 4 * k + 2 * c))
                output_turn(tiles[1][0], tiles[1][2])

            pe.wait_ge(ya_ready, NT)
            modulations(range(DIRECT, 2 * CHUNKS))
            pe.wait_ge(mod_ready, 2 * CHUNKS)
            out_proj("out_e", [zs[:, j, :] for j in range(4)] + [yb_T[:, j, :] for j in range(4)], 0)
            pe.wait_ge(y_taken, NT)

            count = pe.alloc_register("pe_extra")
            pe.reg_mov(count, 0)

            def moe(i, name):
                st = 2 * i + 1
                modulated(st)
                pe.wait_ge(hmT_ready, 2 * NT * (st + 1))
                narrow(i + 2, S_RW, E, bank[4], E, logit_done)
                if i == 0:
                    modulations(range(2 * CHUNKS, 3 * CHUNKS))
                pe.wait_ge(oh_ready, i + 1)
                pe.matmul(bank[5][:, 0:NT * E], cc(C_SUT), r_oh, start=True, stop=False)
                pe.matmul(bank[5][:, 0:NT * E], ones, r_cum[:, 0:NT * E], start=False, stop=True)
                pe.matmul(bank[5][:, NT * E:(NT + 1) * E], ones, r_cum[:, NT * E:(NT + 1) * E], start=True, stop=True).then_inc(rank_done, 1)
                for n in range(2 * NT):
                    k, T = divmod(n, NT)
                    if T == 0:
                        pe.wait_ge(table_ready, 2 * i + k + 1)
                    mm = pe.matmul(bank[4][0:BLK, 0:NG * E], place[k][:, T, :], table[k][:, T].rearrange("p g e -> p (g e)"),
                                   start=(n == 0), stop=(n == 2 * NT - 1))
                mm.then_inc(table_done, 1)
                pe.wait_ge(dest_ready, i + 1)

                def turn_rows(b, bt, s, js):
                    for j in js:
                        mm = pe.transpose(bt[:, BLK * j:BLK * j + BLK],
                                          xg[b][0:BLK, :].rearrange("p (f j) -> p j f", j=NJ)[:, j, :], ident[0:BLK, 0:BLK])
                    if js[-1] == NJ - 1:
                        mm.then_inc(s["t"], 1)

                def rows_arrive(s, arrivals):
                    pe.wait_ge(s["gathered"], arrivals * 16)
                    pe.sem_inc(rows_seen, 1)

                def block_pass(n, b, banks, s, arrived, ahead=(None, None)):
                    bg, bu, bh, bd = banks
                    pe.wait_ge(s["xT"], n)
                    for k, dst, done in ((0, bg, s["gate"]), (1, bu, s["up"])):
                        w = arrived(k)
                        for j in range(NJ):
                            for hf in range(2):
                                mm = pe.matmul(dst[BLK * hf:BLK * hf + BLK, 0:256], xT[b][:, j, :],
                                               w[:, 512 * j + 256 * hf:512 * j + 256 * hf + 256],
                                               start=(j == 0), stop=(j == NJ - 1))
                        mm.then_inc(done, 1)
                    if ahead[0]:
                        ahead[0]()
                    pe.wait_ge(s["h"], n)
                    for c in range(2):
                        mm = pe.transpose(bh[:, P * c:P * c + P], hb[b][:, P * c:P * c + P], ident)
                    mm.then_inc(s["ht"], 1)
                    if ahead[1]:
                        ahead[1]()
                    w = arrived(2)
                    pe.wait_ge(s["hts"], n)
                    for kt in range(4):
                        lhs = hts[b][:, P * (kt % 2) + BLK * (kt // 2):P * (kt % 2) + BLK * (kt // 2) + BLK]
                        for hf in range(2):
                            mm = pe.matmul(bd[BLK * hf:BLK * hf + BLK, :], lhs, w[:, 1024 * kt + 512 * hf:1024 * kt + 512 * hf + 512],
                                           start=(kt == 0), stop=(kt == 3))
                    mm.then_inc(s["down"], 1)

                regular = [dict(gathered=gathered[b], t=t_done, xT=xT_ready, gate=gate_done, up=up_done, h=h_ready,
                                ht=ht_done, hts=hts_ready, down=down_done) for b in range(2)]
                n0 = base[name]

                def expert(it, b, last):
                    n = pe.snap(it * 2 + (E * i + b + 1))

                    def arrived(k):
                        q = n0 + 3 * b + k
                        pe.wait_ge(ring_full[q % RING], it * 16 + 16 * (q // RING + 1))
                        return ring[:, q % RING, :]
                    more = pe.value_load(extra_i[0:1, bass.ds(it * 2 + b, 1)], min_val=0, max_val=NG - 1)
                    with pe.If(more > 0):
                        with pe.Fori(0, more) as _g:
                            pe.reg_add(count, count, 1)
                            m = pe.snap(count)
                            rows_arrive(ex, m)
                            turn_rows(2, bank[1], ex, range(NJ))
                            block_pass(m, 2, (bank[2], bank[3], bank[5], bank[0]), ex, arrived)

                    def next_rows():
                        rows_arrive(regular[1 - b], it + (E // 2 * i + 1 + b))
                        turn_rows(1 - b, bank[4], regular[1 - b], range(NJ // 2))
                    block_pass(n, b, (bank[2], bank[3], bank[5], bank[6 + b]), regular[b], arrived,
                               (None, None) if last else (next_rows, lambda: turn_rows(1 - b, bank[4], regular[1 - b], range(NJ // 2, NJ))))

                if i == 0:
                    pe.wait_ge(mod_ready, 18)
                rows_arrive(regular[0], E // 2 * i + 1)
                turn_rows(0, bank[4], regular[0], range(NJ))
                with pe.Fori(0, E // 2 - 1) as it:
                    for b in range(2):
                        expert(it, b, False)
                last_pair = pe.alloc_register(f"last_pair{i}")
                pe.reg_mov(last_pair, E // 2 - 1)
                for b in range(2):
                    expert(pe.snap(last_pair), b, b == 1)
                pe.wait_ge(y_ready, E * (i + 1))
                pe.wait_ge(diag_ready, i + 1)
                for T in range(NT):
                    pe.wait_ge(y_back[T], 32 * (i + 1))
                    if T >= 2:
                        pe.wait_ge(y_taken, NT * st + T - 1)
                    for n in range(2):
                        for k in range(2):
                            mm = pe.matmul(bank[2 * (T % 2) + n][:, :], diag[k][:, T, :], ycomb[T][:, k, 512 * n:512 * n + 512],
                                           start=(k == 0), stop=(k == 1))
                    mm.then_inc(y_done, 1)
                pe.wait_ge(y_taken, NT * (st + 1))

            moe(0, "moe0")

            modulated(2)
            pe.wait_ge(hmT_ready, 2 * NT * 3)
            wa, wb = full(base["in_o"]), full(base["in_o"] + 1)
            for T in range(NT + 1):
                if T < NT:
                    if T >= 2:
                        pe.wait_ge(lat_ready, T - 1)
                        pe.wait_ge(kr_ready, T - 1)
                    for w, width, ps in ((wa, 384, bank[2 * (T % 2)]), (wb, 320, bank[2 * (T % 2) + 1])):
                        for j in range(NJ):
                            mm = pe.matmul(ps[:, 0:width], hmT[:, j, tcols(T)], w[:, width * j:width * j + width],
                                           start=(j == 0), stop=(j == NJ - 1))
                    mm.then_inc(lat_done, 1)
                if T == NT:
                    pe.wait_ge(lat_done, NT)
                    pe.sem_inc(slot_free, 2)
                if T:
                    pe.wait_ge(lat_ready, T)
                    pe.wait_ge(kr_ready, T)
                    if T >= 2:
                        pe.wait_ge(latT_ready, T - 1)
                        pe.wait_ge(krT_ready, T - 1)
                    for j in range(5):
                        pe.transpose(bank[4 + j // 3][:, P * (j % 3):P * (j % 3) + P], lat[(T - 1) % 2][:, P * j:P * j + P], ident)
                    pe.transpose(bank[5][:, 2 * P:3 * P], krd[(T - 1) % 2], ident).then_inc(latT_done, 1)
            wq = [full(base["qb"] + n)[:, 0:768 * 3].rearrange("p (j h n) -> p j h n", j=3, h=4) for n in range(2)]
            wkv = full(base["kvb"]).rearrange("p (j h n) -> p j h n", j=2, h=MH)
            def head_proj(h):
                if h:
                    pe.wait_ge(qkn_ready, h)
                for j in range(3):
                    pe.matmul(bank[0][:, :], wq[h // 4][:, j, h % 4, 0:NOPE], qaT[:, j, :], start=(j == 0), stop=(j == 2))
                for j in range(2):
                    mm = pe.matmul(bank[1][:, :], wkv[:, j, h, 0:NOPE], kaT[:, j, :], start=(j == 0), stop=(j == 1))
                mm.then_inc(qkn_done, 1)

            for T in range(NT + 1):
                if T < NT:
                    pe.wait_ge(latT_ready, T + 1)
                    if T >= 2:
                        pe.wait_ge(qr_ready, T - 1)
                    for n in range(2):
                        for j in range(3):
                            mm = pe.matmul(bank[(6, 2)[T % 2]][:, 256 * n:256 * n + 256], qaT[:, j, tcols(T)],
                                           wq[n][:, j, :, NOPE:NOPE + ROPE], start=(j == 0), stop=(j == 2))
                    mm.then_inc(qr_done, 1)
                    for n in range(2):
                        if T:
                            pe.wait_ge(v_ready, 2 * T + n - 1)
                        for j in range(2):
                            mm = pe.matmul(bank[n][:, :], kaT[:, j, tcols(T)], wkv[:, j, 4 * n:4 * n + 4, NOPE:NOPE + VD],
                                           start=(j == 0), stop=(j == 1))
                        mm.then_inc(v_done, 1)
                if T == NT:
                    pe.wait_ge(v_ready, 2 * NT)
                    head_proj(0)
                if T:
                    pe.wait_ge(qr_ready, T)
                    if T >= 2:
                        pe.wait_ge(qrT_ready, T - 1)
                    for j in range(4):
                        mm = pe.transpose(bank[7][:, P * j:P * j + P], qr[(T - 1) % 2][:, P * j:P * j + P], ident)
                    mm.then_inc(qrt_done, 1)
            pe.wait_ge(krT_ready, NT)
            pe.wait_ge(qrT_ready, NT)

            def scores(u):
                h, i = divmod(u, NT)
                nk = P * (i + 1)
                pe.wait_ge(qkn_ready, h + 1)
                if u >= 2:
                    pe.wait_ge(p_ready, u - 1)
                ps = bank[2 + u % 2]
                half = slice(ROPE * (h % 2), ROPE * (h % 2) + ROPE)
                pe.matmul(ps[:, 0:nk], qnT[h % 2][:, tcols(i)], knT[h % 2][:, 0:nk], start=True, stop=False)
                pe.matmul(ps[:, 0:nk], qrT[half, h // 2, tcols(i)], krT[half, 0:nk], start=False, stop=False)
                pe.matmul(ps[:, nk - P:nk], ident, cc(C_ATT), start=False, stop=True).then_inc(s_done, 1)

            def turn(u):
                h, i = divmod(u, NT)
                pe.wait_ge(pn_ready, u + 1)
                if u >= 2:
                    pe.wait_ge(pt_ready, u - 1)
                for k in range(i + 1):
                    mm = pe.transpose(bank[4 + u % 2][:, P * k:P * k + P], prob[u % 2][:, P * k:P * k + P], ident)
                mm.then_inc(pt_done, 1)

            def values(u):
                h, i = divmod(u, NT)
                pe.wait_ge(pt_ready, u + 1)
                if i == 0 and h >= 2:
                    pe.wait_ge(oT_ready, h - 1)
                for k in range(i + 1):
                    mm = pe.matmul(bank[6 + h % 2][:, tcols(i)], v_tok[:, k, VD * h:VD * h + VD], probT[u % 2][:, P * k:P * k + P],
                                   start=(k == 0), stop=(k == i))
                mm.then_inc(av_done, 1)

            for u in range(MH * NT + 3):
                if u < MH * NT:
                    scores(u)
                    if u % NT == 0 and u // NT + 1 < MH:
                        head_proj(u // NT + 1)
                if 2 <= u < MH * NT + 2:
                    turn(u - 2)
                if u >= 3:
                    values(u - 3)
            pe.wait_ge(av_done, MH * NT)
            pe.sem_inc(slot_free, 3)
            pe.wait_ge(oT_ready, MH)
            modulations(range(3 * CHUNKS, 4 * CHUNKS))
            pe.wait_ge(mod_ready, 4 * CHUNKS)
            out_proj("out_o", [oT[:, j, :] for j in range(MH)], 2)
            pe.wait_ge(y_taken, 3 * NT)
            moe(1, "moe1")

        @block.scalar
        def _(act):
            step = InOrder(act, act_step)
            act.wait_ge(small_in, 16)
            act.activation(cond[:, :], sml[:, S_C:S_C + NJ], ACT.Silu).then_inc(cond_ready, 1)

            def modulations(chunks, banks=bank[0:2]):
                for k in chunks:
                    st, c = divmod(k, CHUNKS)
                    act.wait_ge(ada_done, k + 1)
                    if c == 0 and st:
                        act.wait_ge(hm_ready, NT * st)
                    dst = modss[:, 512 * c:512 * c + 512] if c < 4 else gates[st % 2][:, 512 * (c - 4):512 * (c - 4) + 512]
                    act.activation(dst, banks[k % 2][:, :], ACT.Copy, bias=(0.0 if c < 2 else 1.0)).then_inc(mod_ready, 1)

            def park(n, ps, taken=None):
                act.wait_ge(park_done, n + 1)
                b = part_buffer[n]
                if kept_before[b][n]:
                    act.wait_ge(part_kept[b], 16 * kept_before[b][n])
                signal(act, act.activation(parts[b], ps[:, :], ACT.Copy), part_ready, n + 1)
                if taken:
                    act.sem_inc(taken, 1)

            def input_tile(st, T):
                k = NT * st + T
                if st % 2:
                    act.wait_ge(hm_ready, k + 1)
                    act.dma_start(hm_rows[st // 2][P * T:P * T + P, :], hm[st][T % 2]).then_inc(hm_stored[T % 2], 16)
                for half in range(2):
                    act.wait_ge(tr_done, 2 * k + half + 1)
                    act.activation(hmT[:, 4 * half:4 * half + 4, tcols(T)],
                                   bank[2 + half][:, :].rearrange("p (j t) -> p j t", j=4), ACT.Copy).then_inc(hmT_ready, 1)

            def load_ln_rows(st):
                for n in range(2):
                    r = 2 * DEPTH * CHUNKS + 4 * st + 2 * n
                    act.dma_start(ln_rows[st % 2][n], rows[r:r + 2, :].rearrange("(o r) n -> o (r n)", o=1).to_broadcast([P, D_MODEL]))\
                        .then_inc(ln_rows_in, 16)

            def layer_norm(st):
                def spread(T):
                    k, c = NT * st + T, 16 * (T % 2)
                    act.wait_ge(var_ready, k + 1)
                    act.activation(statb[:, c + 14:c + 15], statb[:, c + 13:c + 14], ACT.Sqrt, bias=cst[:, C_EPS5:C_EPS5 + 1])\
                        .then_inc(std_ready, 1)
                    act.wait_ge(rstd_ready, k + 1)
                    y = lnr[T % 2] if st % 2 == 0 else ycomb[T][:, 0, :]
                    act.activation(y, y, ACT.Identity, scale=statb[:, c + 15:c + 16], bias=statb[:, c + 14:c + 15]).then_inc(z_ready, 1)

                for T in range(NT):
                    if T == NT - 1 and st < 2 * DEPTH - 1:
                        input_tile(st + 1, 0)
                    spread(T)
                for T in range(1, NT):
                    if st < 2 * DEPTH - 1:
                        input_tile(st + 1, T)

            def quarters(n, ps=bank[4], dst=part[:, :]):
                act.wait_ge(quarters_done, n)
                act.activation(dst, ps[:, :], ACT.Copy).then_inc(quarters_ready, 1)

            for c in range(DIRECT + 1):
                if c < DIRECT:
                    if c >= 2:
                        act.wait_ge(ada_done, c - 1)
                    quarters(c + 1, bank[c % 2], parts[c % 2])
                if c:
                    modulations([c - 1], bank[2:4])
            for T in range(NT):
                input_tile(0, T)
            quarters(DIRECT + 1)
            act.wait_ge(t_ready, 1)
            step(act.activation(g_sp, g_t, ACT.Abs))
            step(act.activation(g_sp, g_sp, ACT.Exp, scale=-1.0))
            step(act.activation(g_sp, g_sp, ACT.Ln, bias=1.0))
            step(act.activation(g_ea, sml[:, S_AL:S_AL + 16], ACT.Exp))
            act.activation(g_beta.rearrange("p (t h) -> p t h", t=NT),
                           bank[7][:, 0:32].rearrange("p (t x) -> p t x", t=NT)[:, :, 0:H], ACT.Exp, scale=-1.0).then_inc(sp_ready, 1)

            def root(m):
                act.wait_ge(ssq_done, m + 1)
                if m >= 2:
                    act.wait_ge(qk_ready, m - 1)
                act.activation(rq[m % 2], bank[4 + m % 2][:, :], ACT.Sqrt, bias=cst[:, C_EPS6:C_EPS6 + 1]).then_inc(rt_ready, 1)

            for m in range(12):
                act.wait_ge(conv_done, m + 1)
                signal(act, act.activation(qkv[:, m, :], qkv[:, m, :], ACT.Silu), silu_done, m + 1)
                if m < 8:
                    if m >= 2:
                        act.wait_ge(ssq_done, m - 1)
                    act.activation(sq[m % 2], qkv[:, m, :], ACT.Square).then_inc(sq_ready, 1)
                if 1 <= m <= 8:
                    root(m - 1)
                if m % 4 == 3:
                    park(m // 4, bank[6])
            act.wait_ge(gcs_ready, 1)
            step(act.activation(g_eg, g_gc, ACT.Exp))
            act.activation(g_kd, g_kd, ACT.Exp).then_inc(ge_ready, 1)

            def take(units):
                for u in units:
                    q, half = UNITS[u]
                    kind, t = FILLING[q]
                    if kind == "park":
                        act.wait_ge(fill_done, q + 1)
                        park(t, bank[6 + q % 2], fill_taken[q % 2])
                    elif half == 1 and kind in "zc":
                        act.wait_ge(fill_done, q + 1)
                        dst = zs[:, t, :] if kind == "z" else yb_T[:, t, :]
                        act.activation(dst, bank[6 + q % 2][:, :], ACT.Silu if kind == "z" else ACT.Copy).then_inc(fill_taken[q % 2], 1)
            take(range(BEFORE))
            act.wait_ge(qk_ready, 8)
            for pair in range(2):
                tiles = [(2 * pair + k, k, [bank[3 * k + n] for n in range(3)]) for k in range(2)]
                for T, k, B in tiles:
                    act.wait_ge(gcb_done, T + 1)
                    act.wait_ge(gates_ready, 1)
                    act.activation(d_U[k], B[0][:, :].rearrange("p (h t) -> p h t", h=H), ACT.Exp).then_inc(eb_ready, 1)
                    act.wait_ge(dd_ready, T + 1)
                    step(act.activation(d_KB[k], d_KB[k], ACT.Exp))
                    act.activation(d_MT[k], d_MT[k], ACT.Exp, scale=-1.0).then_inc(dx_ready, 1)
                take(units_at(pair, 0))
                for T, k, B in tiles:
                    act.wait_ge(xt_done, T + 1)
                    act.activation(d_Y[k], B[0][:, :].rearrange("p (h t) -> p h t", h=H), ACT.Copy).then_inc(y0_ready, 1)
                for point in (1, 2, 3):
                    take(units_at(pair, point))
                for T, k, B in tiles:
                    act.wait_ge(kt_done, T + 1)
                    for h in range(H):
                        q = NT * T + h
                        act.activation(d_KB[k][:, h, :], B[0][:, P * h:P * h + P], ACT.Copy, scale=g_beg[:, q:q + 1])
                        ins = act.activation(d_KD[k][:, h, :], B[0][:, P * h:P * h + P], ACT.Copy, scale=g_kd[:, q:q + 1])
                    ins.then_inc(kd_ready, 1)
                for point in (4, 5, 6, 7):
                    take(units_at(pair, point))
                for T, k, B in tiles:
                    act.wait_ge(vt_done, T + 1)
                    for h in range(H):
                        q = NT * T + h
                        ins = act.activation(qkv[:, 8 + h, tcols(T)], B[0][:, P * h:P * h + P], ACT.Copy, scale=g_beta[:, q:q + 1])
                    ins.then_inc(vb_ready, 1)
                for point in (8, 9, 10):
                    take(units_at(pair, point))
                for T, k, B in tiles:
                    act.wait_ge(uw_done, T + 1)
                    act.activation(d_U[k], B[1][:, :].rearrange("p (h t) -> p h t", h=H), ACT.Copy).then_inc(u_ready, 1)
                take(units_at(pair, 11))
                for T, k, B in tiles:
                    for point in range(4):
                        take(units_at(pair, 12 + 4 * k + point))
                    act.wait_ge(o_done, 2 * T + 2)
                    if T:
                        act.wait_ge(ot_done, T)
                    for h in range(H):
                        step(act.activation(os_[:, h, :], B[2][:, P * h:P * h + P], ACT.Square, accum_out=g_ms[:, NT * T + h:NT * T + h + 1]))
                    act.activation(g_ms[:, NT * T:NT * T + H], g_ms[:, NT * T:NT * T + H], ACT.Sqrt, scale=1.0 / DK,
                                   bias=cst[:, C_EPS6:C_EPS6 + 1]).then_inc(orms_ready, 1)
                    act.wait_ge(orec_ready, T + 1)
                    for h in range(H):
                        ins = act.activation(os_[:, h, :], B[2][:, P * h:P * h + P], ACT.Copy, scale=g_ms[:, NT * T + h:NT * T + h + 1])
                    ins.then_inc(os_ready, 1)
            act.wait_ge(ya_ready, NT)
            act.dma_start(xres[:, :, :], x.rearrange("(t p) d -> p t d", p=P)).then_inc(x_in, 16)
            modulations(range(DIRECT, 2 * CHUNKS))
            load_ln_rows(0)
            layer_norm(0)

            count = act.alloc_register("act_extra")
            act.reg_mov(count, 0)
            row = act.alloc_register("extra_row")

            def moe(i):
                st = 2 * i + 1
                quarters(DIRECT + i + 2)
                act.wait_ge(logit_done, i + 1)
                act.activation(r_sc, bank[4][:, 0:P], ACT.Sigmoid).then_inc(score_ready, 1)
                if i == 0:
                    modulations(range(2 * CHUNKS, 3 * CHUNKS))
                act.wait_ge(dest_ready, i + 1)
                act.wait_ge(ln_done, NT * st)

                def rows_copy(b, bt, s, n):
                    act.wait_ge(s["t"], n + s["t_first"])
                    act.activation(xT[b], bt[:, :].rearrange("p (j s) -> p j s", j=NJ), ACT.Copy).then_inc(s["xT"], 1)

                def silu(b, s, n):
                    act.wait_ge(s["gate"], n)
                    act.activation(sg[b], bank[2][:, 0:256], ACT.Silu).then_inc(s["silu"], 1)

                def store(b, s, n, row):
                    act.wait_ge(s["y"], n)
                    for hf in range(2):
                        act.dma_start(y_rows[bass.ds(row, BLK), 512 * hf:512 * hf + 512],
                                      yb[b][BLK * hf:BLK * hf + BLK, :]).then_inc(s["stored"], 16)

                act.reg_mov(row, BLK * E)
                regular = [dict(t=t_done, t_first=2, xT=xT_ready, gate=gate_done, silu=silu_ready, y=y_ready, stored=y_stored[b])
                           for b in range(2)]
                extra = dict(ex, t_first=1)

                def expert(it, b, last):
                    n = act.snap(it * 2 + (E * i + b + 1))
                    more = act.value_load(extra_i[0:1, bass.ds(it * 2 + b, 1)], min_val=0, max_val=NG - 1)
                    with act.If(more > 0):
                        with act.Fori(0, more) as _g:
                            act.reg_add(count, count, 1)
                            m = act.snap(count)
                            r = act.snap(row)
                            act.reg_add(row, row, BLK)
                            rows_copy(2, bank[1], extra, m)
                            silu(2, extra, m)
                            store(2, extra, m, r)
                    silu(b, regular[b], n)
                    if not last:
                        rows_copy(1 - b, bank[4], regular[1 - b], it * 2 + (E * i + b + 2))
                    store(b, regular[b], n, it * (2 * BLK) + BLK * b)

                rows_copy(0, bank[4], regular[0], E * i + 1)
                with act.Fori(0, E // 2 - 1) as it:
                    for b in range(2):
                        expert(it, b, False)
                load_ln_rows(st)
                last_pair = act.alloc_register(f"act_last_pair{i}")
                act.reg_mov(last_pair, E // 2 - 1)
                for b in range(2):
                    expert(act.snap(last_pair), b, b == 1)
                layer_norm(st)

            moe(0)

            act.wait_ge(ln_done, 2 * NT)
            act.wait_ge(ang_ready, 1)
            step(act.activation(sn_t, ang.rearrange("p (t f) -> p t f", t=NT), ACT.Sin))
            step(act.activation(kround, ang, ACT.Abs))
            act.activation(cs_t, kround.rearrange("p (t f) -> p t f", t=NT), ACT.Sin, scale=-1.0,
                           bias=cst[:, C_HPI:C_HPI + 1]).then_inc(sin_ready, 1)
            for T in range(NT + 1):
                if T < NT:
                    bq, bk, rows_T = bank[2 * (T % 2)], bank[2 * (T % 2) + 1], lat[T % 2]
                    act.wait_ge(lat_done, T + 1)
                    if T >= 2:
                        act.wait_ge(latT_done, T - 1)
                    step(act.activation(rows_T[:, 0:384], bq[:, 0:384], ACT.Square, accum_out=ms_o[:, 8 * T:8 * T + 1]))
                    step(act.activation(rows_T[:, 384:640], bk[:, 0:256], ACT.Square, accum_out=ms_o[:, 8 * T + 1:8 * T + 2]))
                    step(act.activation(ms_o[:, 8 * T + 2:8 * T + 3], ms_o[:, 8 * T:8 * T + 1], ACT.Sqrt, scale=1.0 / Q_LORA,
                                        bias=cst[:, C_EPS6:C_EPS6 + 1]))
                    act.activation(ms_o[:, 8 * T + 3:8 * T + 4], ms_o[:, 8 * T + 1:8 * T + 2], ACT.Sqrt, scale=1.0 / KV_LORA,
                                   bias=cst[:, C_EPS6:C_EPS6 + 1]).then_inc(lms_ready, 1)
                    act.wait_ge(lrs_ready, T + 1)
                    act.activation(rows_T[:, 0:384], bq[:, 0:384], ACT.Copy, scale=ms_o[:, 8 * T + 4:8 * T + 5])
                    act.activation(rows_T[:, 384:640], bk[:, 0:256], ACT.Copy, scale=ms_o[:, 8 * T + 5:8 * T + 6]).then_inc(lat_ready, 1)
                if T:
                    act.wait_ge(latT_done, T)
                    for j in range(5):
                        dst = qaT[:, j, tcols(T - 1)] if j < 3 else kaT[:, j - 3, tcols(T - 1)]
                        w = S_QN + j if j < 3 else S_KN + j - 3
                        ins = act.activation(dst, bank[4 + j // 3][:, P * (j % 3):P * (j % 3) + P], ACT.Copy, scale=sml[:, w:w + 1])
                    ins.then_inc(latT_ready, 1)
            for T in range(NT + 1):
                if T < NT:
                    for n in range(2):
                        act.wait_ge(v_done, 2 * T + n + 1)
                        act.activation(v_tok[:, T, 512 * n:512 * n + 512], bank[n][:, :], ACT.Copy).then_inc(v_ready, 1)
                if T:
                    act.wait_ge(qrt_done, T)
                    act.activation(qrT[:, :, tcols(T - 1)], bank[7][:, :].rearrange("p (j t) -> p j t", j=4), ACT.Copy).then_inc(qrT_ready, 1)

            scale = float(NOPE + ROPE) ** -0.5

            def head_copy(h):
                act.wait_ge(qkn_done, h + 1)
                if h >= 2:
                    act.wait_ge(s_done, NT * (h - 1))
                step(act.activation(qnT[h % 2], bank[0][:, :], ACT.Copy))
                act.activation(knT[h % 2], bank[1][:, :], ACT.Copy).then_inc(qkn_ready, 1)

            head_copy(0)
            for u in range(MH * NT + 3):
                if u < MH * NT:
                    h, i = divmod(u, NT)
                    nk = P * (i + 1)
                    act.wait_ge(nm_ready, u + 1)
                    if u >= 2:
                        act.wait_ge(pt_done, u - 1)
                    act.activation(prob[u % 2][:, 0:nk], bank[2 + u % 2][:, 0:nk], ACT.Exp, bias=att_n[:, u:u + 1], scale=scale,
                                   accum_out=att_s[:, u:u + 1]).then_inc(p_ready, 1)
                    if i == 0 and h + 1 < MH:
                        head_copy(h + 1)
                if 2 <= u < MH * NT + 2:
                    v = u - 2
                    nk = P * (v % NT + 1)
                    act.wait_ge(pt_done, v + 1)
                    if v >= 2:
                        act.wait_ge(av_done, v - 1)
                    act.activation(probT[v % 2][:, 0:nk], bank[4 + v % 2][:, 0:nk], ACT.Copy).then_inc(pt_ready, 1)
                if u >= 3 and (u - 3) % NT == NT - 1:
                    h = (u - 3) // NT
                    act.wait_ge(av_done, NT * (h + 1))
                    act.activation(oT[:, h, :], bank[6 + h % 2][:, :], ACT.Copy).then_inc(oT_ready, 1)
            modulations(range(3 * CHUNKS, 4 * CHUNKS))
            load_ln_rows(2)
            layer_norm(2)
            moe(1)
            for T in range(NT):
                act.wait_ge(*((ln_done, NT * (2 * DEPTH - 1) + T + 1) if T < NT // 2 else (hm_ready, NT * 2 * DEPTH + T - NT // 2 + 1)))
                act.dma_start(out[P * T:P * T + P, :], ycomb[T][:, 0, :]).then_inc(out_stored, 16)
            act.wait_ge(out_stored, 16 * NT)

        @block.vector
        def _(dve):
            step = InOrder(dve, dve_step)

            def modulate(T):
                if T >= 2:
                    dve.wait_ge(tr_done, 2 * (T - 1))
                step(dve.tensor_tensor(hm[0][T % 2], xres[:, T, :], modss[:, 1024:2048], ALU.mult))
                signal(dve, dve.tensor_tensor(hm[0][T % 2], hm[0][T % 2], modss[:, 0:1024], ALU.add), hm_ready, T + 1)

            def working_rows(st, T):
                return lnr[T % 2] if st % 2 == 0 else ycomb[T][:, 0, :]

            def next_modulation(st):
                g, b = ln_rows[st % 2]
                dve.wait_ge(mod_ready, CHUNKS * (st + 2))
                dve.wait_ge(ln_rows_in, 32 * (st + 1))
                product = hm[st][0]
                step(dve.tensor_tensor(product, modss[:, 1024:2048], b, ALU.mult))
                step(dve.tensor_tensor(modss[:, 0:1024], modss[:, 0:1024], product, ALU.add))
                step(dve.tensor_tensor(modss[:, 1024:2048], modss[:, 1024:2048], g, ALU.mult))

            def stage_input(st, T):
                if st == 2 * DEPTH - 1 and T < NT // 2:
                    return
                g, b = (modss[:, 1024:2048], modss[:, 0:1024]) if st < 2 * DEPTH - 1 else ln_rows[1]
                k, y = NT * (st + 1) + T, working_rows(st, T)
                out_rows = hm[st + 1][T % 2] if st < 2 * DEPTH - 1 else y
                dve.wait_ge(z_ready, NT * st + T + 1)
                if T >= 2 and st < 2 * DEPTH - 1:
                    dve.wait_ge(tr_done, 2 * (k - 1))
                    if st % 2 == 0:
                        dve.wait_ge(hm_stored[T % 2], 16 * (NT // 2 * (st // 2) + T // 2))
                step(dve.tensor_tensor(out_rows, y, g, ALU.mult))
                signal(dve, dve.tensor_tensor(out_rows, out_rows, b, ALU.add), hm_ready,
                       k + 1 if st < 2 * DEPTH - 1 else k + 1 - NT // 2)

            def combined(st, T):
                k, c, y = NT * st + T, 16 * (T % 2), working_rows(st, T)
                dve.wait_ge(mod_ready, CHUNKS * (st + 1))
                dve.wait_ge(y_done, k + 1)
                if st % 2 == 0 and T >= 2:
                    dve.wait_ge(ln_done, NT * st + T - 1)
                for n in range(2):
                    ins = dve.tensor_tensor(y[:, 512 * n:512 * n + 512], bank[2 * (T % 2) + n][:, :],
                                            gates[st % 2][:, 512 * n:512 * n + 512], ALU.mult)
                    if n == 0:
                        step(ins)
                signal(dve, ins, y_taken, k + 1)
                step(dve.scalar_tensor_tensor(out=y, in0=xres[:, T, :], scalar=DN_ALPHA, in1=y, op0=ALU.mult, op1=ALU.add))
                for n in range(2):
                    step(dve.bn_stats(statb[:, c + 6 * n:c + 6 * n + 6], y[:, 512 * n:512 * n + 512]))
                signal(dve, dve.bn_aggr(statb[:, c + 12:c + 14], statb[:, c:c + 12]), var_ready, k + 1)

            def normalizer(st, T):
                k, c = NT * st + T, 16 * (T % 2)
                dve.wait_ge(std_ready, k + 1)
                step(dve.reciprocal(statb[:, c + 15:c + 16], statb[:, c + 14:c + 15]))
                signal(dve, dve.scalar_tensor_tensor(out=statb[:, c + 14:c + 15], in0=statb[:, c + 12:c + 13], scalar=-1.0,
                                                     in1=statb[:, c + 15:c + 16], op0=ALU.mult, op1=ALU.mult), rstd_ready, k + 1)

            def norm_stage(st):
                if st:
                    dve.wait_ge(ln_done, NT * st)
                else:
                    dve.wait_ge(x_in, 32)
                if st < 2 * DEPTH - 1:
                    next_modulation(st)
                else:
                    dve.wait_ge(ln_rows_in, 32 * (st + 1))
                if st % 2 == 0:
                    for T in range(NT):
                        combined(st, T)
                        normalizer(st, T)
                        if T < 2:
                            stage_input(st, T)
                    stage_input(st, 2)
                    stage_input(st, 3)
                    return
                for T in range(NT + 2):
                    if 2 <= T < NT:
                        stage_input(st, T - 2)
                    if T < NT:
                        combined(st, T)
                    if 1 <= T <= NT:
                        normalizer(st, T - 1)
                    if T >= NT:
                        stage_input(st, T - 2)

            dve.wait_ge(x_in, 16)
            dve.wait_ge(mod_ready, 4)
            for T in range(NT):
                modulate(T)

            dve.wait_ge(inputs_in, 48)
            dve.wait_ge(ba_done, 1)
            t3 = g_t.rearrange("p (t h) -> p t h", t=NT)
            signal(dve, dve.tensor_tensor(t3, bank[7][:, 0:32].rearrange("p (t x) -> p t x", t=NT)[:, :, H:2 * H],
                                          sml[:, S_DT:S_DT + 16].rearrange("p (t h) -> p t h", t=NT), ALU.add), t_ready, 1)
            dve.wait_ge(sp_ready, 1)
            step(dve.scalar_tensor_tensor(out=g_g, in0=g_t, scalar=0.0, in1=g_sp, op0=ALU.max, op1=ALU.add))
            signal(dve, dve.scalar_tensor_tensor(out=g_g, in0=g_g, scalar=-1.0, in1=g_ea, op0=ALU.mult, op1=ALU.mult), g_ready, 1)
            step(dve.tensor_scalar(g_beta, g_beta, 1.0, None, ALU.add))
            step(dve.reciprocal(g_beta, g_beta))

            def conv(ps, acc, w, taps):
                step(dve.tensor_scalar(acc, ps, sml[:, w + taps - 1:w + taps], None, ALU.mult))
                for i in range(1, taps):
                    ins = dve.scalar_tensor_tensor(out=acc[:, i:SEQ], in0=ps[:, 0:SEQ - i], scalar=sml[:, w + taps - 1 - i:w + taps - i],
                                                   in1=acc[:, i:SEQ], op0=ALU.mult, op1=ALU.add)
                    if i < taps - 1:
                        step(ins)
                return ins

            def normalize(m):
                dve.wait_ge(rt_ready, m + 1)
                step(dve.reciprocal(rq[m % 2], rq[m % 2]))
                dve.wait_ge(sq_ready, m + 1)
                signal(dve, dve.scalar_tensor_tensor(out=qkv[:, m, :], in0=qkv[:, m, :], scalar=(DK ** -0.5 if m < H else 1.0),
                                                     in1=rq[m % 2], op0=ALU.mult, op1=ALU.mult), qk_ready, m + 1)

            for m in range(12):
                dve.wait_ge(proj_done, m + 1)
                signal(dve, conv(bank[m % 4][:, :], qkv[:, m, :], S_CW + 4 * m, 4), conv_done, m + 1)
                if 2 <= m < 10:
                    normalize(m - 2)
            dve.wait_ge(gc_done, 1)
            step(dve.tensor_copy(g_gc, bank[7][:, 0:16]))
            signal(dve, dve.tensor_tensor(g_kd, bank[7][:, 16:32], g_gc, ALU.subtract), gcs_ready, 1)
            def take(units):
                for u in units:
                    q, half = UNITS[u]
                    kind, t = FILLING[q]
                    if half == 1 and kind in "hb":
                        dve.wait_ge(fill_done, q + 1)
                        dst = scc[t % 2] if kind == "h" else yb_T[:, t, :]
                        taken = fill_taken[q % 2]
                        if kind == "h" and t == 1:
                            dve.wait_ge(part_kept[1], 16 * kept_before[1][PARKED])
                        if kind == "h" and t == 0:
                            for r in (q - 1, q - 2):
                                dve.wait_ge(fill_taken[r % 2], r // 2 + 1)
                        signal(dve, dve.tensor_tensor(dst, bank[6 + q % 2][:, :], yb_T[:, t, :], ALU.mult), taken, q // 2 + 1)
                        if kind == "h":
                            step(conv(scc[t % 2], yb_T[:, t, :], S_SW + 3 * t, 3))
            dve.wait_ge(ge_ready, 1)
            signal(dve, dve.tensor_tensor(g_beg, g_beta, g_eg, ALU.mult), gates_ready, 1)
            signal(dve, dve.memset(state, 0.0), s_ready, 1)
            dve.wait_ge(y_cleared, 16)
            dve.wait_ge(hmT_ready, 2 * NT)

            def heads(ap):
                return ap.rearrange("p (h t) -> p h t", h=H)

            def per_head(gates_of, T):
                return gates_of[:, H * T:H * T + H].unsqueeze(2).to_broadcast([P, H, P])

            for pair in range(2):
                tiles = [(2 * pair + k, k, [bank[3 * k + n] for n in range(3)]) for k in range(2)]
                for T, k, B in tiles:
                    if pair:
                        dve.wait_ge(ot_done, NT // 2)
                    signal(dve, dve.tensor_tensor(d_MT[k], cc(C_CUM).unsqueeze(1).to_broadcast([P, H, P]), per_head(g_g, T), ALU.mult),
                           cg_ready, T + 1)
                for T, k, B in tiles:
                    dve.wait_ge(kq_done, T + 1)
                    dve.wait_ge(eb_ready, T + 1)
                    step(dve.tensor_tensor(d_X[k], heads(B[0][:, :]), per_head(g_gc, T), ALU.subtract))
                    step(dve.tensor_tensor(d_KB[k], d_X[k], cc(C_DCT).unsqueeze(1).to_broadcast([P, H, P]), ALU.add))
                    signal(dve, dve.tensor_tensor(d_MT[k], d_X[k], cc(C_DEC).unsqueeze(1).to_broadcast([P, H, P]), ALU.add), dd_ready, T + 1)
                for T, k, B in tiles:
                    dve.wait_ge(dx_ready, T + 1)
                    dve.wait_ge(eb_ready, T + 1)
                    for h in range(H):
                        step(dve.scalar_tensor_tensor(out=d_L[k][:, h, :], in0=B[1][:, P * h:P * h + P],
                                                      scalar=g_beta[:, NT * T + h:NT * T + h + 1], in1=d_MT[k][:, h, :],
                                                      op0=ALU.mult, op1=ALU.mult))
                    step(dve.tensor_tensor(d_IT[k], heads(B[2][:, :]), d_KB[k], ALU.mult))
                    step(dve.tensor_copy(g_last[:, T, :, :], d_U[k][:, :, CH - 1:P:CH]))
                    step(dve.tensor_tensor(qkv[:, 0:H, tcols(T)], qkv[:, 0:H, tcols(T)], d_U[k], ALU.mult))
                    step(dve.tensor_tensor(d_X[k], d_L[k], cc(C_LEV).unsqueeze(1).to_broadcast([P, H, P]), ALU.mult))
                    signal(dve, dve.scalar_tensor_tensor(out=d_X[k], in0=d_X[k], scalar=-1.0,
                                                         in1=ident.unsqueeze(1).to_broadcast([P, H, P]),
                                                         op0=ALU.mult, op1=ALU.add), x0_ready, T + 1)
                take(units_at(pair, 0))
                for lv in range(5):
                    for T, k, B in tiles:
                        n = (pair * 5 + lv) * 2 + k
                        dve.wait_ge(mt_done, n + 1)
                        signal(dve, dve.tensor_tensor(d_MT[k], heads(B[1][:, :]),
                                                      cc(C_LEV + P * (lv + 1)).unsqueeze(1).to_broadcast([P, H, P]), ALU.mult),
                               mt_ready, n + 1)
                    take(units_at(pair, 1 + 2 * lv))
                    for T, k, B in tiles:
                        n = (pair * 5 + lv) * 2 + k
                        dve.wait_ge(y2_done, n + 1)
                        step(dve.tensor_tensor(d_Y[k], d_Y[k], heads(B[2][:, :]), ALU.subtract))
                        signal(dve, dve.tensor_tensor(d_X[k], d_X[k], heads(B[1][:, :]), ALU.subtract), lv_ready, n + 1)
                    take(units_at(pair, 2 + 2 * lv))
                for T, k, B in tiles:
                    dve.wait_ge(uw_done, T + 1)
                    signal(dve, dve.tensor_copy(qkv[:, H:2 * H, tcols(T)], heads(B[2][:, :])), wt_ready, T + 1)
                take(units_at(pair, 11))
                def reciprocal_rms(T):
                    dve.wait_ge(orms_ready, T + 1)
                    signal(dve, dve.reciprocal(g_ms[:, NT * T:NT * T + H], g_ms[:, NT * T:NT * T + H]), orec_ready, T + 1)

                def gated(T, B):
                    dve.wait_ge(ot_done, T + 1)
                    signal(dve, dve.scalar_tensor_tensor(out=zs[:, :, tcols(T)], in0=heads(B[0][:, :]), scalar=sml[:, S_NW:S_NW + 1],
                                                         in1=zs[:, :, tcols(T)], op0=ALU.mult, op1=ALU.mult), ya_ready, T + 1)
                for T, k, B in tiles:
                    dve.wait_ge(u_ready, T + 1)
                    for c in range(2):
                        n, r = 2 * T + c, slice(CH * c, CH * c + CH)
                        dve.wait_ge(vn_done, n + 1)
                        signal(dve, dve.tensor_tensor(d_U[k][r, :, :], d_U[k][r, :, :], heads(B[0][r, :]), ALU.subtract), vn_ready, n + 1)
                        if (k, c) == (1, 0):
                            reciprocal_rms(T - 1)
                        take(units_at(pair, 12 + 4 * k + 2 * c))
                        dve.wait_ge(sd_done, n + 1)
                        dve.wait_ge(o_done, n + 1)
                        for h in range(H):
                            ins = dve.scalar_tensor_tensor(out=state[:, h, :], in0=state[:, h, :], scalar=g_last[:, T, h, c:c + 1],
                                                           in1=B[1][:, P * h:P * h + P], op0=ALU.mult, op1=ALU.add)
                            if h < H - 1:
                                step(ins)
                        signal(dve, ins, s_ready, n + 2)
                        take(units_at(pair, 13 + 4 * k + 2 * c))
                gated(tiles[0][0], tiles[0][2])
                reciprocal_rms(tiles[1][0])
                gated(tiles[1][0], tiles[1][2])

            count = dve.alloc_register("dve_extra")
            dve.reg_mov(count, 0)
            for begun in y_stored + [ex["stored"]]:
                dve.sem_inc(begun, 32)

            def moe(i):
                st = 2 * i + 1
                for b in range(2):
                    dve.wait_ge(hm_stored[b], 16 * NT // 2 * (i + 1))
                dve.wait_ge(hmT_ready, 2 * NT * (st + 1))

                def v4(ap, n=E):
                    return ap[:, 0:NT * n].rearrange("p (t e) -> p t e", t=NT)
                sc, bi, tmp, o1, o2, oh, rk = [v4(a) for a in (r_sc, r_bi, r_tmp, r_o1, r_o2, r_oh, r_rk)]
                iota = cc(C_IO, E).unsqueeze(1).to_broadcast([P, NT, E])
                step(dve.memset(r_gs, -BIG))
                dve.wait_ge(score_ready, i + 1)
                step(dve.tensor_tensor(bi, sc, sml[:, S_RB:S_RB + E].unsqueeze(1).to_broadcast([P, NT, E]), ALU.add))
                for q in range(NT * GROUPS):
                    step(dve.max(r_m8[:, 8 * q:8 * q + 8], r_bi[:, 8 * q:8 * q + 8]))
                m8 = r_m8.rearrange("p (t g k) -> p t g k", t=NT, g=GROUPS)
                gs = v4(r_gs, 8)
                step(dve.tensor_tensor(gs[:, :, 0:GROUPS], m8[:, :, :, 0], m8[:, :, :, 1], ALU.add))
                for T in range(NT):
                    c = slice(8 * T, 8 * T + 8)
                    step(dve.max(r_gm[:, c], r_gs[:, c]))
                    step(dve.max_index(mi[:, c], r_gm[:, c], r_gs[:, c]))
                grp = r_sm[:, 0:NT]
                step(dve.tensor_copy(grp, mi[:, 0:32:8]))
                go = r_sm[:, 16:32].rearrange("p (t g) -> p t g", t=NT)
                step(dve.tensor_tensor(go, cc(C_IO, GROUPS).unsqueeze(1).to_broadcast([P, NT, GROUPS]),
                                       grp.unsqueeze(2).to_broadcast([P, NT, GROUPS]), ALU.is_equal))
                step(dve.tensor_tensor(r_tmp.rearrange("p (q k) -> p q k", k=EPG), r_bi.rearrange("p (q k) -> p q k", k=EPG),
                                       r_sm[:, 16:32].unsqueeze(2).to_broadcast([P, NT * GROUPS, EPG]), ALU.mult))
                step(dve.tensor_reduce(v4(r_ig, 8), r_tmp.rearrange("p (t g k) -> p t k g", t=NT, g=GROUPS), AX.X, ALU.add))
                for T in range(NT):
                    c = slice(8 * T, 8 * T + 8)
                    step(dve.max(r_lm[:, c], r_ig[:, c]))
                    step(dve.max_index(mi[:, c], r_lm[:, c], r_ig[:, c]))
                for k, o in ((0, o1), (1, o2)):
                    ek = r_sm[:, 4 + 4 * k:8 + 4 * k]
                    step(dve.tensor_copy(ek, mi[:, k:32:8]))
                    step(dve.scalar_tensor_tensor(out=ek, in0=grp, scalar=float(EPG), in1=ek, op0=ALU.mult, op1=ALU.add))
                    step(dve.tensor_tensor(o, iota, ek.unsqueeze(2).to_broadcast([P, NT, E]), ALU.is_equal))
                step(dve.tensor_tensor(oh, o1, o2, ALU.add))
                step(dve.memset(r_cum[:, 0:E], 0.0))
                for T in range(NT):
                    ins = dve.tensor_tensor(r_cum[:, E * (T + 1):E * (T + 2)], r_cum[:, E * T:E * (T + 1)], oh[:, T, :], ALU.add)
                    if T < NT - 1:
                        step(ins)
                signal(dve, ins, oh_ready, i + 1)
                for k, o in ((0, o1), (1, o2)):
                    step(dve.tensor_tensor(tmp, sc, o, ALU.mult))
                    step(dve.tensor_reduce(wsel[:, 4 * k:4 * k + 4], tmp, AX.X, ALU.add))
                ws = r_sm[:, 12:16]
                step(dve.tensor_tensor(ws, wsel[:, 0:4], wsel[:, 4:8], ALU.add))
                step(dve.reciprocal(ws, ws))
                for k in range(2):
                    step(dve.tensor_tensor(wsel[:, 4 * k:4 * k + 4], wsel[:, 4 * k:4 * k + 4], ws, ALU.mult))
                step(dve.tensor_copy(r_sm[:, 16:20], intc[:, NT:2 * NT]))
                step(dve.tensor_scalar(r_sm[:, 16:20], r_sm[:, 16:20], 1.0, None, ALU.add))
                dve.wait_ge(rank_done, i + 1)
                step(dve.tensor_copy(rk, bank[5][:, 0:P].rearrange("p (t e) -> p t e", t=NT)))

                def floor64(dst, src):
                    step(dve.tensor_scalar(dst, src, 1.0 / BLK, -(BLK - 1.0) / (2 * BLK), ALU.mult, ALU.add))
                    step(dve.tensor_scalar(dst, dst, MAGIC, None, ALU.add))
                    step(dve.tensor_scalar(dst, dst, MAGIC, None, ALU.subtract))

                def chosen(dst, values):
                    for k, o in ((0, o1), (1, o2)):
                        step(dve.tensor_tensor(tmp, values, o, ALU.mult))
                        step(dve.tensor_reduce(dst[:, 4 * k:4 * k + 4], tmp, AX.X, ALU.add))
                rank, block, rest, row = [r_sm[:, 32 + 8 * n:40 + 8 * n] for n in range(4)]
                chosen(rank, rk)
                floor64(block, rank)
                step(dve.scalar_tensor_tensor(out=rest, in0=block, scalar=-float(BLK), in1=rank, op0=ALU.mult, op1=ALU.add))
                for k, o in ((0, o1), (1, o2)):
                    b4 = block[:, 4 * k:4 * k + 4]
                    step(dve.tensor_tensor(place[k], cc(C_IO, BLK).unsqueeze(1).to_broadcast([P, NT, BLK]),
                                           rest[:, 4 * k:4 * k + 4].unsqueeze(2).to_broadcast([P, NT, BLK]), ALU.is_equal))
                    at = v4(r_gs, NG)
                    step(dve.tensor_tensor(at, cc(C_IO, NG).unsqueeze(1).to_broadcast([P, NT, NG]),
                                           b4.unsqueeze(2).to_broadcast([P, NT, NG]), ALU.is_equal))
                    step(dve.tensor_tensor(at, at, r_sm[:, 16:20].unsqueeze(2).to_broadcast([P, NT, NG]), ALU.mult))
                    ins = dve.tensor_tensor(table[k], at.unsqueeze(3).to_broadcast([P, NT, NG, E]),
                                            o.unsqueeze(2).to_broadcast([P, NT, NG, E]), ALU.mult)
                    signal(dve, ins, table_ready, 2 * i + k + 1)
                cnt, bef = r_sm[:, 64:64 + E], r_sm[:, 96:96 + E]
                step(dve.tensor_scalar(cnt, bank[5][:, P:P + E], 1.0, -1.0, ALU.max, ALU.add))
                floor64(cnt, cnt)
                step(dve.tensor_copy(extra_i[:, :], cnt[0:1, :]))
                step(dve.tensor_tensor_scan(bef, ones[:, 0:E], cnt, 0.0, ALU.mult, ALU.add))
                step(dve.tensor_tensor(bef, bef, cnt, ALU.subtract))
                step(dve.tensor_tensor(bef, bef, cc(C_IO, E), ALU.subtract))
                step(dve.tensor_scalar(bef, bef, float(BLK), float(BLK * (E - 1)), ALU.mult, ALU.add))
                chosen(row, bef.unsqueeze(1).to_broadcast([P, NT, E]))
                step(dve.tensor_scalar(block, block, 1.0, None, ALU.min))
                step(dve.tensor_tensor(row, row, block, ALU.mult))
                step(dve.tensor_tensor(row, row, rank, ALU.add))
                step(dve.scalar_tensor_tensor(out=row, in0=r_sm[:, 4:12], scalar=float(BLK), in1=row, op0=ALU.mult, op1=ALU.add))
                step(dve.tensor_copy(dest_i[:, :], row))
                dve.wait_ge(table_done, i + 1)
                places = area_d[0:BLK, 1024:1280]
                step(dve.tensor_scalar(places, bank[4][0:BLK, 0:NG * E], 0.0, float(SEQ + 1), ALU.is_equal, ALU.mult))
                step(dve.scalar_tensor_tensor(out=places, in0=bank[4][0:BLK, 0:NG * E], scalar=-1.0, in1=places, op0=ALU.add, op1=ALU.add))
                signal(dve, dve.tensor_copy(idx_all[:, :], places), dest_ready, i + 1)

                def block_pass(n, b, bd, s, stores):
                    dve.wait_ge(s["silu"], n)
                    dve.wait_ge(s["up"], n)
                    dve.tensor_tensor(hb[b], sg[b], bank[3][:, 0:256], ALU.mult).then_inc(s["h"], 1)
                    dve.wait_ge(s["ht"], n)
                    dve.tensor_copy(hts[b], bank[5][:, 0:256]).then_inc(s["hts"], 1)
                    dve.wait_ge(s["down"], n)
                    dve.wait_ge(s["stored"], stores)
                    dve.tensor_copy(yb[b], bd[:, :]).then_inc(s["y"], 1)

                regular = [dict(silu=silu_ready, up=up_done, h=h_ready, ht=ht_done, hts=hts_ready, down=down_done, y=y_ready,
                                stored=y_stored[b]) for b in range(2)]
                with dve.Fori(0, E // 2) as it:
                    for b in range(2):
                        more = dve.value_load(extra_i[0:1, bass.ds(it * 2 + b, 1)], min_val=0, max_val=NG - 1)
                        with dve.If(more > 0):
                            with dve.Fori(0, more) as _g:
                                dve.reg_add(count, count, 1)
                                m = dve.snap(count)
                                block_pass(m, 2, bank[0], ex, dve.snap(m * 32))
                        block_pass(dve.snap(it * 2 + (E * i + b + 1)), b, bank[6 + b], regular[b], it * 32 + 32 * (E // 2 * i + 1))
                for k in range(2):
                    ins = dve.tensor_tensor(diag[k], ident.unsqueeze(1).to_broadcast([P, NT, P]),
                                            wsel[:, 4 * k:4 * k + 4].unsqueeze(2).to_broadcast([P, NT, P]), ALU.mult)
                    if k == 0:
                        step(ins)
                signal(dve, ins, diag_ready, i + 1)
                norm_stage(st)

            norm_stage(0)
            moe(0)

            dve.wait_ge(hmT_ready, 2 * NT * 3)
            dve.wait_ge(ln_done, 2 * NT)
            posf = ms_o[:, 28:32]
            step(dve.tensor_copy(posf, intc[:, 0:NT]))
            for T in range(NT):
                step(dve.tensor_scalar(ang[:, 32 * T:32 * T + 32], sml[:, S_INV:S_INV + 32], posf[:, T:T + 1], None, ALU.mult))
            step(dve.tensor_scalar(kround, ang, 1.0 / TWO_PI, None, ALU.mult))
            step(dve.tensor_scalar(kround, kround, MAGIC, None, ALU.add))
            step(dve.tensor_scalar(kround, kround, MAGIC, None, ALU.subtract))
            for part in (PI_A, PI_B, PI_C):
                step(dve.scalar_tensor_tensor(out=ang, in0=kround, scalar=-part, in1=ang, op0=ALU.mult, op1=ALU.add))
            signal(dve, dve.tensor_scalar(ang, ang, 3.1415925, -3.1415925, ALU.min, ALU.max), ang_ready, 1)
            dve.wait_ge(sin_ready, 1)

            def rotate(src, dst, n, T, last):
                cos = cs_t[:, T, :].unsqueeze(1).to_broadcast([P, n, 32])
                sin = sn_t[:, T, :].unsqueeze(1).to_broadcast([P, n, 32])
                x1, x2 = src[:, :, 0:32], src[:, :, 32:64]
                a, b = rt1[:, 0:n, :], rt2[:, 0:n, :]
                step(dve.tensor_tensor(a, x1, cos, ALU.mult))
                step(dve.tensor_tensor(b, x2, sin, ALU.mult))
                step(dve.tensor_tensor(dst[:, :, 0:32], a, b, ALU.subtract))
                step(dve.tensor_tensor(a, x2, cos, ALU.mult))
                step(dve.tensor_tensor(b, x1, sin, ALU.mult))
                last(dve.tensor_tensor(dst[:, :, 32:64], a, b, ALU.add))

            for T in range(NT + 1):
                if T < NT:
                    dve.wait_ge(lms_ready, T + 1)
                    signal(dve, dve.reciprocal(ms_o[:, 8 * T + 4:8 * T + 6], ms_o[:, 8 * T + 2:8 * T + 4]), lrs_ready, T + 1)
                    if T >= 2:
                        dve.wait_ge(latT_done, T - 1)
                    dve.wait_ge(lat_ready, T + 1)
                    k = krd[T % 2]
                    rotate(bank[2 * (T % 2) + 1][:, 256:320].rearrange("p (h f) -> p h f", h=1),
                           k[:, 0:ROPE].rearrange("p (h f) -> p h f", h=1), 1, T, step)
                    signal(dve, dve.tensor_copy(k[:, ROPE:2 * ROPE], k[:, 0:ROPE]), kr_ready, T + 1)
                if T:
                    dve.wait_ge(latT_done, T)
                    dve.wait_ge(latT_ready, T)
                    signal(dve, dve.tensor_copy(krT[:, tcols(T - 1)], bank[5][:, 2 * P:3 * P]), krT_ready, T)
            for T in range(NT):
                dve.wait_ge(qr_done, T + 1)
                if T >= 2:
                    dve.wait_ge(qrt_done, T - 1)
                rotate(bank[(6, 2)[T % 2]][:, :].rearrange("p (h f) -> p h f", h=MH), qr[T % 2].rearrange("p (h f) -> p h f", h=MH), MH, T,
                       lambda ins: signal(dve, ins, qr_ready, T + 1))

            scale = float(NOPE + ROPE) ** -0.5
            for u in range(MH * NT + 1):
                if u < MH * NT:
                    nk = P * (u % NT + 1)
                    dve.wait_ge(s_done, u + 1)
                    step(dve.tensor_reduce(att_m[:, u:u + 1], bank[2 + u % 2][:, 0:nk], AX.X, ALU.max))
                    signal(dve, dve.tensor_scalar(att_n[:, u:u + 1], att_m[:, u:u + 1], -scale, None, ALU.mult), nm_ready, u + 1)
                if u >= 1:
                    v = u - 1
                    nk = P * (v % NT + 1)
                    dve.wait_ge(p_ready, v + 1)
                    step(dve.reciprocal(att_r[:, v:v + 1], att_s[:, v:v + 1]))
                    signal(dve, dve.tensor_scalar(prob[v % 2][:, 0:nk], prob[v % 2][:, 0:nk], att_r[:, v:v + 1], None, ALU.mult),
                           pn_ready, v + 1)
            norm_stage(2)
            moe(1)

        @block.gpsimd
        def _(pool):
            count = pool.alloc_register("pool_extra")
            pool.reg_mov(count, 0)
            pool.sem_inc(t_done, 2)
            pool.sem_inc(ex["t"], 1)

            pool.wait_ge(proj_done, 1)
            spread = MAX_EXTRA * BLK // NG
            signal(pool, pool.memset(area_b[0:spread, 0:D_MODEL], 0.0), pool_step, 1)
            pool.dma_start(y_rows[BLK * E:(E + MAX_EXTRA) * BLK, :].rearrange("(p r) d -> p r d", p=spread),
                           area_b[0:spread, 0:D_MODEL].unsqueeze(1).to_broadcast([spread, NG, D_MODEL])).then_inc(y_cleared, 16)

            for n in range(PARKED):
                pool.wait_ge(part_ready, n + 1)
                pool.dma_start(rws[ROWS + 4 * n:ROWS + 4 * n + 4, :], parts[part_buffer[n]][0:P:32, :]).then_inc(part_kept[part_buffer[n]], 16)

            def layer_norm(st):
                g, b = ln_rows[st % 2]
                pool.wait_ge(ln_rows_in, 32 * (st + 1))
                last = st == 2 * DEPTH - 1
                for T in range(NT // 2 if last else NT):
                    k = NT * st + T
                    pool.wait_ge(z_ready, k + 1)
                    y = lnr[T % 2] if st % 2 == 0 else ycomb[T][:, 0, :]
                    rows_out = y if last else xres[:, T, :]
                    signal(pool, pool.tensor_tensor(rows_out, y, g, ALU.mult), gain_done, k + 1)
                    pool.tensor_tensor(rows_out, rows_out, b, ALU.add).then_inc(ln_done, 1)

            def moe(i):
                layer_norm(2 * i)
                pool.wait_ge(y_cleared, 16)
                for b in range(3):
                    ins = pool.memset(xg[b][0:BLK, :], 0.0)
                    signal(pool, ins, pool_step, 3 * i + b + 2)
                pool.wait_ge(dest_ready, i + 1)
                for b in range(2):
                    pool.wait_ge(hm_stored[b], 16 * NT // 2 * (i + 1))

                def gather(n, b, col, s, guard):
                    guard()
                    pool.tensor_copy(idx_col[:, b:b + 1], idx_all[:, bass.ds(col, 1)]).then_inc(s["col"], 1)
                    pool.wait_ge(s["col"], n)
                    pool.sem_inc(col_seen, 1)
                    pool.indirect_dma_start(out=xg[b][0:BLK, :], out_offset=None, in_=hm_rows[i],
                                            in_offset=bass.IndirectOffsetOnAxis(idx_col[:, b:b + 1], 0),
                                            bounds_check=SEQ - 1, oob_is_err=False).then_inc(s["gathered"], 16)

                regular = [dict(col=col_ready, gathered=gathered[b]) for b in range(2)]
                with pool.Fori(0, E // 2) as it:
                    for b in range(2):
                        n = pool.snap(it * 2 + (E * i + b + 1))
                        gather(n, b, it * 2 + b, regular[b],
                               lambda: pool.wait_ge(t_done, n))
                        more = pool.value_load(extra_i[0:1, bass.ds(it * 2 + b, 1)], min_val=0, max_val=NG - 1)
                        with pool.If(more > 0):
                            with pool.Fori(0, more) as g:
                                pool.reg_add(count, count, 1)
                                m = pool.snap(count)
                                gather(m, 2, it * 2 + g * E + (E + b), ex,
                                       lambda: pool.wait_ge(ex["t"], m))
                for b in range(2):
                    pool.wait_ge(y_stored[b], 32 * (E // 2 * (i + 1) + 1))
                pool.wait_ge(ex["stored"], pool.snap(count) * 32 + 32)
                pool.sem_inc(col_seen, 1)
                for T in range(NT):
                    for k in range(2):
                        pool.indirect_dma_start(out=ycomb[T][:, k, :], out_offset=None, in_=y_rows,
                                                in_offset=bass.IndirectOffsetOnAxis(dest_i[:, 4 * k + T:4 * k + T + 1], 0))\
                            .then_inc(y_back[T], 16)
                layer_norm(2 * i + 1)

            moe(0)
            moe(1)


def kernel(x, c, positions, ada_w, ada_b, ln_g, ln_b, w_in_e, gdn_conv_w, gdn_a_log, gdn_dt_bias, gdn_norm_w,
           sc_conv_w, w_out_e, w_in_o, q_a_norm, w_q_b, kv_a_norm, w_kv_b, w_out_o, router_w, router_bias,
           w_gate, w_up, w_down):
    from concourse import bacc
    from concourse.bass_utils import run_bass_kernel_spmd

    def a(v):
        return np.ascontiguousarray(v)

    def taps(w, tiles):
        return a(w).reshape(w.shape[0], tiles, P).transpose(2, 1, 0).reshape(P, -1)

    def everywhere(v):
        return np.broadcast_to(a(v).reshape(1, -1), (P, a(v).size))

    inv = (np.float32(10000.0) ** (-np.arange(0, ROPE, 2, dtype=np.float32) / np.float32(ROPE))).astype(np.float32)
    ba = 3 * H * DK + H * DK
    small = np.concatenate([
        taps(a(gdn_conv_w)[0], 12), taps(a(sc_conv_w)[0], 4), a(gdn_norm_w)[0].reshape(P, 1),
        a(q_a_norm)[0].reshape(3, P).T, a(kv_a_norm)[0].reshape(2, P).T,
        everywhere(np.tile(a(gdn_a_log)[0], NT)), everywhere(np.tile(a(gdn_dt_bias)[0], NT)),
        a(c).reshape(P, NJ), a(router_w).reshape(P, NJ * E), a(a(w_in_e)[0][:, ba:ba + 2 * H]).reshape(P, NJ * 2 * H),
        everywhere(router_bias), everywhere(inv)], axis=1)
    rows = np.concatenate([a(ada_b).reshape(24, 512),
                           np.concatenate([a(ln_g).reshape(4, 2, 512), a(ln_b).reshape(4, 2, 512)], axis=1).reshape(16, 512)])
    token = np.arange(SEQ, dtype=np.int32).reshape(NT, P).T
    ints = np.concatenate([a(positions).reshape(NT, P).T, token], axis=1)
    arrays = dict(x=a(x)[0], small=a(small), const=constants(), rows=a(rows), ints=a(ints), ada_w=a(ada_w),
                  w_in_e=a(w_in_e)[0], w_out_e=a(w_out_e)[0], w_in_o=a(w_in_o)[0], w_q_b=a(w_q_b)[0], w_kv_b=a(w_kv_b)[0],
                  w_out_o=a(w_out_o)[0], w_gate=a(w_gate), w_up=a(w_up), w_down=a(w_down))
    nc = bacc.Bacc("TRN2", target_bir_lowering=False, num_devices=1)
    args = {n: nc.dram_tensor(f"in_{n}", v.shape, mybir.dt.from_np(v.dtype), kind="ExternalInput").ap() for n, v in arrays.items()}
    out = nc.dram_tensor("out_0", [SEQ, D_MODEL], F32, kind="ExternalOutput").ap()
    decoder_kernel(nc, out=out, **args)
    r = run_bass_kernel_spmd(nc, [{f"in_{n}": v for n, v in arrays.items()}], core_ids=[0])
    return r.results[0]["out_0"].reshape(1, SEQ, D_MODEL)
```
